# Optimizing a Trainium2 kernel written in Bass

```python
import math
import jax, jax.numpy as jnp
from jax import lax
import numpy as np

D_MODEL = 1024
BATCH = 1
SEQ = 1024
DEPTH = 1
DEC_BATCH = 8
DEC_SEQ = 1
PAST_LEN = 1024
PAGE_SIZE = 128

N_HEADS = 8
HEAD_DIM = 64
D_ATTN = N_HEADS * HEAD_DIM
IDX_HEADS = 4
IDX_DIM = 64
TOPK_MAX = 256
Q_BLOCK = 128
SSM_WIDTH = 512
GROUP_CH = 16
N_GROUPS = SSM_WIDTH // GROUP_CH
STATE_DIM = 64
D_FF = 2816
NORM_EPS = 1e-6
NEG_BIG = -1e30
PROJ_SIZES = (D_ATTN, D_ATTN, D_ATTN, IDX_HEADS * IDX_DIM, IDX_DIM, IDX_HEADS, SSM_WIDTH, 2 * D_MODEL)
PROJ_DIM = sum(PROJ_SIZES)
PROJ_SPLITS = [int(s) for s in np.cumsum(PROJ_SIZES)[:-1]]

kernel_name = "dsa_s5_gated_macaron_step"

def rmsnorm(x, g):
    xf = x.astype(jnp.float32)
    y = xf * lax.rsqrt(jnp.mean(xf * xf, axis=-1, keepdims=True) + NORM_EPS)
    return (y * g.astype(jnp.float32)).astype(x.dtype)

def swiglu(x, w_gate, w_up, w_down):
    return (jax.nn.silu(x @ w_gate) * (x @ w_up)) @ w_down

def index_scores(q_idx, w_idx, k_idx):
    dots = jnp.einsum('bthd,bsd->bths', q_idx, k_idx).astype(jnp.float32)
    w = w_idx.astype(jnp.float32) * (IDX_HEADS * IDX_DIM) ** -0.5
    return jnp.einsum('bths,bth->bts', jax.nn.relu(dots), w)

def n_selected(n_keys):
    return min(TOPK_MAX, n_keys // 4)

def select_keys(scores, q_pos, n_keys, k_top):
    k_pos = jnp.arange(n_keys)
    causal = k_pos[None, None, :] <= q_pos[None, :, None]
    _, idx = lax.top_k(jnp.where(causal, scores, NEG_BIG), k_top)
    valid = idx <= q_pos[None, :, None]
    return idx, valid

def gather_rows(rows, idx):
    return jax.vmap(lambda r, i: r[i])(rows, idx)

def sparse_attend(q, kg, vg, valid):
    logits = jnp.einsum('bqhd,bqkhd->bqhk', q, kg).astype(jnp.float32) * HEAD_DIM ** -0.5
    logits = jnp.where(valid[:, :, None, :], logits, -jnp.inf)
    p = jax.nn.softmax(logits, axis=-1)
    return jnp.einsum('bqhk,bqkhd->bqhd', p.astype(vg.dtype), vg)

def s5_scan(u, x0_re, x0_im, a_re, a_im, log_dt, b_re, b_im, c_re, c_im, d_skip):
    f32 = jnp.float32
    bsz, t = u.shape[:2]
    uf = u.astype(f32)
    ug = uf.reshape(bsz, t, N_GROUPS, GROUP_CH)
    dt = jnp.exp(log_dt.astype(f32))[:, None]
    ar, ai = a_re.astype(f32), a_im.astype(f32)
    mag = jnp.exp(dt * ar)
    ab_re, ab_im = mag * jnp.cos(dt * ai), mag * jnp.sin(dt * ai)
    den = ar * ar + ai * ai
    nr, ni = ab_re - 1.0, ab_im
    f_re, f_im = (nr * ar + ni * ai) / den, (ni * ar - nr * ai) / den
    br, bi = b_re.astype(f32), b_im.astype(f32)
    bb_re = f_re[..., None] * br - f_im[..., None] * bi
    bb_im = f_re[..., None] * bi + f_im[..., None] * br
    bu_re = jnp.einsum('gpc,btgc->btgp', bb_re, ug)
    bu_im = jnp.einsum('gpc,btgc->btgp', bb_im, ug)
    a_t_re = jnp.broadcast_to(ab_re, bu_re.shape)
    a_t_im = jnp.broadcast_to(ab_im, bu_im.shape)

    def combine(e1, e2):
        a1r, a1i, b1r, b1i = e1
        a2r, a2i, b2r, b2i = e2
        return (a2r * a1r - a2i * a1i, a2r * a1i + a2i * a1r,
                a2r * b1r - a2i * b1i + b2r, a2r * b1i + a2i * b1r + b2i)

    cr, ci, sr, si = lax.associative_scan(combine, (a_t_re, a_t_im, bu_re, bu_im), axis=1)
    x0r = x0_re.astype(f32)[:, None]
    x0i = x0_im.astype(f32)[:, None]
    xr = cr * x0r - ci * x0i + sr
    xi = cr * x0i + ci * x0r + si
    y = (jnp.einsum('gcp,btgp->btgc', c_re.astype(f32), xr)
         - jnp.einsum('gcp,btgp->btgc', c_im.astype(f32), xi))
    y = y.reshape(bsz, t, SSM_WIDTH) + d_skip.astype(f32) * uf
    return y.astype(u.dtype), xr[:, -1].astype(x0_re.dtype), xi[:, -1].astype(x0_im.dtype)

def setup_inputs(seed: int = 0) -> dict:
    key = jax.random.key(seed)
    keys = iter(jax.random.split(key, 40))
    f32 = jnp.float32

    def nrm(shape, scale):
        return jax.random.normal(next(keys), shape, f32) * scale

    n_pages = PAST_LEN // PAGE_SIZE
    used = DEC_BATCH * n_pages
    n_pool = used + used // 4
    page_table = jax.random.permutation(next(keys), n_pool)[:used].reshape(DEC_BATCH, n_pages).astype(jnp.int32)
    a_im_base = math.pi * jnp.arange(STATE_DIM, dtype=f32)
    return {
        'x_prompt': nrm((BATCH, SEQ, D_MODEL), 1.0),
        'x_sample': nrm((DEC_BATCH, DEC_SEQ, D_MODEL), 1.0),
        'cache_k': nrm((DEPTH, n_pool, PAGE_SIZE, N_HEADS, HEAD_DIM), 1.0),
        'cache_v': nrm((DEPTH, n_pool, PAGE_SIZE, N_HEADS, HEAD_DIM), 1.0),
        'cache_kidx': nrm((DEPTH, n_pool, PAGE_SIZE, IDX_DIM), 1.0),
        'state_ssm_re': nrm((DEPTH, DEC_BATCH, N_GROUPS, STATE_DIM), 0.5),
        'state_ssm_im': nrm((DEPTH, DEC_BATCH, N_GROUPS, STATE_DIM), 0.5),
        'page_table': page_table,
        'g_ffn1': 1.0 + nrm((DEPTH, D_MODEL), 0.02),
        'w1_gate': nrm((DEPTH, D_MODEL, D_FF), D_MODEL ** -0.5),
        'w1_up': nrm((DEPTH, D_MODEL, D_FF), D_MODEL ** -0.5),
        'w1_down': nrm((DEPTH, D_FF, D_MODEL), D_FF ** -0.5),
        'g_mix': 1.0 + nrm((DEPTH, D_MODEL), 0.02),
        'w_in': nrm((DEPTH, D_MODEL, PROJ_DIM), D_MODEL ** -0.5),
        'a_re': -0.5 + nrm((DEPTH, N_GROUPS, STATE_DIM), 0.01),
        'a_im': a_im_base + nrm((DEPTH, N_GROUPS, STATE_DIM), 0.01),
        'log_dt': jax.random.uniform(next(keys), (DEPTH, N_GROUPS), f32, math.log(1e-3), math.log(1e-1)),
        'b_re': nrm((DEPTH, N_GROUPS, STATE_DIM, GROUP_CH), (2 * GROUP_CH) ** -0.5),
        'b_im': nrm((DEPTH, N_GROUPS, STATE_DIM, GROUP_CH), (2 * GROUP_CH) ** -0.5),
        'c_re': nrm((DEPTH, N_GROUPS, GROUP_CH, STATE_DIM), (2 * STATE_DIM) ** -0.5),
        'c_im': nrm((DEPTH, N_GROUPS, GROUP_CH, STATE_DIM), (2 * STATE_DIM) ** -0.5),
        'd_skip': nrm((DEPTH, SSM_WIDTH), 1.0),
        'w_glu': nrm((DEPTH, SSM_WIDTH, SSM_WIDTH), SSM_WIDTH ** -0.5),
        'b_glu': nrm((DEPTH, SSM_WIDTH), 0.01),
        'w_pa': nrm((DEPTH, D_ATTN, D_MODEL), D_ATTN ** -0.5),
        'w_pb': nrm((DEPTH, SSM_WIDTH, D_MODEL), SSM_WIDTH ** -0.5),
        'w_out': nrm((DEPTH, D_MODEL, D_MODEL), D_MODEL ** -0.5),
        'g_ffn2': 1.0 + nrm((DEPTH, D_MODEL), 0.02),
        'w2_gate': nrm((DEPTH, D_MODEL, D_FF), D_MODEL ** -0.5),
        'w2_up': nrm((DEPTH, D_MODEL, D_FF), D_MODEL ** -0.5),
        'w2_down': nrm((DEPTH, D_FF, D_MODEL), D_FF ** -0.5),
        'g_final': 1.0 + nrm((D_MODEL,), 0.02),
    }

def reference(x_prompt, x_sample, cache_k, cache_v, cache_kidx, state_ssm_re, state_ssm_im, page_table,
              g_ffn1, w1_gate, w1_up, w1_down, g_mix, w_in, a_re, a_im, log_dt, b_re, b_im, c_re, c_im,
              d_skip, w_glu, b_glu, w_pa, w_pb, w_out, g_ffn2, w2_gate, w2_up, w2_down, g_final):
    page_size = cache_k.shape[2]
    n_pages = page_table.shape[1]
    past_len = n_pages * page_size

    def attend_prompt(l, q, k, v, qi, ki, wi):
        b, t = q.shape[:2]
        nb = t // Q_BLOCK
        k_top = n_selected(t)

        def to_blocks(a):
            return jnp.swapaxes(a.reshape((b, nb, Q_BLOCK) + a.shape[2:]), 0, 1)

        def block(args):
            qb, qib, wib, t0 = args
            q_pos = t0 + jnp.arange(Q_BLOCK)
            idx, valid = select_keys(index_scores(qib, wib, ki), q_pos, t, k_top)
            return sparse_attend(qb, gather_rows(k, idx), gather_rows(v, idx), valid)

        out = lax.map(block, (to_blocks(q), to_blocks(qi), to_blocks(wi), jnp.arange(nb) * Q_BLOCK))
        return jnp.swapaxes(out, 0, 1).reshape(b, t, N_HEADS, HEAD_DIM)

    def attend_sample(l, q, k, v, qi, ki, wi):
        db, ds = q.shape[:2]
        n_keys = past_len + ds
        ki_past = cache_kidx[l][page_table].reshape(db, past_len, IDX_DIM).astype(ki.dtype)
        ki_all = jnp.concatenate([ki_past, ki], axis=1)
        q_pos = past_len + jnp.arange(ds)
        idx, valid = select_keys(index_scores(qi, wi, ki_all), q_pos, n_keys, n_selected(n_keys))
        in_cache = idx < past_len
        i_c = jnp.minimum(idx, past_len - 1)
        phys = gather_rows(page_table, i_c // page_size)
        off = i_c % page_size
        i_n = jnp.clip(idx - past_len, 0, ds - 1)
        sel = in_cache[..., None, None]
        kg = jnp.where(sel, cache_k[l][phys, off].astype(k.dtype), gather_rows(k, i_n))
        vg = jnp.where(sel, cache_v[l][phys, off].astype(v.dtype), gather_rows(v, i_n))
        return sparse_attend(q, kg, vg, valid)

    def layer(l, x, attend, x0_re, x0_im):
        x = x + 0.5 * swiglu(rmsnorm(x, g_ffn1[l]), w1_gate[l], w1_up[l], w1_down[l])
        h = rmsnorm(x, g_mix[l])
        b, t = x.shape[:2]
        q, k, v, qi, ki, wi, u, gates = jnp.split(h @ w_in[l], PROJ_SPLITS, axis=-1)
        q = q.reshape(b, t, N_HEADS, HEAD_DIM)
        k = k.reshape(b, t, N_HEADS, HEAD_DIM)
        v = v.reshape(b, t, N_HEADS, HEAD_DIM)
        qi = qi.reshape(b, t, IDX_HEADS, IDX_DIM)
        o_a = attend(l, q, k, v, qi, ki, wi).reshape(b, t, D_ATTN)
        y_s, xr, xi = s5_scan(u, x0_re, x0_im, a_re[l], a_im[l], log_dt[l], b_re[l], b_im[l],
                              c_re[l], c_im[l], d_skip[l])
        y_s = jax.nn.gelu(y_s)
        o_b = y_s * jax.nn.sigmoid(y_s @ w_glu[l] + b_glu[l])
        g_a, g_b = jnp.split(jax.nn.sigmoid(gates), 2, axis=-1)
        merged = g_a * (o_a @ w_pa[l]) + g_b * (o_b @ w_pb[l])
        x = x + merged @ w_out[l]
        x = x + 0.5 * swiglu(rmsnorm(x, g_ffn2[l]), w2_gate[l], w2_up[l], w2_down[l])
        return x, (k, v, ki, xr, xi)

    xp, xs = x_prompt, x_sample
    zero_state = jnp.zeros((xp.shape[0], N_GROUPS, STATE_DIM), state_ssm_re.dtype)
    new_p, new_s = [], []
    for l in range(DEPTH):
        xp, st_p = layer(l, xp, attend_prompt, zero_state, zero_state)
        xs, st_s = layer(l, xs, attend_sample, state_ssm_re[l], state_ssm_im[l])
        new_p.append(st_p)
        new_s.append(st_s)

    def stack(states, i):
        return jnp.stack([s[i] for s in states])

    y_prompt = rmsnorm(xp, g_final)
    y_sample = rmsnorm(xs, g_final)
    return (y_prompt, y_sample,
            stack(new_p, 0), stack(new_p, 1), stack(new_p, 2), stack(new_p, 3), stack(new_p, 4),
            stack(new_s, 0), stack(new_s, 1), stack(new_s, 2), stack(new_s, 3), stack(new_s, 4))


_drawn_inputs = setup_inputs


def setup_inputs(seed=0):
    import zlib

    import numpy as np

    out = dict(_drawn_inputs(seed))
    spreads = {}
    factors = {'g_ffn1': 5.503,
     'g_mix': 2.673,
     'a_re': 64.381,
     'b_glu': 200.0,
     'g_ffn2': 8.0,
     'g_final': 23.302,
     'c_re': 4.822,
     'c_im': 4.781}
    for name, (base, spread) in spreads.items():
        noise = np.random.default_rng([zlib.crc32(name.encode()), seed]).standard_normal(out[name].shape)
        drawn = base * np.exp(spread * noise) if base else spread * noise
        out[name] = __import__('jax').numpy.asarray(drawn.astype(out[name].dtype))
    for name, factor in factors.items():
        out[name] = (out[name] * factor).astype(out[name].dtype)
    return out
```

```python
from collections import namedtuple
from contextlib import ExitStack

import numpy as np

import concourse.bass as bass
from concourse import mybir

F32 = mybir.dt.float32
F32R = mybir.dt.float32r
I32 = mybir.dt.int32
ALU = mybir.AluOpType
ACT = mybir.ActivationFunctionType
AX = mybir.AxisListType

P = 128
D = 1024
KD = D // P
TP, TS = 1024, 8
T = TP + TS
NCH = 3
CH = T // NCH
D_FF = 2816
NF = D_FF // P
NPAIR = NF // 2
EPS = 1e-6
PASSES = ((0, 0), (0, 1), (1, 0))


class Space:
    pass


def record(name, fields):
    return namedtuple(name, list(fields))(**fields)


def cols(c):
    return slice(c * CH, (c + 1) * CH)



def norm_act(nc, act, m, s):
    for c in range(NCH):
        for k in range(KD):
            n = c * KD + k
            if n >= 3:
                act.wait_ge(s.sum, s.was.sum + n - 2)
            nc.scalar.activation(m.sg[:, n % 3, :], m.x[:, k, cols(c)], ACT.Square).then_inc(s.sq, 1)
        act.wait_ge(s.var, s.was.var + c + 1)
        nc.scalar.activation(m.rstd[:, 1, :], m.rstd[:, 0, :], ACT.Sqrt).then_inc(s.std, 1)
        for k in range(KD):
            n = c * KD + k
            act.wait_ge(s.xn, s.was.xn + n + 1)
            nc.scalar.activation(m.xn[:, k, 0, cols(c)], m.hf[:, n % 3, :], ACT.Copy).then_inc(s.hi, 1)


def norm_pe(nc, pe, m, s, bank):
    for c in range(NCH):
        if c:
            pe.wait_ge(s.var, s.was.var + c)
        for k in range(KD):
            n = c * KD + k
            pe.wait_ge(s.sq, s.was.sq + n + 1)
            nc.tensor.matmul(m.ps[:, bank, :CH], m.ones[:], m.sg[:, n % 3, :],
                             start=(k == 0), stop=(k == KD - 1)).then_inc(s.sum, 1)


def norm_dve(nc, dve, m, s, bank, gain):
    for c in range(NCH):
        dve.wait_ge(s.sum, s.was.sum + KD * (c + 1))
        nc.vector.tensor_scalar(m.rstd[:, 0, :], m.ps[:, bank, :CH], 1.0 / D, EPS, ALU.mult,
                                ALU.add).then_inc(s.var, 1)
        dve.wait_ge(s.std, s.was.std + c + 1)
        nc.vector.reciprocal(m.rstd[:, 2, :], m.rstd[:, 1, :]).then_inc(s.rs, 1)
        dve.wait_ge(s.rs, s.was.rs + c + 1)
        for k in range(KD):
            n = c * KD + k
            if n >= 3:
                dve.wait_ge(s.lo, s.was.lo + n - 2)
            nc.vector.scalar_tensor_tensor(out=m.hf[:, n % 3, :], in0=m.x[:, k, cols(c)],
                                           scalar=gain[:, k:k + 1], in1=m.rstd[:, 2, :],
                                           op0=ALU.mult, op1=ALU.mult).then_inc(s.xn, 1)


def norm_pool(nc, pool, m, s):
    for n in range(NCH * KD):
        c, k = divmod(n, KD)
        pool.wait_ge(s.hi, s.was.hi + n + 1)
        nc.gpsimd.tensor_tensor(m.xn[:, k, 1, cols(c)], m.hf[:, n % 3, :],
                                m.xn[:, k, 0, cols(c)].bitcast(F32), ALU.subtract).then_inc(s.lo, 1)



def ffn_sp(nc, sp, m, s, w_gate, w_up, w_down, first_wait):
    def load_unit(f, half, static):
        u = 2 * f + half if static is None else static
        w = (w_gate, w_up)[half]
        return u, w

    def gate_up(f, skip_wait=False):
        for half in range(2):
            if not skip_wait:
                sp.wait_ge(s.wlo, s.was.wlo + 2 * f + half - 1)
            w = (w_gate, w_up)[half].rearrange("(k p) n -> p k n", p=P)
            sp.dma_start(m.wr[:, half, :].rearrange("p (k n) -> p k n", k=KD),
                         w[:, :, bass.ds(f * P, P)]).then_inc(s.wraw[half], 16)

    def down(p, skip_wait=False):
        for e in range(2):
            if not skip_wait:
                sp.wait_ge(s.dlo, s.was.dlo + 2 * p + e - 1)
            sp.dma_start(m.dr[:, e, :], w_down[bass.ds((2 * p + e) * P, P), :]).then_inc(s.draw[e], 16)

    first_wait(sp)
    gate_up(0, True)
    gate_up(1)
    down(0, True)
    with sp.Fori(0, (NPAIR - 1) // 2) as i:
        for q in range(2):
            p = 2 * i + 1 + q
            gate_up(2 * p)
            gate_up(2 * p + 1)
            down(p)


def ffn_act(nc, act, m, s):
    def split_unit(f, e, half, used=True):
        act.wait_ge(s.wraw[half], s.was.wraw + 16 * (f + 1))
        if used:
            act.wait_ge(s.up, s.was.up + NCH * (f - 1))
        nc.scalar.activation(m.wh[:, 2 * e + half, 0, :], m.wr[:, half, :], ACT.Copy).then_inc(s.whi, 1)

    def silu(f, used=True):
        for c in range(NCH):
            act.wait_ge(s.gate, s.was.gate + NCH * f + c + 1)
            if used:
                act.wait_ge(s.mul, s.was.mul + NCH * (f - 1) + c + 1)
            nc.scalar.activation(m.sg[:, c, :], m.ps[:, c, :CH], ACT.Silu).then_inc(s.silu, 1)

    def split_down(p, used=True):
        for e in range(2):
            act.wait_ge(s.draw[e], s.was.draw + 16 * (p + 1))
            if used:
                act.wait_ge(s.down, s.was.down + NCH * KD * p)
            nc.scalar.activation(m.dh[:, e, 0, :], m.dr[:, e, :], ACT.Copy).then_inc(s.dhi, 1)

    def pair(p, e0_used=True, last=False):
        f = 2 * p
        for e in range(2):
            if not (last and e):
                for half in range(2):
                    split_unit(f + e + 1, (e + 1) % 2, half, e0_used or e)
            silu(f + e, e0_used or e)
        split_down(p, e0_used)

    for half in range(2):
        split_unit(0, 0, half, False)
    pair(0, False)
    with act.Fori(0, (NPAIR - 1) // 2 - 1) as i:
        pair(2 * i + 1)
        pair(2 * i + 2)
    pair(NPAIR - 2)
    pair(NPAIR - 1, last=True)


def ffn_pool(nc, pool, m, s):
    def split_unit(f, e, half):
        pool.wait_ge(s.whi, s.was.whi + 2 * f + half + 1)
        nc.gpsimd.tensor_tensor(m.wh[:, 2 * e + half, 1, :], m.wr[:, half, :],
                                m.wh[:, 2 * e + half, 0, :].bitcast(F32), ALU.subtract).then_inc(s.wlo, 1)

    def hidden(f, slot):
        for c in range(NCH):
            pool.wait_ge(s.hhi, s.was.hhi + NCH * f + c + 1)
            nc.gpsimd.tensor_tensor(m.hh[:, slot, 1, cols(c)], m.hf[:, c, :],
                                    m.hh[:, slot, 0, cols(c)].bitcast(F32), ALU.subtract).then_inc(s.hlo, 1)

    def split_down(p):
        for e in range(2):
            pool.wait_ge(s.dhi, s.was.dhi + 2 * p + e + 1)
            nc.gpsimd.tensor_tensor(m.dh[:, e, 1, :], m.dr[:, e, :],
                                    m.dh[:, e, 0, :].bitcast(F32), ALU.subtract).then_inc(s.dlo, 1)

    def pair(p, par, last=False):
        for e in range(2):
            if not (last and e):
                for half in range(2):
                    split_unit(2 * p + e + 1, (e + 1) % 2, half)
            hidden(2 * p + e, 2 * par + e)
        split_down(p)

    for half in range(2):
        split_unit(0, 0, half)
    pair(0, 0)
    with pool.Fori(0, (NPAIR - 1) // 2 - 1) as i:
        pair(2 * i + 1, 1)
        pair(2 * i + 2, 0)
    pair(NPAIR - 2, 1)
    pair(NPAIR - 1, 0, last=True)


def ffn_pe(nc, pe, m, s):
    def gate_up(f, e, used=True):
        pe.wait_ge(s.wlo, s.was.wlo + 2 * f + 2)
        for c in range(NCH):
            for half, done in ((0, s.gate), (1, s.up)):
                if used:
                    pe.wait_ge((s.silu, s.mul)[half], s.was.silu + NCH * (f - 1) + c + 1)
                for k in range(KD):
                    for n, (a, b) in enumerate(PASSES):
                        mm = nc.tensor.matmul(m.ps[:, NCH * half + c, :CH],
                                              m.wh[:, 2 * e + half, a, k * P:(k + 1) * P],
                                              m.xn[:, k, b, cols(c)],
                                              start=(k == 0 and n == 0), stop=(k == KD - 1 and n == 2))
                mm.then_inc(done, 1)

    def down(p, par, used=True):
        pe.wait_ge(s.hlo, s.was.hlo + NCH * (2 * p + 2))
        pe.wait_ge(s.dlo, s.was.dlo + 2 * p + 2)
        for o in range(KD):
            for c in range(NCH):
                n = NCH * o + c
                if used or n >= 2:
                    pe.wait_ge(s.acc, s.was.acc + NCH * KD * p + n - 1)
                for e in range(2):
                    for t, (a, b) in enumerate(PASSES):
                        mm = nc.tensor.matmul(m.ps[:, 6 + n % 2, :CH], m.dh[:, e, a, o * P:(o + 1) * P],
                                              m.hh[:, 2 * par + e, b, cols(c)],
                                              start=(e == 0 and t == 0), stop=(e == 1 and t == 2))
                mm.then_inc(s.down, 1)

    pe.wait_ge(s.lo, s.was.lo + NCH * KD)
    gate_up(0, 0, False)
    gate_up(1, 1)
    gate_up(2, 0)
    gate_up(3, 1)
    down(0, 0, False)
    gate_up(4, 0)
    gate_up(5, 1)
    down(1, 1)
    with pe.Fori(0, (NPAIR - 3) // 2) as i:
        for q in range(2):
            f = 4 * i + 2 * q + 6
            gate_up(f, 0)
            gate_up(f + 1, 1)
            down(2 * i + q + 2, q)
    down(NPAIR - 1, 0)


def ffn_dve(nc, dve, m, s):
    def hidden(f, slot, used=True, reuse=True):
        for c in range(NCH):
            dve.wait_ge(s.silu, s.was.silu + NCH * f + c + 1)
            dve.wait_ge(s.up, s.was.up + NCH * f + c + 1)
            if used:
                dve.wait_ge(s.hlo, s.was.hlo + NCH * (f - 1) + c + 1)
            nc.vector.tensor_tensor(m.hf[:, c, :], m.sg[:, c, :], m.ps[:, NCH + c, :CH],
                                    ALU.mult).then_inc(s.mul, 1)
            dve.wait_ge(s.mul, s.was.mul + NCH * f + c + 1)
            nc.vector.tensor_copy(m.hh[:, slot, 0, cols(c)], m.hf[:, c, :]).then_inc(s.hhi, 1)

    def accumulate(p):
        for n in range(NCH * KD):
            o, c = divmod(n, NCH)
            dve.wait_ge(s.down, s.was.down + NCH * KD * p + n + 1)
            xs = m.x[:, o, cols(c)]
            nc.vector.scalar_tensor_tensor(out=xs, in0=m.ps[:, 6 + n % 2, :CH], scalar=0.5, in1=xs,
                                           op0=ALU.mult, op1=ALU.add).then_inc(s.acc, 1)

    hidden(0, 0, False)
    hidden(1, 1)
    hidden(2, 2)
    hidden(3, 3)
    accumulate(0)
    hidden(4, 0)
    hidden(5, 1)
    accumulate(1)
    with dve.Fori(0, (NPAIR - 3) // 2) as i:
        for q in range(2):
            f = 4 * i + 2 * q + 6
            hidden(f, 2 * ((1 + q) % 2))
            hidden(f + 1, 2 * ((1 + q) % 2) + 1)
            accumulate(2 * i + q + 2)
    accumulate(NPAIR - 1)


FFN_SEMS = ("sq", "sum", "var", "std", "rs", "xn", "hi", "lo",
            "whi", "wlo", "gate", "up", "silu", "mul", "hhi", "hlo", "dhi", "dlo", "down", "acc")


NORM_ADDS = dict(sq=NCH * KD, sum=NCH * KD, var=NCH, std=NCH, rs=NCH, xn=NCH * KD, hi=NCH * KD, lo=NCH * KD)
FFN_ADDS = dict(whi=2 * NF, wlo=2 * NF, gate=NCH * NF, up=NCH * NF, silu=NCH * NF, mul=NCH * NF, hhi=NCH * NF,
                hlo=NCH * NF, dhi=NF, dlo=NF, down=NCH * KD * NPAIR, acc=NCH * KD * NPAIR, wraw=16 * NF,
                draw=16 * NPAIR)


def ffn_sems(sem, name):
    s = {n: sem(f"{name}_{n}") for n in FFN_SEMS}
    s["wraw"] = [sem(f"{name}_gate_landed"), sem(f"{name}_up_landed")]
    s["draw"] = [sem(f"{name}_down_even_landed"), sem(f"{name}_down_odd_landed")]
    return s


def after_uses(s, norms, ffns):
    was = {n: norms * c for n, c in NORM_ADDS.items()} | {n: ffns * c for n, c in FFN_ADDS.items()}
    return record("FfnSems", s | {"was": record("Counts", was)})


def ffn_memory(sb, m, name):
    m.wh = sb(f"{name}_weights_split", [P, 4, 2, KD * P], F32R)
    m.wr = sb(f"{name}_weights_raw", [P, 2, KD * P])
    m.hh = sb(f"{name}_hidden_split", [P, 4, 2, T], F32R)
    m.dh = sb(f"{name}_down_split", [P, 2, 2, D], F32R)
    m.dr = sb(f"{name}_down_raw", [P, 2, D])
    m.sg = sb(f"{name}_silu", [P, NCH, CH])
    m.hf = sb(f"{name}_hidden", [P, NCH, CH])
    m.rstd = sb(f"{name}_rstd", [P, 3, CH])
N_HEADS, HD = 8, 64
D_ATTN = N_HEADS * HD
IDX_HEADS, IDX = 4, 64
TOPK = 256
SSM_W = 512
C_Q, C_K, C_V = 0, D_ATTN, 2 * D_ATTN
C_QI = 3 * D_ATTN
C_KI = C_QI + IDX_HEADS * IDX
C_U = C_KI + IDX + IDX_HEADS
C_G = C_U + SSM_W
NB = TP // P
NEG = -1e30
TAKEN = -3e38
GROUPS = (("ki", C_KI, IDX + IDX_HEADS, 1), ("qi", C_QI, P, 2), ("q", C_Q, P, 4), ("k", C_K, P, 4),
          ("v", C_V, P, 4), ("u", C_U, P, 4), ("g", C_G, P, 2 * KD - 2),
          ("g_last", C_G + (2 * KD - 2) * P, P, 2))
FIRST = {}
_n = 0
for _name, _, _, _units in GROUPS:
    FIRST[_name] = _n
    _n += _units
N_UNITS = _n
SCORE_AT = {b: P * sum(range(3, b + 1)) for b in range(2, NB)}
SCORE_COLS = P * sum(range(3, NB + 1))


def mix_memory(sb, m):
    m.qT = sb("q_T", [P, 4, T])
    m.kT = sb("k_T", [P, 4, T])
    m.qiT = sb("q_index_T", [P, 2, T])
    m.kiw = sb("k_index_and_weights_T", [P, T])
    m.ki2 = sb("k_index_T_high", [P, T])
    m.score = sb("scores", [P, SCORE_COLS])
    m.wi = sb("index_weights", [P, NB, IDX_HEADS])
    m.top8 = sb("top8", [P, 8])
    m.smp_i = sb("sample_index_rows", [TS, IDX_HEADS * IDX + IDX_HEADS])
    m.bias01 = sb("bias_of_first_blocks", [P, 2 * P])


def proj_memory(sb, m):
    m.ph = sb("in_weights_split", [P, 2, 2, KD * P], F32R)
    m.pr = sb("in_weights_raw", [P, 2, KD * P])
    m.tmp = sb("projected", [P, 2, T])
    m.stage = sb("token_major", [P, 8, P])
    m.stage_s = sb("token_major_samples", [TS, P])


MIX_SEMS = ("hi", "lo", "mm", "ev", "tr", "tev", "staged", "ki_copied", "wi_T", "wi", "smp_T", "smp_out", "dots", "relu",
            "score", "top", "found", "chain", "bias", "gate_out", "dram", "raw0", "raw1")


def each_unit(engine, body):
    for name, _, _, units in GROUPS:
        f = FIRST[name]
        if units <= 2:
            for j in range(units):
                body(name, j, (f + j) % 2, f + j)
        else:
            with engine.Fori(0, units // 2) as i:
                for e in range(2):
                    body(name, 2 * i + e, (f + e) % 2, 2 * i + (f + e))
        yield name


def run_units(engine, body, after=lambda name: None):
    for name in each_unit(engine, body):
        after(name)


TOKEN_MAJOR = ("ki", "q", "k", "v", "u")
TMAJ_BEFORE = {}
_n = 0
for _name, _, _, _units in GROUPS:
    TMAJ_BEFORE[_name] = _n
    if _name in TOKEN_MAJOR:
        _n += _units
N_TMAJ = _n


def proj_sp(nc, sp, m, s, w_in, o):
    w = w_in.rearrange("(k p) n -> p k n", p=P)
    col = {g[0]: g[1] for g in GROUPS}
    raw = (s.raw0, s.raw1)

    def load(name, j, par, u):
        width = dict((g[0], g[2]) for g in GROUPS)[name]
        if not (isinstance(u, int) and u < 2):
            sp.wait_ge(s.lo, u - 1)
        sp.dma_start(m.pr[:, par, :].rearrange("p (k n) -> p k n", k=KD)[:, :, :width],
                     w[:, :, bass.ds(j * P + col[name], width)]).then_inc(raw[par], 16)

    run_units(sp, load)


def proj_act(nc, act, m, s, o):
    raw = (s.raw0, s.raw1)

    def split(u, par, width=P):
        act.wait_ge(raw[par], 8 * (u - par) + 16)
        if not (isinstance(u, int) and u < 2):
            act.wait_ge(s.mm, NCH * (u - 1))
        src = m.pr[:, par, :].rearrange("p (k n) -> p k n", k=KD)[:, :, :width]
        dst = m.ph[:, par, 0, :].rearrange("p (k n) -> p k n", k=KD)[:, :, :width]
        nc.scalar.activation(dst, src, ACT.Copy).then_inc(s.hi, 1)

    def unit(name, j, par, u):
        width = dict((g[0], g[2]) for g in GROUPS)[name]
        if not (isinstance(u, int) and u == N_UNITS - 1):
            split(u + 1, 1 - par)
        out = {"ki": lambda c: m.kiw[:width, cols(c)],
               "qi": lambda c: m.qiT[:, j, cols(c)]}.get(name, lambda c: m.tmp[:, par, cols(c)])
        if name == "q":
            act.wait_ge(s.score, IDX_HEADS * (NB - 2))
        for c in range(NCH):
            act.wait_ge(s.mm, NCH * u + c + 1)
            src = m.ps[:width, 3 * par + c, :CH]
            if name in ("q", "k"):
                to = m.qT if name == "q" else m.kT
                nc.scalar.activation(to[:, bass.ds(j, 1), cols(c)].rearrange("p a t -> p (a t)"), src, ACT.Copy)
            f = ACT.Sigmoid if name[0] == "g" else ACT.Copy
            nc.scalar.activation(out(c), src, f).then_inc(s.ev, 1)
        if name in TOKEN_MAJOR:
            turn_out(name, j, par, u)
        if name[0] == "g":
            act.wait_ge(s.ev, NCH * (u + 1))
            g = j if name == "g" else j + 2 * KD - 2
            act.dma_start(o.gates[bass.ds(g * P, P), :], m.tmp[:, par, :]).then_inc(s.gate_out, 16)
            act.wait_ge(s.gate_out, 16 * (g + 1))

    def turn_out(name, j, par, u):
        width = IDX if name == "ki" else P
        n = u - FIRST[name] + TMAJ_BEFORE[name]
        if name != "ki":
            act.wait_ge(s.dram, 32 * n)
        for half in range(2):
            act.wait_ge(s.tr, 3 * n + half + 1)
            if name == "u":
                dst = m.stage[:].rearrange("p b n -> p (b n)").rearrange("p (g r c) -> p g r c", g=8, r=8)
                dst = dst[:, :, 4 * half:4 * half + 4, :]
                src = m.ps[:, 6 + half, :].rearrange("p (r g c) -> p g r c", r=4, g=8)
            else:
                dst = m.stage[:, 4 * half:4 * half + 4, :width]
                src = m.ps[:, 6 + half, :].rearrange("p (b n) -> p b n", b=4)[:, :, :width]
            nc.scalar.activation(dst, src, ACT.Copy).then_inc(s.tev, 1)
        act.wait_ge(s.tr, 3 * n + 3)
        nc.scalar.activation(m.stage_s[:, :width], m.ps[:TS, 3 * par, :width], ACT.Copy).then_inc(s.tev, 1)
        act.wait_ge(s.tev, 3 * n + 3)
        tok, smp = o.token_major[name]
        c0 = bass.ds(j * P, width) if name != "ki" else slice(0, IDX)
        if name == "u":
            act.dma_start(tok[:, bass.ds(j * NB * P, NB * P)],
                          m.stage[:].rearrange("p b n -> p (b n)")).then_inc(s.dram, 16)
        else:
            act.dma_start(tok[:, :, c0], m.stage[:, :, :width]).then_inc(s.dram, 16)
        act.dma_start(smp[:, c0], m.stage_s[:, :width]).then_inc(s.dram, 16)

    def after(name):
        if name == "ki":
            act.wait_ge(s.ev, NCH)
            act.dma_start(m.ki2[IDX:2 * IDX, :], m.kiw[0:IDX, :]).then_inc(s.ki_copied, 16)
            act.wait_ge(s.wi_T, 1)
            nc.scalar.activation(m.wi[:].rearrange("p b h -> p (b h)"), m.ps[:, 6, :NB * IDX_HEADS],
                                 ACT.Copy, scale=(IDX_HEADS * IDX) ** -0.5).then_inc(s.wi, 1)
            nc.scalar.activation(m.smp_i[:, 2 * P:], m.ps[:TS, 6, 2 * P:2 * P + IDX_HEADS],
                                 ACT.Copy, scale=(IDX_HEADS * IDX) ** -0.5).then_inc(s.wi, 1)
        if name == "qi":
            act.wait_ge(s.smp_T, 1)
            nc.scalar.activation(m.smp_i[:, :2 * P], m.ps[:TS, 7, :2 * P], ACT.Copy).then_inc(s.wi, 1)
            act.wait_ge(s.wi, 3)
            act.dma_start(o.qi_s, m.smp_i[:, :2 * P]).then_inc(s.smp_out, 16)
            act.dma_start(o.wi_s, m.smp_i[:, 2 * P:]).then_inc(s.smp_out, 16)
            for n, (b, h) in enumerate((b, h) for b in range(2, NB) for h in range(IDX_HEADS)):
                w = (b + 1) * P
                act.wait_ge(s.dots, n + 1)
                if n >= 2:
                    act.wait_ge(s.score, n - 1)
                nc.scalar.activation(m.tmp[:, n % 2, :w],
                                     m.ps[:, 4 + 2 * (n % 2):6 + 2 * (n % 2), :]
                                     .rearrange("p a n -> p (a n)")[:, :w], ACT.Relu).then_inc(s.relu, 1)

    split(0, 0, IDX + IDX_HEADS)
    run_units(act, unit, after)
    act.wait_ge(s.dram, 32 * N_TMAJ)
    act.wait_ge(s.smp_out, 32)
    act.wait_ge(s.gate_out, 16 * 2 * KD)


def proj_pool(nc, pool, m, s):
    def unit(name, j, par, u):
        width = dict((g[0], g[2]) for g in GROUPS)[name]
        pool.wait_ge(s.hi, u + 1)
        v = [x.rearrange("p (k n) -> p k n", k=KD)[:, :, :width]
             for x in (m.ph[:, par, 1, :], m.pr[:, par, :], m.ph[:, par, 0, :])]
        nc.gpsimd.tensor_tensor(v[0], v[1], v[2].bitcast(F32), ALU.subtract).then_inc(s.lo, 1)
    run_units(pool, unit)


def proj_pe(nc, pe, m, s):
    def unit(name, j, par, u):
        width = dict((g[0], g[2]) for g in GROUPS)[name]
        static = isinstance(u, int)
        pe.wait_ge(s.lo, u + 1)
        if not (static and u < 2):
            pe.wait_ge(s.ev, NCH * (u - 1))
        if name == "q":
            pe.wait_ge(s.relu, IDX_HEADS * (NB - 2))
        for c in range(NCH):
            for k in range(KD):
                for n, (a, b) in enumerate(PASSES):
                    mm = nc.tensor.matmul(m.ps[:width, 3 * par + c, :CH],
                                          m.ph[:, par, a, k * P:k * P + width], m.xn[:, k, b, cols(c)],
                                          start=(k == 0 and n == 0), stop=(k == KD - 1 and n == 2))
            mm.then_inc(s.mm, 1)
        if name in TOKEN_MAJOR:
            turn(name, j, par, u)

    def turn(name, j, par, u):
        width = IDX if name == "ki" else P
        n = u - FIRST[name] + TMAJ_BEFORE[name]
        src = m.kiw[:, :] if name == "ki" else m.tmp[:, par, :]
        turn_blocks(src, name, width, par, u, n)

    def turn_blocks(src, name, width, par, u, n):
        pe.wait_ge(s.ev, NCH * (u + 1))
        if name != "ki":
            pe.wait_ge(s.tev, 3 * n)
        for b in range(NB):
            blk = src[:width, NB - 1 - b:TP:NB] if name == "u" else src[:width, b * P:(b + 1) * P]
            mm = nc.tensor.transpose(m.ps[:, 6 + b // 4, (b % 4) * P:(b % 4) * P + width], blk,
                                     m.ident[:width, :width])
            if b % 4 == 3:
                mm.then_inc(s.tr, 1)
        nc.tensor.transpose(m.ps[:TS, 3 * par, :width], src[:width, TP:T],
                            m.ident[:width, :width]).then_inc(s.tr, 1)
        if name == "ki":
            pe.wait_ge(s.tev, 3)
            for b in range(NB):
                mm = nc.tensor.transpose(m.ps[:, 6, b * IDX_HEADS:(b + 1) * IDX_HEADS],
                                         m.kiw[IDX:IDX + IDX_HEADS, b * P:(b + 1) * P],
                                         m.ident[IDX:IDX + IDX_HEADS, IDX:IDX + IDX_HEADS])
            nc.tensor.transpose(m.ps[:TS, 6, 2 * P:2 * P + IDX_HEADS], m.kiw[IDX:IDX + IDX_HEADS, TP:T],
                                m.ident[IDX:IDX + IDX_HEADS, IDX:IDX + IDX_HEADS]).then_inc(s.wi_T, 1)

    def after(name):
        if name != "qi":
            return
        pe.wait_ge(s.ki_copied, 16)
        pe.wait_ge(s.ev, NCH * 3)
        for j in range(2):
            mm = nc.tensor.transpose(m.ps[:TS, 7, j * P:(j + 1) * P], m.qiT[:, j, TP:T], m.ident[:])
        mm.then_inc(s.smp_T, 1)
        pe.wait_ge(s.wi, 3)
        for n, (b, h) in enumerate((b, h) for b in range(2, NB) for h in range(IDX_HEADS)):
            lo = (h % 2) * IDX
            keys = (m.kiw, m.ki2)[h % 2]
            if n >= 2:
                pe.wait_ge(s.relu, n - 1)
            for k0 in range(0, (b + 1) * P, 512):
                k1 = min(k0 + 512, (b + 1) * P)
                mm = nc.tensor.matmul(m.ps[:, 4 + 2 * (n % 2) + k0 // 512, :k1 - k0],
                                      m.qiT[lo:lo + IDX, h // 2, b * P:(b + 1) * P],
                                      keys[lo:lo + IDX, k0:k1], start=True, stop=True)
            mm.then_inc(s.dots, 1)

    run_units(pe, unit, after)


def select_dve(nc, dve, m, s):
    dve.wait_ge(s.wi, 1)
    for n, (b, h) in enumerate((b, h) for b in range(2, NB) for h in range(IDX_HEADS)):
        w = (b + 1) * P
        sc = m.score[:, SCORE_AT[b]:SCORE_AT[b] + w]
        dve.wait_ge(s.relu, n + 1)
        if h == 0:
            nc.vector.tensor_scalar(sc, m.tmp[:, n % 2, :w], m.wi[:, b, 0:1], None,
                                    ALU.mult).then_inc(s.score, 1)
        else:
            dve.wait_ge(s.score, n)
            nc.vector.scalar_tensor_tensor(out=sc, in0=m.tmp[:, n % 2, :w], scalar=m.wi[:, b, h:h + 1],
                                           in1=sc, op0=ALU.mult, op1=ALU.add).then_inc(s.score, 1)
    dve.wait_ge(s.score, IDX_HEADS * (NB - 2))
    for b in range(2, NB):
        diag = m.score[:, SCORE_AT[b] + b * P:SCORE_AT[b] + (b + 1) * P]
        nc.vector.tensor_tensor(diag, diag, m.bias01[:, P:], ALU.add).then_inc(s.chain, 1)
    dve.wait_ge(s.chain, NB - 2)
    for b in range(2, NB):
        sc = m.score[:, SCORE_AT[b]:SCORE_AT[b] + (b + 1) * P]
        done = (b - 2) * TOPK // 8
        with dve.Fori(0, TOPK // 8) as r:
            nc.vector.max(m.top8[:], sc).then_inc(s.top, 1)
            dve.wait_ge(s.top, 2 * (r + done) + 1)
            dve.sem_inc(s.found, 1)
            nc.vector.match_replace(out=sc, in_to_replace=m.top8[:], in_values=sc,
                                    imm_value=TAKEN).then_inc(s.top, 1)
            dve.wait_ge(s.top, 2 * (r + done) + 2)
        nc.vector.tensor_scalar(sc, sc, TAKEN / 2, NEG, ALU.is_gt, ALU.mult).then_inc(s.bias, 1)

STEPS = [(b, h) for b in range(NB) for h in range(N_HEADS)]
ATT_SEMS = ("v_in", "qk", "biased", "neg", "exp", "inv", "scaled", "turned", "pt", "pv", "ohi", "olo")


def att_memory(sb, m):
    m.v = sb("values", [P, NB, D_ATTN])
    m.prob = sb("probs", [P, 2, TP])
    m.pT = sb("probs_T", [P, 2, TP])
    m.st = sb("softmax_stats", [P, 2, 4])


def att_pe(nc, pe, m, s, samples):
    def qk(n):
        b, h = STEPS[n]
        lo = (h % 2) * HD
        if n >= 2:
            pe.wait_ge(s.biased, n - 1)
        for k0 in range(0, (b + 1) * P, 512):
            k1 = min(k0 + 512, (b + 1) * P)
            mm = nc.tensor.matmul(m.ps[:, 2 * (n % 2) + k0 // 512, :k1 - k0],
                                  m.qT[lo:lo + HD, h // 2, b * P:(b + 1) * P],
                                  m.kT[lo:lo + HD, h // 2, k0:k1], start=True, stop=True)
        mm.then_inc(s.qk, 1)

    def turn(n):
        b, h = STEPS[n]
        pe.wait_ge(s.scaled, n + 1)
        if n >= 1:
            pe.wait_ge(s.pt, n)
        for k in range(b + 1):
            mm = nc.tensor.transpose(m.ps[:, 4 + k // 4, (k % 4) * P:(k % 4 + 1) * P],
                                     m.prob[:, n % 2, k * P:(k + 1) * P], m.ident[:])
        mm.then_inc(s.turned, 1)

    def pv(n):
        b, h = STEPS[n]
        lo = (h % 2) * HD
        pe.wait_ge(s.pt, n + 1)
        if n >= 2:
            pe.wait_ge(s.olo, n - 1)
        for k in range(b + 1):
            mm = nc.tensor.matmul(m.ps[lo:lo + HD, 6, :P], m.v[:, k, h * HD:(h + 1) * HD],
                                  m.pT[:, n % 2, k * P:(k + 1) * P], start=(k == 0), stop=(k == b))
        mm.then_inc(s.pv, 1)

    n_last = len(STEPS)
    pe.wait_ge(s.v_in, 16)
    for n in range(n_last + 2):
        samples(n)
        if n < n_last:
            qk(n)
        if 1 <= n <= n_last:
            turn(n - 1)
        if n >= 2:
            pv(n - 2)


def att_dve(nc, dve, m, s, samples):
    def bias(n):
        b, h = STEPS[n]
        w = (b + 1) * P
        by = m.bias01[:, (1 - b) * P:2 * P] if b < 2 else m.score[:, SCORE_AT[b]:SCORE_AT[b] + w]
        dve.wait_ge(s.qk, n + 1)
        if n >= 2:
            dve.wait_ge(s.turned, n - 1)
        nc.vector.tensor_tensor_reduce(m.prob[:, n % 2, :w],
                                       m.ps[:, 2 * (n % 2):2 * (n % 2) + 2, :].rearrange("p a n -> p (a n)")[:, :w],
                                       by, HD ** -0.5, TAKEN, ALU.add, ALU.max,
                                       m.st[:, n % 2, 0:1]).then_inc(s.biased, 1)
        dve.wait_ge(s.biased, n + 1)
        nc.vector.tensor_scalar(m.st[:, n % 2, 1:2], m.st[:, n % 2, 0:1], -1.0, None,
                                ALU.mult).then_inc(s.neg, 1)

    def normalise(n):
        b, h = STEPS[n]
        w = (b + 1) * P
        dve.wait_ge(s.exp, n + 1)
        nc.vector.reciprocal(m.st[:, n % 2, 3:4], m.st[:, n % 2, 2:3]).then_inc(s.inv, 1)
        dve.wait_ge(s.inv, n + 1)
        nc.vector.tensor_scalar(m.prob[:, n % 2, :w], m.prob[:, n % 2, :w], m.st[:, n % 2, 3:4], None,
                                ALU.mult).then_inc(s.scaled, 1)

    def low(n):
        b, h = STEPS[n]
        lo = (h % 2) * HD
        dve.wait_ge(s.ohi, n + 1)
        q = slice(b * P, (b + 1) * P)
        nc.vector.tensor_tensor(m.xn[lo:lo + HD, h // 2, 1, q], m.ps[lo:lo + HD, 6, :P],
                                m.xn[lo:lo + HD, h // 2, 0, q].bitcast(F32), ALU.subtract).then_inc(s.olo, 1)

    n_last = len(STEPS)
    for n in range(n_last + 3):
        samples(n)
        if n < n_last:
            bias(n)
        if 1 <= n <= n_last:
            normalise(n - 1)
        if n >= 3:
            low(n - 3)


def att_act(nc, act, m, s, samples):
    def exp(n):
        b, h = STEPS[n]
        w = (b + 1) * P
        act.wait_ge(s.neg, n + 1)
        nc.scalar.activation(m.prob[:, n % 2, :w], m.prob[:, n % 2, :w], ACT.Exp, bias=m.st[:, n % 2, 1:2],
                             accum_out=m.st[:, n % 2, 2:3]).then_inc(s.exp, 1)

    def keep_turned(n):
        b, h = STEPS[n]
        w = (b + 1) * P
        act.wait_ge(s.turned, n + 1)
        if n >= 2:
            act.wait_ge(s.pv, n - 1)
        nc.scalar.activation(m.pT[:, n % 2, :w],
                             m.ps[:, 4:6, :].rearrange("p a n -> p (a n)")[:, :w], ACT.Copy).then_inc(s.pt, 1)

    def high(n):
        b, h = STEPS[n]
        lo = (h % 2) * HD
        act.wait_ge(s.pv, n + 1)
        nc.scalar.activation(m.xn[lo:lo + HD, h // 2, 0, b * P:(b + 1) * P], m.ps[lo:lo + HD, 6, :P],
                             ACT.Copy).then_inc(s.ohi, 1)

    n_last = len(STEPS)
    for n in range(n_last + 3):
        samples(n)
        if n < n_last:
            exp(n)
        if 1 <= n <= n_last:
            keep_turned(n - 1)
        if n >= 3:
            high(n - 3)


PAGE = 128
N_PAGES = TP // PAGE
NK = N_PAGES * PAGE + 1
SMP_SEMS = ("small", "small_out", "bcast", "prod", "c", "pc", "dots", "tree",
            "rows", "turned", "taken", "top", "found", "mask_T", "k0", "k1", "v0", "v1", "kdone", "ln_out", "ln_in",
            "peak", "exp", "total", "ready", "olo", "vmm")
AT_NEW, AT_DOTS, AT_ROWS, AT_TOP = 2, 8, 9, 11
ROUNDS = 2
AT_MASK = AT_TOP + TOPK // 8 // ROUNDS
AT_SOFT = AT_MASK + 3
AT_PV = AT_SOFT + 3
PV_EVERY = 3
AT_OUT = AT_PV + PV_EVERY * TS


def smp_memory(sb, m):
    m.kidx = sb("past_k_index", [P, TS, N_PAGES, IDX])
    m.newi = sb("new_index_rows", [TS, IDX_HEADS + 1, IDX])
    m.sm8 = sb("new_small", [TS, 32 + IDX_HEADS * IDX])


def smp_views(m):
    x = m.x[:].rearrange("p k t -> p (k t)")
    m.page = x[:, :2 * N_PAGES * D_ATTN].rearrange("p (b j c) -> p b j c", b=2, j=N_PAGES)
    h = m.spare
    at = [0]

    def take(n, rows=P):
        at[0] += n
        return h[:rows, at[0] - n:at[0]]

    m.qb = take(TS * D_ATTN).rearrange("p (b c) -> p b c", b=TS)
    m.iprod = take(N_PAGES * IDX_HEADS * IDX)
    m.dot = take(TS * N_PAGES * IDX_HEADS).rearrange("p (b j h) -> p b j h", b=TS, j=N_PAGES)
    m.sk = take(TS * N_PAGES).rearrange("p (b j) -> p b j", b=TS)
    m.wib = take(TS * IDX_HEADS)
    m.kb = take(N_PAGES * TS).rearrange("p (j b) -> p j b", j=N_PAGES)
    m.lg = take(TS * N_PAGES * N_HEADS).rearrange("p (b j h) -> p b j h", b=TS, j=N_PAGES)
    m.s64 = take(8 * TS * N_HEADS).rearrange("p (n c) -> p n c", n=8)
    m.of = take(4 * TS).rearrange("p (j b) -> p j b", j=4)
    m.pn = take(TS * N_HEADS, TS).rearrange("p (b h) -> p b h", b=TS)
    m.vnew = take(D_ATTN, TS)
    assert at[0] <= KD * T
    m.qib = m.qiT[:].rearrange("p j t -> p (j t)")[:, :TS * IDX_HEADS * IDX]
    m.qkn = m.kiw[:TS, :2 * D_ATTN].rearrange("p (n c) -> p n c", n=2)
    m.row = m.ki2[:TS, :NK]


def smp_load(sp, m, i, b, dst, src, land):
    with sp.Fori(0, N_PAGES) as j:
        page = sp.value_load(m.table[0:1, bass.ds(j + b * N_PAGES, 1)], min_val=0, max_val=i.cache_k.shape[0] - 1)
        sp.dma_start(dst[:, bass.ds(j, 1), :].rearrange("p a c -> p (a c)"),
                     src[bass.ds(page, 1)].rearrange("a p c -> p (a c)")).then_inc(land, 16)


def smp_sp(nc, sp, m, s, i, o):
    sp.dma_start(m.qkn[:, 0, :], o.q_s).then_inc(s.small_out, 16)
    sp.dma_start(m.qkn[:, 1, :], o.k_s).then_inc(s.small_out, 16)
    sp.dma_start(m.vnew, o.v_s).then_inc(s.small_out, 16)
    sp.dma_start(m.newi[:, IDX_HEADS, :], o.ki_s).then_inc(s.small_out, 16)
    sp.dma_start(m.newi[:, :IDX_HEADS, :].rearrange("p h d -> p (h d)"), o.qi_s).then_inc(s.small_out, 16)
    sp.dma_start(m.sm8[:, 0:IDX_HEADS], o.wi_s).then_inc(s.small_out, 16)
    for dst, src in ((m.qib, o.qi_s), (m.wib, o.wi_s), (m.qb.rearrange("p b c -> p (b c)"), o.q_s)):
        sp.dma_start(dst, src.rearrange("(a b) c -> a (b c)", a=1).to_broadcast([P, dst.shape[1]])).then_inc(s.bcast, 16)
    for b in range(TS):
        if b >= 2:
            sp.wait_ge(s.kdone, b - 1)
        smp_load(sp, m, i, b, m.page[:, b % 2], i.cache_k, (s.k0, s.k1)[b % 2])
    sp.wait_ge(s.ln_out, 1)
    sp.dma_start(o.ln_s, m.sm8[:, 16:24]).then_inc(s.small, 16)
    sp.wait_ge(s.small, 16)
    sp.dma_start(m.s64[:, 4, :], o.ln_s.rearrange("(a b) c -> a (b c)", a=1)
                 .to_broadcast([P, TS * N_HEADS])).then_inc(s.ln_in, 16)
    for b in range(TS):
        sp.wait_ge(*((s.kdone, TS - 1 + b) if b < 2 else (s.vmm, b - 1)))
        smp_load(sp, m, i, b, m.page[:, b % 2], i.cache_v, (s.v0, s.v1)[b % 2])


def smp_pool(nc, pool, m, s):
    G = nc.gpsimd
    steps = [0]

    def dot(a, b, out, done):
        prod, x, y = a
        G.tensor_tensor(prod, x, y, ALU.mult).then_inc(s.tree, 1)
        steps[0] += 1
        n = IDX // 2
        while n >= 1:
            pool.wait_ge(s.tree, steps[0])
            to = b(n)
            if n == 1:
                G.tensor_tensor(out, to[0], to[1], ALU.add).then_inc(done, 1)
            else:
                G.tensor_tensor(to[0], to[0], to[1], ALU.add).then_inc(s.tree, 1)
                steps[0] += 1
            n //= 2

    pool.wait_ge(s.bcast, 32 + 16)
    ip = m.iprod.rearrange("p (j h d) -> p j h d", j=N_PAGES, h=IDX_HEADS)
    for b in range(TS):
        if b:
            pool.wait_ge(s.dots, b)
        sh = [P, N_PAGES, IDX_HEADS, IDX]
        q = m.qib[:, b * IDX_HEADS * IDX:(b + 1) * IDX_HEADS * IDX].rearrange("p (a h d) -> p a h d", a=1, h=IDX_HEADS)
        dot((ip, m.kidx[:, b, :, None, :].to_broadcast(sh), q.to_broadcast(sh)),
            lambda n: (ip[:, :, :, :n], ip[:, :, :, n:2 * n]), m.dot[:, b, :, :, None], s.dots)
    for b in range(TS):
        pool.wait_ge((s.k0, s.k1)[b % 2], 16 * N_PAGES * (b // 2 + 1))
        pg = m.page[:, b % 2]
        pv = pg.rearrange("p j (h d) -> p j h d", h=N_HEADS)
        dot((pg, pg, m.qb[:, b:b + 1, :].to_broadcast([P, N_PAGES, D_ATTN])),
            lambda n: (pv[:, :, :, :n], pv[:, :, :, n:2 * n]), m.lg[:, b, :, :, None], s.kdone)
    pool.wait_ge(s.peak, 1)
    G.partition_all_reduce(m.s64[:, 1, :], m.s64[:, 0, :], P, bass.bass_isa.ReduceOp.max).then_inc(s.pc, 1)
    pool.wait_ge(s.total, 1)
    G.partition_all_reduce(m.s64[:, 3, :], m.s64[:, 2, :], P, bass.bass_isa.ReduceOp.add).then_inc(s.pc, 1)


def smp_dve(nc, dve, m, s):
    c = [0]

    def link(ins):
        c[0] += 1
        ins.then_inc(s.c, 1)
        dve.wait_ge(s.c, c[0])

    V = nc.vector
    S = lambda n: m.s64[:, n, :]
    S2 = lambda n: m.s64[:, n, :].rearrange("p (b h) -> p b h", b=TS)
    by_page = [P, TS, N_PAGES, N_HEADS]
    per_head = lambda n: m.s64[:, n, :].rearrange("p (b a h) -> p b a h", b=TS, a=1).to_broadcast(by_page)

    def new_keys():
        dve.wait_ge(s.small_out, 96)
        ip = m.sm8[:, 32:].rearrange("p (h d) -> p h d", h=IDX_HEADS)
        link(V.tensor_tensor(ip, m.newi[:, :IDX_HEADS, :],
                             m.newi[:, IDX_HEADS:, :].to_broadcast([TS, IDX_HEADS, IDX]), ALU.mult))
        link(V.tensor_reduce(m.sm8[:, 4:8], ip, AX.X, ALU.add))
        link(V.tensor_scalar(m.sm8[:, 4:8], m.sm8[:, 4:8], 0.0, None, ALU.max))
        link(V.tensor_tensor(m.sm8[:, 4:8], m.sm8[:, 4:8], m.sm8[:, 0:4], ALU.mult))
        link(V.tensor_reduce(m.row[:, NK - 1:NK], m.sm8[:, 4:8], AX.X, ALU.add))
        link(V.tensor_tensor(m.qkn[:, 0, :], m.qkn[:, 0, :], m.qkn[:, 1, :], ALU.mult))
        link(V.tensor_reduce(m.sm8[:, 8:16], m.qkn[:, 0, :].rearrange("p (h d) -> p h d", h=N_HEADS), AX.X, ALU.add))

    def index_scores():
        dve.wait_ge(s.dots, TS)
        link(V.tensor_scalar(m.dot, m.dot, 0.0, None, ALU.max))
        link(V.tensor_tensor(m.dot, m.dot, m.wib.rearrange("p (b a h) -> p b a h", b=TS, a=1)
                             .to_broadcast([P, TS, N_PAGES, IDX_HEADS]), ALU.mult))
        V.tensor_reduce(m.sk, m.dot, AX.X, ALU.add).then_inc(s.rows, 1)

    def take_rows():
        for r in range(2):
            dve.wait_ge(s.turned, r + 1)
            V.tensor_copy(m.row[:, r * 4 * P:(r + 1) * 4 * P], m.ps[:TS, 7, :]).then_inc(s.taken, 1)
        dve.wait_ge(s.taken, 2)

    def select(n):
        for r in range((n - AT_TOP) * ROUNDS, (n - AT_TOP + 1) * ROUNDS):
            V.max(m.sm8[:, 24:32], m.row).then_inc(s.top, 1)
            dve.wait_ge(s.top, 2 * r + 1)
            V.match_replace(out=m.row, in_to_replace=m.sm8[:, 24:32], in_values=m.row,
                            imm_value=TAKEN).then_inc(s.top, 1)
            dve.wait_ge(s.top, 2 * r + 2)

    def mask():
        link(V.tensor_scalar(m.row, m.row, TAKEN / 2, NEG, ALU.is_gt, ALU.mult))
        dve.sem_inc(s.rows, 1)
        V.tensor_scalar(m.sm8[:, 16:24], m.sm8[:, 8:16], HD ** -0.5, m.row[:, NK - 1:NK], ALU.mult,
                        ALU.add).then_inc(s.ln_out, 1)

    def maxima():
        dve.wait_ge(s.mask_T, 1)
        link(V.tensor_copy(m.kb.rearrange("p j b -> p (j b)"), m.ps[:, 7, :N_PAGES * TS]))
        dve.wait_ge(s.kdone, TS)
        link(V.tensor_scalar(m.lg, m.lg, HD ** -0.5, None, ALU.mult))
        link(V.tensor_tensor(m.lg, m.lg, m.kb.rearrange("p j (b a) -> p b j a", a=1).to_broadcast(by_page), ALU.add))
        dve.wait_ge(s.ln_in, 16)
        link(V.tensor_reduce(S2(0), m.lg.rearrange("p b j h -> p b h j"), AX.X, ALU.max))
        V.tensor_tensor(S(0), S(0), S(4), ALU.max).then_inc(s.peak, 1)

    def subtract():
        dve.wait_ge(s.pc, 1)
        link(V.tensor_tensor(S(5), S(4), S(1), ALU.subtract))
        V.tensor_tensor(m.lg, m.lg, per_head(1), ALU.subtract).then_inc(s.ready, 1)

    def totals():
        dve.wait_ge(s.exp, 2)
        V.tensor_reduce(S2(2), m.lg.rearrange("p b j h -> p b h j"), AX.X, ALU.add).then_inc(s.total, 1)

    def probabilities():
        dve.wait_ge(s.pc, 2)
        link(V.tensor_tensor(S(6), S(3), S(5), ALU.add))
        link(V.reciprocal(S(7), S(6)))
        link(V.tensor_tensor(m.lg, m.lg, per_head(7), ALU.mult))
        link(V.tensor_tensor(S(5), S(5), S(7), ALU.mult))
        V.tensor_tensor(m.pn, m.s64[:TS, 5, :].rearrange("p (b h) -> p b h", b=TS),
                        m.ident[:TS, :TS, None].to_broadcast([TS, TS, N_HEADS]), ALU.mult).then_inc(s.ready, 1)

    def outputs():
        dve.wait_ge(s.vmm, TS)
        pv = m.ps[:, 7, P:P + 4 * TS * 2].rearrange("p (b j e) -> p j b e", j=4, e=2)
        for e in range(2):
            r = slice(64 * e, 64 * e + 64)
            link(V.tensor_copy(m.of[r], pv[r, :, :, e]))
        link(V.tensor_copy(m.xn[:, :4, 0, TP:T], m.of))
        V.tensor_tensor(m.xn[:, :4, 1, TP:T], m.of, m.xn[:, :4, 0, TP:T].bitcast(F32), ALU.subtract).then_inc(s.olo, 1)

    stages = {AT_NEW: new_keys, AT_DOTS: index_scores, AT_ROWS: take_rows, AT_MASK: mask, AT_SOFT: maxima,
              AT_SOFT + 1: subtract, AT_SOFT + 2: totals, AT_PV: probabilities, AT_OUT: outputs}

    def before(n):
        if n in stages:
            stages[n]()
        elif AT_TOP <= n < AT_MASK:
            select(n)
    return before


def smp_pe(nc, pe, m, s):
    def rows():
        pe.wait_ge(s.rows, 1)
        for r in range(2):
            if r:
                pe.wait_ge(s.taken, 1)
            for j in range(4 * r, 4 * r + 4):
                mm = nc.tensor.transpose(m.ps[:TS, 7, (j % 4) * P:(j % 4 + 1) * P], m.sk[:, :, j], m.ident[:])
            mm.then_inc(s.turned, 1)

    def biases():
        pe.wait_ge(s.rows, 2)
        for j in range(N_PAGES):
            mm = nc.tensor.transpose(m.ps[:, 7, j * TS:(j + 1) * TS], m.row[:, j * P:(j + 1) * P],
                                     m.ident[:TS, :TS])
        mm.then_inc(s.mask_T, 1)

    def values(b):
        if b == 0:
            pe.wait_ge(s.taken, 2)
            pe.wait_ge(s.ready, 2)
        pe.wait_ge((s.v0, s.v1)[b % 2], 16 * N_PAGES * (b // 2 + 1))
        for j in range(4):
            out = m.ps[:, 7, P + 8 * b + 2 * j:P + 8 * b + 2 * j + 2]
            for g in range(N_PAGES):
                nc.tensor.matmul(out, m.page[:, b % 2, g, j * P:(j + 1) * P], m.lg[:, b, g, 2 * j:2 * j + 2],
                                 start=(g == 0), stop=False)
            mm = nc.tensor.matmul(out, m.vnew[:, j * P:(j + 1) * P], m.pn[:, b, 2 * j:2 * j + 2],
                                  start=False, stop=True)
        mm.then_inc(s.vmm, 1)

    def before(n):
        if n == AT_ROWS:
            rows()
        elif n == AT_MASK:
            biases()
        elif AT_PV <= n < AT_OUT and (n - AT_PV) % PV_EVERY == 0:
            values((n - AT_PV) // PV_EVERY)
    return before


def smp_act(nc, act, m, s):
    def before(n):
        if n == AT_SOFT + 1:
            act.wait_ge(s.ready, 1)
            lg = m.lg.rearrange("p b j h -> p (b j h)")
            nc.scalar.activation(lg, lg, ACT.Exp).then_inc(s.exp, 1)
            nc.scalar.activation(m.s64[:, 5, :], m.s64[:, 5, :], ACT.Exp).then_inc(s.exp, 1)
    return before
NG, GC, NS = 32, 16, 64
L = 8
NCK = TP // L
NI = NG // 2
HI = NI // 2
TWO_PI = (6.28125, 0.0019350051879882812, 3.0199159819567529e-07)
MAGIC = 12582912.0
SSM_SEMS = ("load", "c", "a", "dve", "pe", "evac", "kz_out", "m_in", "zero", "u_load", "u_T", "out", "late", "wg", "glu",
            "sig", "gate", "hi")
NAMES = ("ar", "ai", "dt", "dtr", "dti", "n", "r", "mag", "sin", "sh", "er", "ei", "abr", "abi", "r8",
         "den", "nr", "fr", "fi", "t1", "t2", "e8r", "e8i", "u1", "u2")
SLOT = {n: k for k, n in enumerate(NAMES)}


def ssm_memory_keep(sb, m):
    m.Z = sb("chunk_states", [P, 2, NI, NCK + 1])
    m.y = sb("y_by_chunk", [P, L, SSM_W])
    m.ys = sb("y_samples", [TS, SSM_W])
    m.x0 = sb("sample_states", [P, 2, NI, TS])
    m.xs = sb("sample_new_states", [P, 2, NI, TS])
    z = m.Z[:].rearrange("p n i k -> p (n i k)")
    y = m.y[:].rearrange("p t c -> p (t c)")
    m.Qt = z[:, :2 * NI * L * GC].rearrange("p (n i r c) -> p n i r c", n=2, i=NI, r=L)
    m.xi = z[:TS, :2 * NI * P].rearrange("p (n s) -> p n s", n=2)
    m.Kz = y[:GC].rearrange("p (g t) -> p g t", g=NG)
    m.ut = y
    m.Sm = y[:, :2 * HI * NCK].rearrange("p (n i k) -> p n i k", n=2, i=HI)
    m.tz = y[:, 2 * HI * NCK:2 * HI * NCK + HI * (NCK + 1)]


def ssm_memory_base(sb, m):
    m.W = sb("state_to_output", [P, 2, NI, L + 1, GC])
    m.QL = sb("input_to_state_T", [P, NI, 2, P])
    m.M = sb("input_to_output", [P, NG, P])
    m.sc = sb("per_state", [P, len(NAMES), NI])
    m.pw = sb("powers", [P, 2, NI, L + 1])


def ssm_memory_build(sb, m):
    m.tb = sb("build_products", [P, NI * (L + 1) * GC])
    m.rows = sb("parameter_rows", [NI, 3, P])
    m.ldt = sb("log_dt_rows", [NI, 2])
    m.bin = sb("b_in", [P, 2, NI, GC])
    m.bb = sb("b_bar", [P, 2, NI, GC])
    m.cin = sb("c_in", [P, 2, 4, 2, NS])
    m.cs = sb("c_by_state", [P, 2, NI, GC])


def ssm_memory_run(sb, m):
    m.U = sb("chunk_inputs", [P, NG, NCK])
    m.u2 = m.U[:].rearrange("p g k -> p (g k)").rearrange("p (g r c) -> p g r c", g=NG, r=L)
    m.uT = sb("sample_inputs_T", [GC, NG, TS])
    m.us = sb("u_samples", [TS, SSM_W])
    m.us2 = m.us
    m.E = sb("phases", [P, 2, HI, NCK + 1])
    m.db = sb("d_skip_on_all", [P, SSM_W])


def ssm_memory_glu(sb, m):
    m.yT = sb("y_T", [P, 4, T])
    m.wgl = sb("w_glu", [P, 4, SSM_W])
    m.bgr = sb("b_glu_rows", [4, P])
    m.bg = sb("b_glu_column", [P, 4])
    m.gl = sb("glu", [P, 2, CH])
    m.so = sb("state_out", [NI, 2, P])
    m.sos = sb("state_out_samples", [TS, 2, NI * P])


def ssm_sp(nc, sp, m, s, i, o):
    sp.dma_start(m.rows[:, 0, :], i.a_re.rearrange("(i e) s -> i (e s)", e=2)).then_inc(s.load, 16)
    sp.dma_start(m.rows[:, 1, :], i.a_im.rearrange("(i e) s -> i (e s)", e=2)).then_inc(s.load, 16)
    sp.dma_start(m.ldt[:], i.log_dt.rearrange("(i e) -> i e", e=2)).then_inc(s.load, 16)
    for n, b in enumerate((i.b_re, i.b_im)):
        sp.dma_start(m.bin[:, n], b.rearrange("(i e) s c -> (e s) i c", e=2)).then_inc(s.load, 16)
    for n, c in enumerate((i.c_re, i.c_im)):
        for d in range(2):
            sp.dma_start(m.cin[:, n, :, d, :], c.rearrange("(q g) c s -> (g c) q s", q=4)).then_inc(s.load, 16)
    sp.wait_ge(s.zero, 1)
    sp.wait_ge(s.evac, 16)
    for r in range(L):
        t0 = L - 1 - r
        sp.dma_start(m.M[GC * r:GC * (r + 1), :, GC * t0:], m.Kz[:, :, :P - GC * t0]).then_inc(s.m_in, 16)
    sp.wait_ge(s.m_in, 16 * L)
    sp.dma_start(m.ut, o.u_p).then_inc(s.u_load, 16)
    sp.dma_start(m.us[:], o.u_s).then_inc(s.u_load, 16)
    for n, x in enumerate((i.state_re, i.state_im)):
        sp.dma_start(m.xi[:, n, :], x).then_inc(s.u_load, 16)
    sp.wait_ge(s.a, 24)
    sp.dma_start(m.U[:].rearrange("p g k -> p (g k)"), o.u_p).then_inc(s.wg, 16)
    sp.dma_start(m.us2[:], o.u_s).then_inc(s.wg, 16)
    sp.dma_start(m.db[:], i.d_skip.rearrange("(a n) -> a n", a=1).to_broadcast([P, SSM_W])).then_inc(s.wg, 16)
    sp.wait_ge(s.late, 1)
    sp.dma_start(m.wgl[:], i.w_glu.rearrange("(k p) n -> p k n", p=P)).then_inc(s.wg, 16)
    sp.dma_start(m.bgr[:], i.b_glu.rearrange("(k p) -> k p", p=P)).then_inc(s.wg, 16)
    sp.wait_ge(s.out, 2)
    for n in range(2):
        sp.dma_start((o.ssm_re_p, o.ssm_im_p)[n], m.so[:, n, :]).then_inc(s.kz_out, 16)
        sp.dma_start((o.ssm_re_s, o.ssm_im_s)[n], m.sos[:, n, :]).then_inc(s.kz_out, 16)
    sp.wait_ge(s.kz_out, 64)


def ssm_pool(nc, pool, m, s):
    nc.gpsimd.memset(m.M[:], 0.0).then_inc(s.zero, 1)


def ssm_act(nc, act, m, s):
    A = nc.scalar.activation
    k = lambda n: m.sc[:, SLOT[n], :]
    act.wait_ge(s.dve, 1)
    A(k("dt"), k("dt"), ACT.Exp).then_inc(s.a, 1)
    act.wait_ge(s.dve, 2)
    A(k("mag"), k("dtr"), ACT.Exp).then_inc(s.a, 1)
    A(k("r8"), k("dtr"), ACT.Exp, scale=float(L)).then_inc(s.a, 1)
    A(k("sin"), k("r"), ACT.Sin).then_inc(s.a, 1)
    A(k("sh"), k("r"), ACT.Sin, scale=0.5).then_inc(s.a, 1)
    n = [0]

    def evac(out, src):
        n[0] += 1
        act.wait_ge(s.pe, 1 + n[0])
        A(out, src, ACT.Copy).then_inc(s.evac, 1)

    for bank in range(8):
        evac(m.QL[:, 2 * bank:2 * bank + 2].rearrange("p i n s -> p (i n s)"), m.ps[:, bank, :])
    for bank in range(8):
        evac(m.Kz[:].rearrange("p (q i e) t -> p q e i t", q=4, e=2)[:, bank % 4, bank // 4],
             m.ps[:GC, bank, :].rearrange("p (i t) -> p i t", i=4))
    for bank in range(8):
        act.wait_ge(s.u_T, bank + 1)
        A(m.U[:, 4 * bank:4 * bank + 4, :].rearrange("p g t -> p (g t)"), m.ps[:, bank, :],
          ACT.Copy).then_inc(s.a, 1)
    act.wait_ge(s.u_T, 9)
    A(m.uT[:].rearrange("p g t -> p (g t)"), m.ps[:GC, 0, :NG * TS], ACT.Copy).then_inc(s.a, 1)
    A(m.x0[:].rearrange("p n g t -> p (n g t)"), m.ps[:, 1, :2 * NI * TS], ACT.Copy).then_inc(s.a, 1)
    for bank in range(8):
        act.wait_ge(s.u_T, 10 + bank)
        A(m.y[:].rearrange("p t (q i e c) -> p q e i t c", q=4, i=4, e=2)[:, bank % 4, bank // 4],
          m.ps[:, bank, :].rearrange("p (g t c) -> p g t c", g=4, t=L), ACT.Copy).then_inc(s.a, 1)
    act.wait_ge(s.u_T, 18)
    A(m.ys[:].rearrange("p (i e c) -> p e i c", e=2, c=GC),
      m.ps[:TS, 0:2, :NI * GC].rearrange("p e (i c) -> p e i c", c=GC), ACT.Copy).then_inc(s.a, 1)
    act.wait_ge(s.dve, 8)
    A(m.y[:].rearrange("p t c -> p (t c)"), m.y[:].rearrange("p t c -> p (t c)"),
      ACT.Gelu_apprx_tanh).then_inc(s.a, 1)
    A(m.ys[:], m.ys[:], ACT.Gelu_apprx_tanh).then_inc(s.late, 1)
    act.wait_ge(s.late, 1)
    for h in range(8):
        j, half = h // 2, h % 2
        act.wait_ge(s.u_T, 19 + h)
        A(m.yT[:, j, :TP].rearrange("p (k t) -> p t k", t=L)[:, 4 * half:4 * half + 4, :],
          m.ps[:, h, :].rearrange("p (t k) -> p t k", t=4), ACT.Copy).then_inc(s.a, 1)
    act.wait_ge(s.u_T, 27)
    A(m.yT[:, :, TP:T], m.ps[:, 0, :4 * TS].rearrange("p (j t) -> p j t", j=4), ACT.Copy).then_inc(s.a, 1)
    A(m.bg[:], m.ps[:, 1, :4], ACT.Copy).then_inc(s.a, 1)
    A(m.so[:].rearrange("p n s -> p (n s)"), m.ps[:NI, 2, :2 * P], ACT.Copy).then_inc(s.out, 1)
    for n in range(8):
        act.wait_ge(s.u_T, 28 + n)
        A(m.sos[:, n // 4, (n % 4) * 512:(n % 4 + 1) * 512], m.ps[:TS, 3 + n % 4, :], ACT.Copy).then_inc(s.a, 1)
    act.wait_ge(s.a, 43)
    act.sem_inc(s.out, 1)
    for n in range(4 * NCH):
        j, c = divmod(n, NCH)
        act.wait_ge(s.glu, n + 1)
        if n >= 2:
            act.wait_ge(s.gate, n - 1)
        A(m.gl[:, n % 2, :], m.ps[:, n % 4, :CH], ACT.Sigmoid, bias=m.bg[:, j:j + 1]).then_inc(s.sig, 1)
        act.wait_ge(s.gate, n + 1)
        A(m.xn[:, 4 + j, 0, cols(c)], m.gl[:, n % 2, :], ACT.Copy).then_inc(s.hi, 1)


def ssm_pe(nc, pe, m, s):
    tr = nc.tensor.transpose
    mm = nc.tensor.matmul
    pe.wait_ge(s.load, 16 * 9)
    pe.wait_ge(s.c, 1)
    for n in range(3):
        tr(m.ps[:, 0, n * NI:(n + 1) * NI], m.rows[:, n, :], m.ident[:NI, :NI])
    for n in range(2):
        for q in range(4):
            x = tr(m.ps[:, 1 + n, q * P:(q + 1) * P], m.cin[:, n, q].rearrange("p d s -> p (d s)"), m.ident[:])
    x.then_inc(s.pe, 1)
    pe.wait_ge(s.dve, 3)
    for i in range(NI):
        for n in range(2):
            x = tr(m.ps[:, i // 2, ((i % 2) * 2 + n) * P:((i % 2) * 2 + n + 1) * P],
                   m.Qt[:, n, i].rearrange("p r c -> p (r c)"), m.ident[:])
        if i % 2:
            x.then_inc(s.pe, 1)
    for n_g in range(NG):
        bank = n_g // 4
        i, e = 4 * (bank % 4) + n_g % 4, bank // 4
        if n_g % 4 == 0:
            pe.wait_ge(s.evac, bank + 1)
        for n in range(2):
            x = mm(m.ps[:GC, bank, (n_g % 4) * P:(n_g % 4 + 1) * P], m.bb[NS * e:NS * (e + 1), n, i, :],
                   m.W[NS * e:NS * (e + 1), n, i, :L, :].rearrange("p t c -> p (t c)"), start=(n == 0), stop=(n == 1))
        if n_g % 4 == 3:
            x.then_inc(s.pe, 1)
    pe.wait_ge(s.u_load, 64)
    for g in range(NG):
        if g % 4 == 0:
            pe.wait_ge(s.evac, g // 4 + 9)
        x = tr(m.ps[:, g // 4, (g % 4) * P:(g % 4 + 1) * P], m.ut[:, P * g:P * (g + 1)], m.ident[:])
        if g % 4 == 3:
            x.then_inc(s.u_T, 1)
    pe.wait_ge(s.a, 7)
    for g in range(NG):
        tr(m.ps[:GC, 0, g * TS:(g + 1) * TS], m.us[:, GC * g:GC * (g + 1)], m.ident[:TS, :TS])
    for n in range(2):
        for i in range(NI):
            x = tr(m.ps[:, 1, (n * NI + i) * TS:(n * NI + i + 1) * TS], m.xi[:, n, i * P:(i + 1) * P], m.ident[:TS, :TS])
    x.then_inc(s.u_T, 1)
    pe.wait_ge(s.a, 15)
    for h in range(2):
        for n in range(2):
            for il in range(HI):
                i = h * HI + il
                for e in range(2):
                    x = mm(m.ps[NS * e:NS * (e + 1), 4 * h + 2 * n + il // 4, (il % 4) * P:(il % 4 + 1) * P],
                           m.QL[:, i, n, NS * e:NS * (e + 1)], m.U[:, 2 * i + e, :], start=True, stop=True)
        x.then_inc(s.pe, 1)
    pe.wait_ge(s.dve, 5)
    for n in range(2):
        for i in range(NI):
            for e in range(2):
                x = mm(m.ps[NS * e:NS * (e + 1), 0, (n * NI + i) * TS:(n * NI + i + 1) * TS],
                       m.QL[:GC, i, n, NS * e:NS * (e + 1)], m.uT[:, 2 * i + e, :], start=True, stop=True)
    x.then_inc(s.pe, 1)
    pe.wait_ge(s.dve, 7)
    for n_g in range(NG):
        bank = n_g // 4
        i, e = 4 * (bank % 4) + n_g % 4, bank // 4
        g = 2 * i + e
        out = m.ps[:, bank, (n_g % 4) * P:(n_g % 4 + 1) * P]
        mm(out, m.U[:, g, :], m.M[:, g, :], start=True, stop=False)
        for n in range(2):
            x = mm(out, m.Z[NS * e:NS * (e + 1), n, i, :NCK],
                   m.W[NS * e:NS * (e + 1), n, i, 1:, :].rearrange("p t c -> p (t c)"), start=False, stop=(n == 1))
        if n_g % 4 == 3:
            x.then_inc(s.u_T, 1)
    pe.wait_ge(s.a, 17)
    for g in range(NG):
        i, e = divmod(g, 2)
        for n in range(2):
            x = mm(m.ps[:TS, e, i * GC:(i + 1) * GC], m.xs[NS * e:NS * (e + 1), n, i, :],
                   m.W[NS * e:NS * (e + 1), n, i, 0, :], start=(n == 0), stop=(n == 1))
    x.then_inc(s.u_T, 1)
    pe.wait_ge(s.late, 1)
    for h in range(8):
        j, half = h // 2, h % 2
        for t in range(4):
            x = tr(m.ps[:, h, t * P:(t + 1) * P], m.y[:, 4 * half + t, j * P:(j + 1) * P], m.ident[:])
        x.then_inc(s.u_T, 1)
    pe.wait_ge(s.a, 30)
    pe.wait_ge(s.wg, 16 * 5)
    for j in range(4):
        tr(m.ps[:, 0, j * TS:(j + 1) * TS], m.ys[:, j * P:(j + 1) * P], m.ident[:TS, :TS])
    tr(m.ps[:, 1, :4], m.bgr[:], m.ident[:4, :4])
    for n in range(2):
        x = tr(m.ps[:NI, 2, n * P:(n + 1) * P], m.Z[:, n, :, NCK], m.ident[:])
    x.then_inc(s.u_T, 1)
    for n in range(8):
        if n < 4:
            pe.wait_ge(s.a, 30 + n)
        else:
            pe.wait_ge(s.a, 36 + n - 4)
        for q in range(4):
            i = (n % 4) * 4 + q
            x = tr(m.ps[:TS, 3 + n % 4, q * P:(q + 1) * P], m.xs[:, n // 4, i, :], m.ident[:])
        x.then_inc(s.u_T, 1)
    pe.wait_ge(s.a, 41)
    for n in range(4 * NCH):
        j, c = divmod(n, NCH)
        if n >= 4:
            pe.wait_ge(s.sig, n - 3)
        for k in range(4):
            x = mm(m.ps[:, n % 4, :CH], m.wgl[:, k, j * P:(j + 1) * P], m.yT[:, k, cols(c)],
                   start=(k == 0), stop=(k == 3))
        x.then_inc(s.glu, 1)


def ssm_dve(nc, dve, m, s):
    V = nc.vector
    cnt = [0]

    def done(*ins):
        for x in ins:
            x.then_inc(s.c, 1)
        cnt[0] += len(ins)
        dve.wait_ge(s.c, cnt[0])

    def tt(o, a, b, op):
        return V.tensor_tensor(o, a, b, op)

    def cmul(o, a, b, t1, t2=None, conj_b=False, negate_im=False):
        sr, si = (ALU.add, ALU.subtract) if conj_b else (ALU.subtract, ALU.add)
        if t2 is None:
            done(tt(o[0], a[0], b[0], ALU.mult), tt(t1, a[1], b[1], ALU.mult))
            done(tt(o[0], o[0], t1, sr))
            done(tt(o[1], a[1], b[0], ALU.mult), tt(t1, a[0], b[1], ALU.mult))
            done(tt(o[1], o[1], t1, si))
        else:
            done(tt(o[0], a[0], b[0], ALU.mult), tt(t1, a[1], b[1], ALU.mult),
                 tt(o[1], a[1], b[0], ALU.mult), tt(t2, a[0], b[1], ALU.mult))
            done(tt(o[0], o[0], t1, sr), tt(o[1], o[1], t2, si))

    k = lambda n: m.sc[:, SLOT[n], :]
    dve.wait_ge(s.load, 16 * 9)
    done(V.tensor_copy(m.rows[:, 2, :].rearrange("p (e s) -> p e s", e=2),
                       m.ldt[:, :, None].to_broadcast([NI, 2, NS])))
    dve.wait_ge(s.pe, 1)
    pr = lambda n: m.ps[:, 0, n * NI:(n + 1) * NI]
    done(V.tensor_copy(k("ar"), pr(0)), V.tensor_copy(k("ai"), pr(1)))
    V.tensor_copy(k("dt"), pr(2)).then_inc(s.dve, 1)
    for n in range(2):
        for e in range(2):
            r = slice(NS * e, NS * (e + 1))
            done(V.tensor_copy(m.cs[r, n].rearrange("p (q g) c -> p q g c", q=4),
                               m.ps[r, 1 + n, :].rearrange("p (q g e c) -> p q g e c", q=4, g=4, e=2)[:, :, :, e, :]))
    dve.wait_ge(s.a, 1)
    done(tt(k("dtr"), k("dt"), k("ar"), ALU.mult), tt(k("dti"), k("dt"), k("ai"), ALU.mult))
    done(V.tensor_scalar(k("n"), k("dti"), float(1 / (2 * np.pi)), MAGIC, ALU.mult, ALU.add))
    done(V.tensor_scalar(k("n"), k("n"), -MAGIC, None, ALU.add))
    src = k("dti")
    for part in TWO_PI:
        done(V.scalar_tensor_tensor(out=k("r"), in0=k("n"), scalar=-part, in1=src, op0=ALU.mult, op1=ALU.add))
        src = k("r")
    V.tensor_scalar(k("r"), k("r"), 3.1415925, -3.1415925, ALU.min, ALU.max).then_inc(s.dve, 1)
    dve.wait_ge(s.a, 5)
    done(tt(k("t1"), k("sh"), k("sh"), ALU.mult))
    done(V.tensor_scalar(k("er"), k("t1"), -2.0, 1.0, ALU.mult, ALU.add), V.tensor_copy(k("ei"), k("sin")))
    done(tt(k("abr"), k("mag"), k("er"), ALU.mult), tt(k("abi"), k("mag"), k("ei"), ALU.mult))
    cmul((k("u1"), k("u2")), (k("er"), k("ei")), (k("er"), k("ei")), k("t1"), k("t2"))
    cmul((k("e8r"), k("e8i")), (k("u1"), k("u2")), (k("u1"), k("u2")), k("t1"), k("t2"))
    cmul((k("u1"), k("u2")), (k("e8r"), k("e8i")), (k("e8r"), k("e8i")), k("t1"), k("t2"))
    done(V.tensor_copy(k("e8r"), k("u1")), V.tensor_copy(k("e8i"), k("u2")))
    done(V.memset(m.pw[:, 0, :, 0], 1.0), V.memset(m.pw[:, 1, :, 0], 0.0),
         V.tensor_copy(m.pw[:, 0, :, 1], k("abr")), V.tensor_copy(m.pw[:, 1, :, 1], k("abi")))
    n = 1
    while n < L:
        pw = lambda a, b: [m.pw[:, q, :, a:b] for q in range(2)]
        top = [x.to_broadcast([P, NI, n]) for x in pw(n, n + 1)]
        t = [m.tb[:, q * NI * n:(q + 1) * NI * n].rearrange("p (i n) -> p i n", n=n) for q in range(2)]
        cmul(pw(n + 1, 2 * n + 1), pw(1, n + 1), top, *t)
        n *= 2
    done(tt(k("t1"), k("ar"), k("ar"), ALU.mult), tt(k("t2"), k("ai"), k("ai"), ALU.mult),
         V.tensor_scalar(k("nr"), k("abr"), -1.0, None, ALU.add))
    done(tt(k("den"), k("t1"), k("t2"), ALU.add))
    cmul((k("fr"), k("fi")), (k("nr"), k("abi")), (k("ar"), k("ai")), k("t1"), k("t2"), conj_b=True)
    done(V.reciprocal(k("u1"), k("den")))
    done(tt(k("fr"), k("fr"), k("u1"), ALU.mult), tt(k("fi"), k("fi"), k("u1"), ALU.mult))
    f = [k(q)[:, :, None].to_broadcast([P, NI, GC]) for q in ("fr", "fi")]
    t = m.tb[:, :NI * GC].rearrange("p (i c) -> p i c", i=NI)
    cmul((m.bb[:, 0], m.bb[:, 1]), (m.bin[:, 0], m.bin[:, 1]), f, t)
    sh = [P, NI, L, GC]
    t = m.tb[:, :NI * L * GC].rearrange("p (i r c) -> p i r c", i=NI, r=L)
    bbx = [m.bb[:, q, :, None, :].to_broadcast(sh) for q in range(2)]
    pwx = [m.pw[:, q, :, :L, None].to_broadcast(sh) for q in range(2)]
    cmul((m.Qt[:, 0], m.Qt[:, 1]), bbx, pwx, t)
    sh = [P, NI, L + 1, GC]
    t = m.tb[:].rearrange("p (i r c) -> p i r c", i=NI, r=L + 1)
    cx = [m.cs[:, q, :, None, :].to_broadcast(sh) for q in range(2)]
    pwx = [m.pw[:, q, :, :, None].to_broadcast(sh) for q in range(2)]
    cmul((m.W[:, 0], m.W[:, 1]), cx, pwx, t)
    V.tensor_scalar(m.W[:, 1].rearrange("p i t c -> p (i t c)"), m.W[:, 1].rearrange("p i t c -> p (i t c)"),
                    -1.0, None, ALU.mult).then_inc(s.dve, 1)
    dve.wait_ge(s.pe, 17)
    dve.wait_ge(s.u_T, 9)
    V.memset(m.Z[:, :, :, 0], 0.0).then_inc(s.dve, 1)
    dve.wait_ge(s.dve, 4)
    for h in range(2):
        il = slice(h * HI, (h + 1) * HI)
        E = lambda a, b: [m.E[:, q, :, a:b] for q in range(2)]
        done(V.memset(m.E[:, 0, :, 0], 1.0), V.memset(m.E[:, 1, :, 0], 0.0),
             V.tensor_copy(m.E[:, 0, :, 1], k("e8r")[:, il]), V.tensor_copy(m.E[:, 1, :, 1], k("e8i")[:, il]))
        n = 1
        while n < NCK:
            top = [x.to_broadcast([P, HI, n]) for x in E(n, n + 1)]
            t = m.tz[:, :HI * n].rearrange("p (i n) -> p i n", n=n)
            cmul(E(n + 1, 2 * n + 1), E(1, n + 1), top, t)
            n *= 2
        dve.wait_ge(s.pe, 18 + h)
        S = [m.ps[:, 4 * h + 2 * q:4 * h + 2 * q + 2, :].rearrange("p a (i n) -> p (a i) n", n=NCK) for q in range(2)]
        t = m.tz[:, :HI * NCK].rearrange("p (i n) -> p i n", n=NCK)
        cmul([m.Sm[:, q] for q in range(2)], S, E(1, NCK + 1), t, conj_b=True)
        done(*[V.tensor_tensor_scan(out=m.Z[:, q, h * HI + j, 1:], data0=k("r8")[:, h * HI + j:h * HI + j + 1]
                                    .to_broadcast([P, NCK]), data1=m.Sm[:, q, j, :], initial=0.0,
                                    op0=ALU.mult, op1=ALU.add) for j in range(HI) for q in range(2)])
        Zh = [m.Z[:, q, il, :] for q in range(2)]
        Ef = E(0, NCK + 1)
        t = m.tz[:].rearrange("p (i n) -> p i n", n=NCK + 1)
        t2 = m.Sm[:].rearrange("p q i n -> p (q i n)")[:, :HI * (NCK + 1)].rearrange("p (i n) -> p i n", n=NCK + 1)
        done(tt(t, Zh[1], Ef[1], ALU.mult), tt(t2, Zh[0], Ef[1], ALU.mult))
        done(tt(Zh[0], Zh[0], Ef[0], ALU.mult), tt(Zh[1], Zh[1], Ef[0], ALU.mult))
        done(tt(Zh[0], Zh[0], t, ALU.subtract), tt(Zh[1], Zh[1], t2, ALU.add))
        dve.sem_inc(s.dve, 1)
    dve.wait_ge(s.pe, 20)
    a = [k(q)[:, :, None].to_broadcast([P, NI, TS]) for q in ("abr", "abi")]
    t = m.tz[:, :NI * TS].rearrange("p (i n) -> p i n", n=TS)
    cmul([m.xs[:, q] for q in range(2)], [m.x0[:, q] for q in range(2)], a, t)
    bx = m.ps[:, 0, :2 * NI * TS].rearrange("p (q i n) -> p q i n", q=2, n=TS)
    done(tt(m.xs[:], m.xs[:], bx, ALU.add))
    dve.sem_inc(s.dve, 1)
    dve.wait_ge(s.wg, 48)
    byg = lambda x: x.rearrange("p (g c) -> p g c", g=NG)
    done(tt(m.u2, m.u2, byg(m.db[:])[:, :, None, :].to_broadcast([P, NG, L, GC]), ALU.mult),
         tt(m.us2[:], m.us2[:], m.db[:TS, :], ALU.mult))
    dve.wait_ge(s.a, 24)
    done(*[tt(byg(m.y[:, t, :]), byg(m.y[:, t, :]), m.u2[:, :, L - 1 - t, :], ALU.add) for t in range(L)],
         tt(m.ys[:], m.ys[:], m.us2[:], ALU.add))
    dve.sem_inc(s.dve, 1)
    for n in range(4 * NCH):
        j, c = divmod(n, NCH)
        dve.wait_ge(s.sig, n + 1)
        tt(m.gl[:, n % 2, :], m.gl[:, n % 2, :], m.yT[:, j, cols(c)], ALU.mult).then_inc(s.gate, 1)
        dve.wait_ge(s.hi, n + 1)
        done(tt(m.xn[:, 4 + j, 1, cols(c)], m.gl[:, n % 2, :], m.xn[:, 4 + j, 0, cols(c)].bitcast(F32), ALU.subtract))
OUT_SEMS = ("raw0", "raw1", "gates0", "gates1", "hi", "lo", "a", "b", "prod", "sum", "mhi", "mlo",
            "draw0", "draw1", "dhi", "dlo", "down", "acc")
ORDER = (0, 1, 2, 3, "d0", 4, 5, "d1", 6, 7, "d2", "d3")


def out_memory(sb, m):
    m.wh = sb("branch_weights_split", [P, 2, 2, KD * P], F32R)
    m.wr = sb("branch_weights_raw", [P, 2, KD * P])
    m.hh = sb("merged_split", [P, 4, 2, T], F32R)
    m.dh = sb("out_weights_split", [P, 2, 2, D], F32R)
    m.dr = sb("out_weights_raw", [P, 2, D])
    m.gt = sb("gates", [P, 2, 2, CH * NCH])
    m.mg = sb("merged", [P, 2, 2, CH])


def out_sp(nc, sp, m, s, i, o):
    for t in ORDER:
        if isinstance(t, int):
            e = t % 2
            if t >= 2:
                sp.wait_ge(s.lo, t - 1)
            for n, w in enumerate((i.w_pa, i.w_pb)):
                sp.dma_start(m.wr[:, e, n * 4 * P:(n + 1) * 4 * P].rearrange("p (k n) -> p k n", k=4),
                             w.rearrange("(k p) n -> p k n", p=P)[:, :, t * P:(t + 1) * P]).then_inc((s.raw0, s.raw1)[e], 16)
            if t >= 2:
                sp.wait_ge(s.sum, NCH * (t - 1))
            for n in range(2):
                sp.dma_start(m.gt[:, e, n, :], o.gates[(n * KD + t) * P:(n * KD + t + 1) * P, :]).then_inc((s.gates0, s.gates1)[e], 16)
        else:
            p = int(t[1])
            for e in range(2):
                if p:
                    sp.wait_ge(s.dlo, 2 * p + e - 1)
                sp.dma_start(m.dr[:, e, :], i.w_out[(2 * p + e) * P:(2 * p + e + 1) * P, :]).then_inc((s.draw0, s.draw1)[e], 16)


def out_act(nc, act, m, s):
    def split(t):
        e = t % 2
        act.wait_ge((s.raw0, s.raw1)[e], 32 * (t // 2 + 1))
        if t >= 2:
            act.wait_ge(s.b, NCH * (t - 1))
        nc.scalar.activation(m.wh[:, e, 0, :], m.wr[:, e, :], ACT.Copy).then_inc(s.hi, 1)

    split(0)
    for t in ORDER:
        if isinstance(t, int):
            if t + 1 < KD:
                split(t + 1)
            for c in range(NCH):
                n = NCH * t + c
                act.wait_ge(s.sum, n + 1)
                nc.scalar.activation(m.hh[:, t % 4, 0, cols(c)], m.mg[:, n % 2, 0, :], ACT.Copy).then_inc(s.mhi, 1)
        else:
            p = int(t[1])
            for e in range(2):
                act.wait_ge((s.draw0, s.draw1)[e], 16 * (p + 1))
                if p:
                    act.wait_ge(s.down, NCH * KD * p)
                nc.scalar.activation(m.dh[:, e, 0, :], m.dr[:, e, :], ACT.Copy).then_inc(s.dhi, 1)


def out_pool(nc, pool, m, s):
    def split(t):
        pool.wait_ge(s.hi, t + 1)
        nc.gpsimd.tensor_tensor(m.wh[:, t % 2, 1, :], m.wr[:, t % 2, :], m.wh[:, t % 2, 0, :].bitcast(F32),
                                ALU.subtract).then_inc(s.lo, 1)

    split(0)
    for t in ORDER:
        if isinstance(t, int):
            if t + 1 < KD:
                split(t + 1)
            for c in range(NCH):
                n = NCH * t + c
                pool.wait_ge(s.mhi, n + 1)
                nc.gpsimd.tensor_tensor(m.hh[:, t % 4, 1, cols(c)], m.mg[:, n % 2, 0, :],
                                        m.hh[:, t % 4, 0, cols(c)].bitcast(F32), ALU.subtract).then_inc(s.mlo, 1)
        else:
            p = int(t[1])
            for e in range(2):
                pool.wait_ge(s.dhi, 2 * p + e + 1)
                nc.gpsimd.tensor_tensor(m.dh[:, e, 1, :], m.dr[:, e, :], m.dh[:, e, 0, :].bitcast(F32),
                                        ALU.subtract).then_inc(s.dlo, 1)


def out_pe(nc, pe, m, s):
    for t in ORDER:
        if isinstance(t, int):
            pe.wait_ge(s.lo, t + 1)
            for c in range(NCH):
                if t:
                    pe.wait_ge(s.prod, NCH * (t - 1) + c + 1)
                for half, done in ((0, s.a), (1, s.b)):
                    for k in range(4 * half, 4 * half + 4):
                        for n, (a, b) in enumerate(PASSES):
                            mm = nc.tensor.matmul(m.ps[:, NCH * half + c, :CH], m.wh[:, t % 2, a, k * P:(k + 1) * P],
                                                  m.xn[:, k, b, cols(c)], start=(k % 4 == 0 and n == 0),
                                                  stop=(k % 4 == 3 and n == 2))
                    mm.then_inc(done, 1)
        else:
            p = int(t[1])
            pe.wait_ge(s.mlo, NCH * (2 * p + 2))
            pe.wait_ge(s.dlo, 2 * p + 2)
            for n in range(NCH * KD):
                o, c = divmod(n, NCH)
                if p or n >= 2:
                    pe.wait_ge(s.acc, NCH * KD * p + n - 1)
                for e in range(2):
                    for q, (a, b) in enumerate(PASSES):
                        mm = nc.tensor.matmul(m.ps[:, 6 + n % 2, :CH], m.dh[:, e, a, o * P:(o + 1) * P],
                                              m.hh[:, (2 * p + e) % 4, b, cols(c)], start=(e == 0 and q == 0),
                                              stop=(e == 1 and q == 2))
                mm.then_inc(s.down, 1)


def out_dve(nc, dve, m, s):
    for t in ORDER:
        if isinstance(t, int):
            dve.wait_ge((s.gates0, s.gates1)[t % 2], 32 * (t // 2 + 1))
            for c in range(NCH):
                n = NCH * t + c
                dve.wait_ge(s.b, n + 1)
                if n >= 2:
                    dve.wait_ge(s.mlo, n - 1)
                mg = [m.mg[:, n % 2, h, :] for h in range(2)]
                nc.vector.tensor_tensor(mg[0], m.gt[:, t % 2, 0, cols(c)], m.ps[:, c, :CH], ALU.mult)
                nc.vector.tensor_tensor(mg[1], m.gt[:, t % 2, 1, cols(c)], m.ps[:, NCH + c, :CH],
                                        ALU.mult).then_inc(s.prod, 1)
                dve.wait_ge(s.prod, n + 1)
                nc.vector.tensor_tensor(mg[0], mg[0], mg[1], ALU.add).then_inc(s.sum, 1)
        else:
            p = int(t[1])
            for n in range(NCH * KD):
                o, c = divmod(n, NCH)
                dve.wait_ge(s.down, NCH * KD * p + n + 1)
                xs = m.x[:, o, cols(c)]
                nc.vector.tensor_tensor(xs, xs, m.ps[:, 6 + n % 2, :CH], ALU.add).then_inc(s.acc, 1)


IO_SEMS = ("x_in0", "x_in1", "turned", "kept", "gain_in", "gain_T", "gains", "const", "sq", "sum", "var", "std",
           "rs", "y", "back", "staged", "y_out0", "y_out1", "phase", "leave", "x_away", "x_back",
           "ki_in", "table")


def in_sp(nc, sp, m, s, i):
    for n, g in enumerate(i.gains):
        sp.dma_start(m.grow[KD * n:KD * (n + 1), :], g.rearrange("(k p) -> k p", p=P)).then_inc(s.gain_in, 16)
    for b in range(NB + 1):
        rows = P if b < NB else TS
        if b >= 2:
            sp.wait_ge(s.turned, 2 * (b - 1))
        src = i.x_prompt[b * P:(b + 1) * P, :] if b < NB else i.x_sample
        sp.dma_start(m.xin[:rows, b % 2, :], src).then_inc((s.x_in0, s.x_in1)[b % 2], 16)


def in_pe(nc, pe, m, s):
    pe.wait_ge(s.const, 5)
    pe.wait_ge(s.gain_in, 16 * 4)
    nc.tensor.transpose(m.ps[:, 7, :4 * KD], m.grow[:], m.ident[:4 * KD, :4 * KD]).then_inc(s.gain_T, 1)
    for b in range(NB + 1):
        rows = P if b < NB else TS
        pe.wait_ge((s.x_in0, s.x_in1)[b % 2], 16 * (b // 2 + 1))
        for h in range(2):
            n = 2 * b + h
            if n >= 4:
                pe.wait_ge(s.kept, n - 3)
            for q in range(4):
                k = 4 * h + q
                mm = nc.tensor.transpose(m.ps[:, n % 4, q * P:q * P + rows], m.xin[:rows, b % 2, k * P:(k + 1) * P],
                                         m.ident[:rows, :rows])
            mm.then_inc(s.turned, 1)


def in_act(nc, act, m, s):
    act.wait_ge(s.gain_T, 1)
    nc.scalar.activation(m.gains[:], m.ps[:, 7, :4 * KD], ACT.Copy).then_inc(s.gains, 1)
    for b in range(NB + 1):
        rows = P if b < NB else TS
        for h in range(2):
            n = 2 * b + h
            act.wait_ge(s.turned, n + 1)
            nc.scalar.activation(m.x[:, 4 * h:4 * h + 4, b * P:b * P + rows],
                                 m.ps[:, n % 4, :].rearrange("p (q t) -> p q t", q=4)[:, :, :rows],
                                 ACT.Copy).then_inc(s.kept, 1)
    act.wait_ge(s.kept, 2 * NB + 2)


def fin_memory(sb, m):
    m.sg = sb("final_squares", [P, NCH, CH])
    m.rstd = sb("final_rstd", [P, 3, CH])
    m.yn = sb("final_normed", [P, KD, T])
    m.yo = sb("final_rows", [P, 2, D])


def fin_act(nc, act, m, s, o):
    for c in range(NCH):
        for k in range(KD):
            n = c * KD + k
            if n >= 3:
                act.wait_ge(s.sum, n - 2)
            nc.scalar.activation(m.sg[:, n % 3, :], m.x[:, k, cols(c)], ACT.Square).then_inc(s.sq, 1)
        act.wait_ge(s.var, c + 1)
        nc.scalar.activation(m.rstd[:, 1, :], m.rstd[:, 0, :], ACT.Sqrt).then_inc(s.std, 1)
    for b in range(NB + 1):
        rows = P if b < NB else TS
        if b >= 2:
            act.wait_ge((s.y_out0, s.y_out1)[b % 2], 16 * (b // 2))
        for h in range(2):
            act.wait_ge(s.back, 2 * b + h + 1)
            nc.scalar.activation(m.yo[:rows, b % 2, h * 512:(h + 1) * 512], m.ps[:rows, (2 * b + h) % 4, :],
                                 ACT.Copy).then_inc(s.staged, 1)


def fin_pe(nc, pe, m, s):
    for c in range(NCH):
        if c:
            pe.wait_ge(s.var, c)
        for k in range(KD):
            n = c * KD + k
            pe.wait_ge(s.sq, n + 1)
            nc.tensor.matmul(m.ps[:, 4, :CH], m.ones[:], m.sg[:, n % 3, :],
                             start=(k == 0), stop=(k == KD - 1)).then_inc(s.sum, 1)
    pe.wait_ge(s.y, NCH * KD)
    for b in range(NB + 1):
        rows = P if b < NB else TS
        for h in range(2):
            n = 2 * b + h
            if n >= 4:
                pe.wait_ge(s.staged, n - 3)
            for q in range(4):
                mm = nc.tensor.transpose(m.ps[:rows, n % 4, q * P:(q + 1) * P],
                                         m.yn[:, 4 * h + q, b * P:b * P + rows], m.ident[:])
            mm.then_inc(s.back, 1)


def fin_dve(nc, dve, m, s):
    for c in range(NCH):
        dve.wait_ge(s.sum, KD * (c + 1))
        nc.vector.tensor_scalar(m.rstd[:, 0, :], m.ps[:, 4, :CH], 1.0 / D, EPS, ALU.mult, ALU.add).then_inc(s.var, 1)
        dve.wait_ge(s.std, c + 1)
        nc.vector.reciprocal(m.rstd[:, 2, :], m.rstd[:, 1, :]).then_inc(s.rs, 1)
        dve.wait_ge(s.rs, c + 1)
        for k in range(KD):
            nc.vector.scalar_tensor_tensor(out=m.yn[:, k, cols(c)], in0=m.x[:, k, cols(c)],
                                           scalar=m.gains[:, 3 * KD + k:3 * KD + k + 1], in1=m.rstd[:, 2, :],
                                           op0=ALU.mult, op1=ALU.mult).then_inc(s.y, 1)


def fin_sp(nc, sp, m, s, i, o):
    for b in range(NB + 1):
        rows = P if b < NB else TS
        sp.wait_ge(s.staged, 2 * b + 2)
        dst = o.y_prompt[b * P:(b + 1) * P, :] if b < NB else o.y_sample
        sp.dma_start(dst, m.yo[:rows, b % 2, :]).then_inc((s.y_out0, s.y_out1)[b % 2], 16)
    sp.wait_ge(s.y_out0, 16 * 5)
    sp.wait_ge(s.y_out1, 16 * 4)


OUTS = (("y_prompt", (1, TP, D)), ("y_sample", (TS, 1, D)),
        ("k_prompt", (1, 1, TP, N_HEADS, HD)), ("v_prompt", (1, 1, TP, N_HEADS, HD)), ("kidx_prompt", (1, 1, TP, IDX)),
        ("ssm_re_prompt", (1, 1, NG, NS)), ("ssm_im_prompt", (1, 1, NG, NS)),
        ("k_sample", (1, TS, 1, N_HEADS, HD)), ("v_sample", (1, TS, 1, N_HEADS, HD)), ("kidx_sample", (1, TS, 1, IDX)),
        ("ssm_re_sample", (1, TS, NG, NS)), ("ssm_im_sample", (1, TS, NG, NS)))
INS = ("x_prompt", "x_sample", "cache_k", "cache_v", "cache_kidx", "state_ssm_re", "state_ssm_im", "page_table",
       "g_ffn1", "w1_gate", "w1_up", "w1_down", "g_mix", "w_in", "a_re", "a_im", "log_dt", "b_re", "b_im",
       "c_re", "c_im", "d_skip", "w_glu", "b_glu", "w_pa", "w_pb", "w_out", "g_ffn2", "w2_gate", "w2_up",
       "w2_down", "g_final")


def build_layer(nc, i, o):
    with ExitStack() as stack:
        def sem(name):
            return stack.enter_context(nc.semaphore(name))

        def sems(prefix, names):
            return record("Sems", {n: sem(f"{prefix}_{n}") for n in names})

        def scope(*makers):
            inner = ExitStack()
            for make in makers:
                make(lambda name, shape, dt=F32: inner.enter_context(nc.sbuf_tensor(name, shape, dt)))
            return inner

        def space():
            m = Space()
            m.x, m.xn, m.spare, m.ident, m.ones, m.gains, m.table, m.ps = (
                base.x, base.xn, base.spare, base.ident, base.ones, base.gains, base.table, base.ps)
            return m

        base = Space()

        def spare_memory(sb):
            sb("first_half", [P, KD * T])
            base.spare = sb("samples_attention", [P, KD * T])

        def persistent(sb):
            base.x = sb("x_T", [P, KD, T])
            scope(spare_memory).close()
            base.xn = sb("normed_split", [P, KD, 2, T], F32R)
            base.ident = sb("identity", [P, P])
            base.ones = sb("ones", [P, P])
            base.gains = sb("gains", [P, 4 * KD])
            base.table = sb("page_table", [1, TS * N_PAGES], I32)

        base.ps = stack.enter_context(nc.psum_tensor("ps", [P, 8, 512], F32))
        stack.enter_context(scope(persistent))

        m_in = space()

        def in_memory(sb):
            m_in.xin = sb("x_rows", [P, 2, D])
            m_in.grow = sb("gain_rows", [4 * KD, P])
        scope(in_memory).close()
        m_f1, m_f2, m_mix, m_out, m_fin = (space() for _ in range(5))
        scope(lambda sb: ffn_memory(sb, m_f1, "f1")).close()

        with scope(lambda sb: mix_memory(sb, m_mix), lambda sb: smp_memory(sb, m_mix)):
            def norm_memory(sb):
                m_mix.sg = sb("mix_squares", [P, NCH, CH])
                m_mix.hf = sb("mix_normed", [P, NCH, CH])
                m_mix.rstd = sb("mix_rstd", [P, 3, CH])
            scope(norm_memory).close()
            scope(lambda sb: proj_memory(sb, m_mix)).close()
            scope(lambda sb: att_memory(sb, m_mix)).close()
        smp_views(m_mix)
        m_ssm = space()
        with scope(lambda sb: ssm_memory_keep(sb, m_ssm)):
            with scope(lambda sb: ssm_memory_base(sb, m_ssm)):
                scope(lambda sb: ssm_memory_build(sb, m_ssm)).close()
                scope(lambda sb: ssm_memory_run(sb, m_ssm)).close()
            scope(lambda sb: ssm_memory_glu(sb, m_ssm)).close()
        scope(lambda sb: out_memory(sb, m_out)).close()
        scope(lambda sb: ffn_memory(sb, m_f2, "f2")).close()
        scope(lambda sb: fin_memory(sb, m_fin)).close()

        s_io = sems("io", IO_SEMS)
        s_ffn = ffn_sems(sem, "ffn")
        s_mix = sems("mix", MIX_SEMS)
        s_att = sems("att", ATT_SEMS)
        s_smp = sems("smp", SMP_SEMS)
        s_ssm = sems("ssm", SSM_SEMS)
        s_out = sems("out", OUT_SEMS)
        s_f1, s_nm, s_f2 = after_uses(s_ffn, 0, 0), after_uses(s_ffn, 1, 1), after_uses(s_ffn, 2, 1)

        def barrier(engine, n):
            engine.drain().then_inc(s_io.phase, 1)
            engine.wait_ge(s_io.phase, 5 * n)

        gain = lambda n: base.gains[:, n * KD:(n + 1) * KD]
        block = stack.enter_context(nc.Block())

        @block.sync
        def _(sp):
            in_sp(nc, sp, m_in, s_io, i)
            sp.dma_start(base.table[:], i.page_table.rearrange("(a b) p -> a (b p)", a=1)).then_inc(s_io.table, 16)
            sp.wait_ge(s_io.table, 16)
            barrier(sp, 1)
            ffn_sp(nc, sp, m_f1, s_f1, i.w1_gate, i.w1_up, i.w1_down, lambda e: None)
            barrier(sp, 2)
            barrier(sp, 3)
            sp.wait_ge(s_nm.lo, s_nm.was.lo + NCH * KD)
            proj_sp(nc, sp, m_mix, s_mix, i.w_in, o)
            sp.dma_start(o.x_away, base.x[:].rearrange("p k t -> p (k t)")).then_inc(s_io.x_away, 16)
            for b in range(TS):
                smp_load(sp, m_mix, i, b, m_mix.kidx[:, b], i.cache_kidx, s_io.ki_in)
            sp.wait_ge(s_io.x_away, 16)
            barrier(sp, 4)
            sp.dma_start(m_mix.v[:], o.token_major["v"][0]).then_inc(s_att.v_in, 16)
            smp_sp(nc, sp, m_mix, s_smp, i, o)
            barrier(sp, 5)
            ssm_sp(nc, sp, m_ssm, s_ssm, i, o)
            barrier(sp, 6)
            sp.dma_start(base.x[:].rearrange("p k t -> p (k t)"), o.x_away).then_inc(s_io.x_back, 16)
            out_sp(nc, sp, m_out, s_out, i, o)
            barrier(sp, 7)
            ffn_sp(nc, sp, m_f2, s_f2, i.w2_gate, i.w2_up, i.w2_down, lambda e: None)
            barrier(sp, 8)
            fin_sp(nc, sp, m_fin, s_io, i, o)

        @block.scalar
        def _(act):
            in_act(nc, act, m_in, s_io)
            barrier(act, 1)
            norm_act(nc, act, m_f1, s_f1)
            ffn_act(nc, act, m_f1, s_f1)
            barrier(act, 2)
            barrier(act, 3)
            norm_act(nc, act, m_mix, s_nm)
            act.wait_ge(s_nm.lo, s_nm.was.lo + NCH * KD)
            proj_act(nc, act, m_mix, s_mix, o)
            barrier(act, 4)
            att_act(nc, act, m_mix, s_att, smp_act(nc, act, m_mix, s_smp))
            barrier(act, 5)
            ssm_act(nc, act, m_ssm, s_ssm)
            barrier(act, 6)
            out_act(nc, act, m_out, s_out)
            barrier(act, 7)
            norm_act(nc, act, m_f2, s_f2)
            ffn_act(nc, act, m_f2, s_f2)
            barrier(act, 8)
            fin_act(nc, act, m_fin, s_io, o)

        @block.vector
        def _(dve):
            nc.vector.memset(base.ones[:], 1.0).then_inc(s_io.const, 1)
            barrier(dve, 1)
            norm_dve(nc, dve, m_f1, s_f1, 6, gain(0))
            ffn_dve(nc, dve, m_f1, s_f1)
            barrier(dve, 2)
            barrier(dve, 3)
            norm_dve(nc, dve, m_mix, s_nm, 6, gain(1))
            select_dve(nc, dve, m_mix, s_mix)
            barrier(dve, 4)
            att_dve(nc, dve, m_mix, s_att, smp_dve(nc, dve, m_mix, s_smp))
            barrier(dve, 5)
            ssm_dve(nc, dve, m_ssm, s_ssm)
            barrier(dve, 6)
            dve.wait_ge(s_io.x_back, 16)
            out_dve(nc, dve, m_out, s_out)
            barrier(dve, 7)
            norm_dve(nc, dve, m_f2, s_f2, 6, gain(2))
            ffn_dve(nc, dve, m_f2, s_f2)
            barrier(dve, 8)
            fin_dve(nc, dve, m_fin, s_io)

        @block.gpsimd
        def _(pool):
            nc.gpsimd.memset(base.ident[:], 0.0).then_inc(s_io.const, 1)
            pool.wait_ge(s_io.const, 2)
            nc.gpsimd.affine_select(out=base.ident[:], in_=base.ident[:], compare_op=ALU.not_equal, fill=1.0,
                                    base=0, pattern=[[-1, P]], channel_multiplier=1).then_inc(s_io.const, 3)
            barrier(pool, 1)
            norm_pool(nc, pool, m_f1, s_f1)
            ffn_pool(nc, pool, m_f1, s_f1)
            barrier(pool, 2)
            nc.gpsimd.memset(m_mix.bias01[:], 0.0).then_inc(s_io.leave, 1)
            pool.wait_ge(s_io.leave, 1)
            nc.gpsimd.affine_select(out=m_mix.bias01[:, P:], in_=m_mix.bias01[:, P:], compare_op=ALU.is_ge, fill=NEG,
                                    base=0, pattern=[[-1, P]], channel_multiplier=1)
            barrier(pool, 3)
            norm_pool(nc, pool, m_mix, s_nm)
            proj_pool(nc, pool, m_mix, s_mix)
            barrier(pool, 4)
            pool.wait_ge(s_io.ki_in, 16 * TS * N_PAGES)
            smp_pool(nc, pool, m_mix, s_smp)
            barrier(pool, 5)
            ssm_pool(nc, pool, m_ssm, s_ssm)
            barrier(pool, 6)
            out_pool(nc, pool, m_out, s_out)
            barrier(pool, 7)
            norm_pool(nc, pool, m_f2, s_f2)
            ffn_pool(nc, pool, m_f2, s_f2)
            barrier(pool, 8)

        @block.tensor
        def _(pe):
            in_pe(nc, pe, m_in, s_io)
            barrier(pe, 1)
            norm_pe(nc, pe, m_f1, s_f1, 6)
            ffn_pe(nc, pe, m_f1, s_f1)
            barrier(pe, 2)
            barrier(pe, 3)
            norm_pe(nc, pe, m_mix, s_nm, 6)
            pe.wait_ge(s_nm.lo, s_nm.was.lo + NCH * KD)
            proj_pe(nc, pe, m_mix, s_mix)
            barrier(pe, 4)
            att_pe(nc, pe, m_mix, s_att, smp_pe(nc, pe, m_mix, s_smp))
            barrier(pe, 5)
            ssm_pe(nc, pe, m_ssm, s_ssm)
            barrier(pe, 6)
            out_pe(nc, pe, m_out, s_out)
            barrier(pe, 7)
            norm_pe(nc, pe, m_f2, s_f2, 6)
            ffn_pe(nc, pe, m_f2, s_f2)
            barrier(pe, 8)
            fin_pe(nc, pe, m_fin, s_io)


def views(nc, ins, outs):
    i = {}
    i["x_prompt"] = ins["x_prompt"].rearrange("b t d -> (b t) d")
    i["x_sample"] = ins["x_sample"].rearrange("b t d -> (b t) d")
    i["cache_k"] = ins["cache_k"].rearrange("l n p h d -> (l n) p (h d)")
    i["cache_v"] = ins["cache_v"].rearrange("l n p h d -> (l n) p (h d)")
    i["cache_kidx"] = ins["cache_kidx"].rearrange("l n p d -> (l n) p d")
    i["state_re"] = ins["state_ssm_re"].rearrange("l b g s -> (l b) (g s)")
    i["state_im"] = ins["state_ssm_im"].rearrange("l b g s -> (l b) (g s)")
    i["page_table"] = ins["page_table"]
    for name in ("w1_gate", "w1_up", "w1_down", "w_in", "w_glu", "w_pa", "w_pb", "w_out", "w2_gate", "w2_up",
                 "w2_down", "a_re", "a_im"):
        i[name] = ins[name].rearrange("l a b -> (l a) b")
    for name in ("b_re", "b_im", "c_re", "c_im"):
        i[name] = ins[name].rearrange("l a b c -> (l a) b c")
    for name in ("log_dt", "d_skip", "b_glu"):
        i[name] = ins[name].rearrange("l a -> (l a)")
    i["gains"] = [ins[n].rearrange("l a -> (l a)") for n in ("g_ffn1", "g_mix", "g_ffn2")] + [ins["g_final"]]

    def scratch(name, shape):
        return nc.dram_tensor(name, shape, F32).ap()

    o = {}
    o["y_prompt"] = outs["y_prompt"].rearrange("b t d -> (b t) d")
    o["y_sample"] = outs["y_sample"].rearrange("b t d -> (b t) d")
    k_p, v_p = (outs[n].rearrange("l b (n p) h d -> p (l b n) (h d)", p=P) for n in ("k_prompt", "v_prompt"))
    ki_p = outs["kidx_prompt"].rearrange("l b (n p) d -> p (l b n) d", p=P)
    o["k_s"], o["v_s"] = (outs[n].rearrange("l b t h d -> (l b t) (h d)") for n in ("k_sample", "v_sample"))
    o["ki_s"] = outs["kidx_sample"].rearrange("l b t d -> (l b t) d")
    o["ssm_re_p"], o["ssm_im_p"] = (outs[n].rearrange("l b (i e) s -> (l b i) (e s)", e=2)
                              for n in ("ssm_re_prompt", "ssm_im_prompt"))
    o["ssm_re_s"], o["ssm_im_s"] = (outs[n].rearrange("l b g s -> (l b) (g s)")
                              for n in ("ssm_re_sample", "ssm_im_sample"))
    o["x_away"] = scratch("x_meanwhile", (P, KD * T))
    o["q_s"] = scratch("q_sample_rows", (TS, D_ATTN))
    o["q_p"] = scratch("q_rows", (P, NB, D_ATTN))
    o["qi_s"] = scratch("q_index_sample_rows", (TS, IDX_HEADS * IDX))
    o["wi_s"] = scratch("index_weight_sample_rows", (TS, IDX_HEADS))
    o["ln_s"] = scratch("new_key_logits", (TS, N_HEADS))
    o["u_p"] = scratch("u_by_chunk_rows", (P, L * SSM_W))
    o["u_s"] = scratch("u_sample_rows", (TS, SSM_W))
    o["gates"] = scratch("gates_T", (2 * D, T))
    o["token_major"] = {"k": (k_p, o["k_s"]), "v": (v_p, o["v_s"]), "ki": (ki_p, o["ki_s"]), "q": (o["q_p"], o["q_s"]),
                     "u": (o["u_p"], o["u_s"])}
    return record("Ins", i), record("Outs", o)


def kernel(**inputs):
    import concourse.bacc as bacc
    from concourse.bass_utils import run_bass_kernel_spmd as run

    nc = bacc.Bacc("TRN2", target_bir_lowering=False, num_devices=1, dynamic_dma_scratch_size=1024)
    arrays, ins, outs = {}, {}, {}
    for name in INS:
        a = np.ascontiguousarray(inputs[name])
        arrays[f"in_{name}"] = a
        ins[name] = nc.dram_tensor(f"in_{name}", a.shape, mybir.dt.from_np(a.dtype), kind="ExternalInput").ap()
    for name, shape in OUTS:
        outs[name] = nc.dram_tensor(f"out_{name}", shape, F32, kind="ExternalOutput").ap()
    build_layer(nc, *views(nc, ins, outs))
    r = run(nc, [arrays], core_ids=[0])
    return tuple(r.results[0][f"out_{name}"] for name, _ in OUTS)
```

```python
from collections import namedtuple
from contextlib import ExitStack

import numpy as np

import concourse.bass as bass
from concourse import mybir

F32 = mybir.dt.float32
F32R = mybir.dt.float32r
I32 = mybir.dt.int32
U32 = mybir.dt.uint32
ALU = mybir.AluOpType
ACT = mybir.ActivationFunctionType
AX = mybir.AxisListType

P = 128
D = 1024
KD = D // P
TP, TS = 1024, 8
T = TP + TS
NCH = 3
CH = T // NCH
D_FF = 2816
NF = D_FF // P
NPAIR = NF // 2
EPS = 1e-6
PASSES = ((0, 0), (0, 1), (1, 0))


class Space:
    pass


def record(name, fields):
    return namedtuple(name, list(fields))(**fields)


def cols(c):
    return slice(c * CH, (c + 1) * CH)



def norm_act(nc, act, m, s, first_weights):
    def squares(c):
        for k in range(KD):
            n = c * KD + k
            if n >= 3:
                act.wait_ge(s.sum, s.was.sum + n - 2)
            nc.scalar.activation(m.sg[:, n % 3, :], m.x[:, k, cols(c)], ACT.Square).then_inc(s.sq, 1)

    squares(0)
    for c in range(NCH):
        if c + 1 < NCH:
            squares(c + 1)
        if c == 0:
            first_weights()
        act.wait_ge(s.var, s.was.var + c + 1)
        nc.scalar.activation(m.rstd[:, 1, :], m.rstd[:, 0, :], ACT.Sqrt).then_inc(s.std, 1)
        for k in range(KD):
            n = c * KD + k
            act.wait_ge(s.xn, s.was.xn + n + 1)
            nc.scalar.activation(m.xn[:, k, 0, cols(c)], m.hf[:, n % 3, :], ACT.Copy).then_inc(s.hi, 1)


def norm_pe(nc, pe, m, s):
    for n in range(NCH * KD):
        c, k = divmod(n, KD)
        if c == 2 and k == 0:
            pe.wait_ge(s.var, s.was.var + 1)
        pe.wait_ge(s.sq, s.was.sq + n + 1)
        nc.tensor.matmul(m.ps[:, 6 + c % 2, :CH], m.ones[:], m.sg[:, n % 3, :],
                         start=(k == 0), stop=(k == KD - 1)).then_inc(s.sum, 1)


def norm_dve(nc, dve, m, s, gain):
    for c in range(NCH):
        dve.wait_ge(s.sum, s.was.sum + KD * (c + 1))
        nc.vector.tensor_scalar(m.rstd[:, 0, :], m.ps[:, 6 + c % 2, :CH], 1.0 / D, EPS, ALU.mult,
                                ALU.add).then_inc(s.var, 1)
        dve.wait_ge(s.std, s.was.std + c + 1)
        nc.vector.reciprocal(m.rstd[:, 2, :], m.rstd[:, 1, :]).then_inc(s.rs, 1)
        dve.wait_ge(s.rs, s.was.rs + c + 1)
        for k in range(KD):
            n = c * KD + k
            if n >= 3:
                dve.wait_ge(s.lo, s.was.lo + n - 2)
            nc.vector.scalar_tensor_tensor(out=m.hf[:, n % 3, :], in0=m.x[:, k, cols(c)],
                                           scalar=gain[:, k:k + 1], in1=m.rstd[:, 2, :],
                                           op0=ALU.mult, op1=ALU.mult).then_inc(s.xn, 1)


def norm_pool(nc, pool, m, s, first_weights):
    first_weights()
    for n in range(NCH * KD):
        c, k = divmod(n, KD)
        pool.wait_ge(s.hi, s.was.hi + n + 1)
        nc.gpsimd.tensor_tensor(m.xn[:, k, 1, cols(c)], m.hf[:, n % 3, :],
                                m.xn[:, k, 0, cols(c)].bitcast(F32), ALU.subtract).then_inc(s.lo, 1)



def ffn_sp(nc, sp, m, s, w_gate, w_up, w_down):
    def gate_up(f, skip_wait=False):
        for half in range(2):
            if not skip_wait:
                sp.wait_ge(s.wlo, s.was.wlo + 2 * f + half - 1)
            w = (w_gate, w_up)[half].rearrange("(k p) n -> p k n", p=P)
            sp.dma_start(m.wr[:, half, :].rearrange("p (k n) -> p k n", k=KD),
                         w[:, :, bass.ds(f * P, P)]).then_inc(s.wraw[half], 16)

    def down(p, skip_wait=False):
        for e in range(2):
            if not skip_wait:
                sp.wait_ge(s.dlo, s.was.dlo + 2 * p + e - 1)
            sp.dma_start(m.dr[:, e, :], w_down[bass.ds((2 * p + e) * P, P), :]).then_inc(s.draw[e], 16)

    gate_up(0, True)
    gate_up(1)
    down(0, True)
    with sp.Fori(0, (NPAIR - 1) // 2) as i:
        for q in range(2):
            p = 2 * i + 1 + q
            gate_up(2 * p)
            gate_up(2 * p + 1)
            down(p)


def ffn_act_split(nc, act, m, s, f, e, half, used=True):
    act.wait_ge(s.wraw[half], s.was.wraw + 16 * (f + 1))
    if used:
        act.wait_ge(s.up, s.was.up + NCH * (f - 1))
    nc.scalar.activation(m.wh[:, 2 * e + half, 0, :], m.wr[:, half, :], ACT.Copy).then_inc(s.whi, 1)


def ffn_act(nc, act, m, s):
    def silu(f, used=True):
        for c in range(NCH):
            act.wait_ge(s.gate, s.was.gate + NCH * f + c + 1)
            if used:
                act.wait_ge(s.mul, s.was.mul + NCH * (f - 1) + c + 1)
            nc.scalar.activation(m.sg[:, c, :], m.ps[:, c, :CH], ACT.Silu).then_inc(s.silu, 1)

    def split_down(p, used=True):
        for e in range(2):
            act.wait_ge(s.draw[e], s.was.draw + 16 * (p + 1))
            if used:
                act.wait_ge(s.down, s.was.down + NCH * KD * p)
            nc.scalar.activation(m.dh[:, e, 0, :], m.dr[:, e, :], ACT.Copy).then_inc(s.dhi, 1)

    def pair(p, e0_used=True, last=False):
        f = 2 * p
        for e in range(2):
            if not (last and e):
                for half in range(2):
                    ffn_act_split(nc, act, m, s, f + e + 1, (e + 1) % 2, half, e0_used or e)
            silu(f + e, e0_used or e)
        split_down(p, e0_used)

    pair(0, False)
    with act.Fori(0, (NPAIR - 1) // 2 - 1) as i:
        pair(2 * i + 1)
        pair(2 * i + 2)
    pair(NPAIR - 2)
    pair(NPAIR - 1, last=True)


def ffn_pool_split(nc, pool, m, s, f, e, half):
    pool.wait_ge(s.whi, s.was.whi + 2 * f + half + 1)
    nc.gpsimd.tensor_tensor(m.wh[:, 2 * e + half, 1, :], m.wr[:, half, :],
                            m.wh[:, 2 * e + half, 0, :].bitcast(F32), ALU.subtract).then_inc(s.wlo, 1)


def ffn_pool(nc, pool, m, s):
    def hidden(f, slot):
        for c in range(NCH):
            pool.wait_ge(s.hhi, s.was.hhi + NCH * f + c + 1)
            nc.gpsimd.tensor_tensor(m.hh[:, slot, 1, cols(c)], m.hf[:, c, :],
                                    m.hh[:, slot, 0, cols(c)].bitcast(F32), ALU.subtract).then_inc(s.hlo, 1)

    def split_down(p):
        for e in range(2):
            pool.wait_ge(s.dhi, s.was.dhi + 2 * p + e + 1)
            nc.gpsimd.tensor_tensor(m.dh[:, e, 1, :], m.dr[:, e, :],
                                    m.dh[:, e, 0, :].bitcast(F32), ALU.subtract).then_inc(s.dlo, 1)

    def pair(p, par, last=False):
        for e in range(2):
            if not (last and e):
                for half in range(2):
                    ffn_pool_split(nc, pool, m, s, 2 * p + e + 1, (e + 1) % 2, half)
            hidden(2 * p + e, 2 * par + e)
        split_down(p)

    pair(0, 0)
    with pool.Fori(0, (NPAIR - 1) // 2 - 1) as i:
        pair(2 * i + 1, 1)
        pair(2 * i + 2, 0)
    pair(NPAIR - 2, 1)
    pair(NPAIR - 1, 0, last=True)


def ffn_pe(nc, pe, m, s):
    def gate_up(f, e, used=True):
        pe.wait_ge(s.wlo, s.was.wlo + 2 * f + 2)
        for c in range(NCH):
            if not used:
                pe.wait_ge(s.lo, s.was.lo + KD * (c + 1))
            for half, done in ((0, s.gate), (1, s.up)):
                if used:
                    pe.wait_ge((s.silu, s.mul)[half], s.was.silu + NCH * (f - 1) + c + 1)
                for k in range(KD):
                    for n, (a, b) in enumerate(PASSES):
                        mm = nc.tensor.matmul(m.ps[:, NCH * half + c, :CH],
                                              m.wh[:, 2 * e + half, a, k * P:(k + 1) * P],
                                              m.xn[:, k, b, cols(c)],
                                              start=(k == 0 and n == 0), stop=(k == KD - 1 and n == 2))
                mm.then_inc(done, 1)

    def down(p, par, used=True):
        pe.wait_ge(s.hlo, s.was.hlo + NCH * (2 * p + 2))
        pe.wait_ge(s.dlo, s.was.dlo + 2 * p + 2)
        for o in range(KD):
            for c in range(NCH):
                n = NCH * o + c
                if used or n >= 2:
                    pe.wait_ge(s.acc, s.was.acc + NCH * KD * p + n - 1)
                for e in range(2):
                    for t, (a, b) in enumerate(PASSES):
                        mm = nc.tensor.matmul(m.ps[:, 6 + n % 2, :CH], m.dh[:, e, a, o * P:(o + 1) * P],
                                              m.hh[:, 2 * par + e, b, cols(c)],
                                              start=(e == 0 and t == 0), stop=(e == 1 and t == 2))
                mm.then_inc(s.down, 1)

    gate_up(0, 0, False)
    gate_up(1, 1)
    gate_up(2, 0)
    gate_up(3, 1)
    down(0, 0, False)
    gate_up(4, 0)
    gate_up(5, 1)
    down(1, 1)
    with pe.Fori(0, (NPAIR - 3) // 2) as i:
        for q in range(2):
            f = 4 * i + 2 * q + 6
            gate_up(f, 0)
            gate_up(f + 1, 1)
            down(2 * i + q + 2, q)
    down(NPAIR - 1, 0)


def ffn_dve(nc, dve, m, s):
    def hidden(f, slot, used=True, reuse=True):
        for c in range(NCH):
            dve.wait_ge(s.silu, s.was.silu + NCH * f + c + 1)
            dve.wait_ge(s.up, s.was.up + NCH * f + c + 1)
            if not used:
                dve.wait_ge(s.lo, s.was.lo + NCH * KD)
            if used:
                dve.wait_ge(s.hlo, s.was.hlo + NCH * (f - 1) + c + 1)
            nc.vector.tensor_tensor(m.hf[:, c, :], m.sg[:, c, :], m.ps[:, NCH + c, :CH],
                                    ALU.mult).then_inc(s.mul, 1)
            dve.wait_ge(s.mul, s.was.mul + NCH * f + c + 1)
            nc.vector.tensor_copy(m.hh[:, slot, 0, cols(c)], m.hf[:, c, :]).then_inc(s.hhi, 1)

    def accumulate(p):
        for n in range(NCH * KD):
            o, c = divmod(n, NCH)
            dve.wait_ge(s.down, s.was.down + NCH * KD * p + n + 1)
            xs = m.x[:, o, cols(c)]
            nc.vector.scalar_tensor_tensor(out=xs, in0=m.ps[:, 6 + n % 2, :CH], scalar=0.5, in1=xs,
                                           op0=ALU.mult, op1=ALU.add).then_inc(s.acc, 1)

    hidden(0, 0, False)
    hidden(1, 1)
    hidden(2, 2)
    hidden(3, 3)
    accumulate(0)
    hidden(4, 0)
    hidden(5, 1)
    accumulate(1)
    with dve.Fori(0, (NPAIR - 3) // 2) as i:
        for q in range(2):
            f = 4 * i + 2 * q + 6
            hidden(f, 2 * ((1 + q) % 2))
            hidden(f + 1, 2 * ((1 + q) % 2) + 1)
            accumulate(2 * i + q + 2)
    accumulate(NPAIR - 1)


FFN_SEMS = ("sq", "sum", "var", "std", "rs", "xn", "hi", "lo",
            "whi", "wlo", "gate", "up", "silu", "mul", "hhi", "hlo", "dhi", "dlo", "down", "acc")


NORM_ADDS = dict(sq=NCH * KD, sum=NCH * KD, var=NCH, std=NCH, rs=NCH, xn=NCH * KD, hi=NCH * KD, lo=NCH * KD)
FFN_ADDS = dict(whi=2 * NF, wlo=2 * NF, gate=NCH * NF, up=NCH * NF, silu=NCH * NF, mul=NCH * NF, hhi=NCH * NF,
                hlo=NCH * NF, dhi=NF, dlo=NF, down=NCH * KD * NPAIR, acc=NCH * KD * NPAIR, wraw=16 * NF,
                draw=16 * NPAIR)


def ffn_sems(sem, name):
    s = {n: sem(f"{name}_{n}") for n in FFN_SEMS}
    s["wraw"] = [sem(f"{name}_gate_landed"), sem(f"{name}_up_landed")]
    s["draw"] = [sem(f"{name}_down_even_landed"), sem(f"{name}_down_odd_landed")]
    return s


def after_uses(s, norms, ffns):
    was = {n: norms * c for n, c in NORM_ADDS.items()} | {n: ffns * c for n, c in FFN_ADDS.items()}
    return record("FfnSems", s | {"was": record("Counts", was)})


def ffn_memory(sb, m, name):
    m.wh = sb(f"{name}_weights_split", [P, 4, 2, KD * P], F32R)
    m.wr = sb(f"{name}_weights_raw", [P, 2, KD * P])
    m.hh = sb(f"{name}_hidden_split", [P, 4, 2, T], F32R)
    m.dh = sb(f"{name}_down_split", [P, 2, 2, D], F32R)
    m.dr = sb(f"{name}_down_raw", [P, 2, D])
    m.sg = sb(f"{name}_silu", [P, NCH, CH])
    m.hf = sb(f"{name}_hidden", [P, NCH, CH])
    m.rstd = sb(f"{name}_rstd", [P, 3, CH])
N_HEADS, HD = 8, 64
D_ATTN = N_HEADS * HD
IDX_HEADS, IDX = 4, 64
TOPK = 256
SSM_W = 512
C_Q, C_K, C_V = 0, D_ATTN, 2 * D_ATTN
C_QI = 3 * D_ATTN
C_KI = C_QI + IDX_HEADS * IDX
C_U = C_KI + IDX + IDX_HEADS
C_G = C_U + SSM_W
NB = TP // P
NEG = -1e30
TAKEN = -3e38
GROUPS = (("ki", C_KI, IDX + IDX_HEADS, 1), ("qi", C_QI, P, 2), ("q", C_Q, P, 4), ("k", C_K, P, 4),
          ("v", C_V, P, 4), ("u", C_U, P, 4), ("g", C_G, P, 2 * KD - 2),
          ("g_last", C_G + (2 * KD - 2) * P, P, 2))
FIRST = {}
_n = 0
for _name, _, _, _units in GROUPS:
    FIRST[_name] = _n
    _n += _units
N_UNITS = _n
SCORE_AT = {b: P * sum(range(3, b + 1)) for b in range(2, NB)}
SCORE_COLS = P * sum(range(3, NB + 1))


def mix_memory(sb, m):
    m.qT = sb("q_T", [P, 4, T])
    m.kT = sb("k_T", [P, 4, T])
    m.qiT = sb("q_index_T", [P, 2, T])
    m.kiw = sb("k_index_and_weights_T", [P, T])
    m.ki2 = sb("k_index_T_high", [P, T])
    m.score = sb("scores", [P, SCORE_COLS])
    m.wi = sb("index_weights", [P, NB, IDX_HEADS])
    m.smp_i = sb("sample_index_rows", [TS, IDX_HEADS * IDX + IDX_HEADS])
    m.bias01 = sb("bias_of_first_blocks", [P, 2 * P])


def proj_memory(sb, m):
    m.ph = sb("in_weights_split", [P, 2, 2, KD * P], F32R)
    m.pr = sb("in_weights_raw", [P, 2, KD * P])
    m.tmp = sb("projected", [P, 2, T])
    m.stage = sb("token_major", [P, 8, P])
    m.stage_s = sb("token_major_samples", [TS, P])


MIX_SEMS = ("hi", "lo", "mm", "ev", "tr", "tev", "staged", "ki_copied", "wi_T", "wi", "smp_T", "smp_out", "dots", "relu",
            "score", "chain", "steps", "gate_out", "dram", "bcast", "rows", "turned", "taken", "link", "raw0", "raw1")


def each_unit(engine, body):
    for name, _, _, units in GROUPS:
        f = FIRST[name]
        if units <= 2:
            for j in range(units):
                body(name, j, (f + j) % 2, f + j)
        else:
            with engine.Fori(0, units // 2) as i:
                for e in range(2):
                    body(name, 2 * i + e, (f + e) % 2, 2 * i + (f + e))
        yield name


def run_units(engine, body, after=lambda name: None):
    for name in each_unit(engine, body):
        after(name)


TOKEN_MAJOR = ("ki", "q", "k", "v", "u")
TMAJ_BEFORE = {}
_n = 0
for _name, _, _, _units in GROUPS:
    TMAJ_BEFORE[_name] = _n
    if _name in TOKEN_MAJOR:
        _n += _units
N_TMAJ = _n


def proj_sp(nc, sp, m, s, w_in, o, x_away):
    w = w_in.rearrange("(k p) n -> p k n", p=P)
    col = {g[0]: g[1] for g in GROUPS}
    raw = (s.raw0, s.raw1)

    def load(name, j, par, u):
        if name == "qi" and j == 1:
            x_away()
        width = dict((g[0], g[2]) for g in GROUPS)[name]
        if not (isinstance(u, int) and u < 2):
            sp.wait_ge(s.lo, u - 1)
        sp.dma_start(m.pr[:, par, :].rearrange("p (k n) -> p k n", k=KD)[:, :, :width],
                     w[:, :, bass.ds(j * P + col[name], width)]).then_inc(raw[par], 16)

    run_units(sp, load)


def proj_act_split(nc, act, m, s, u, par, width=P):
    act.wait_ge((s.raw0, s.raw1)[par], 8 * (u - par) + 16)
    if not (isinstance(u, int) and u < 2):
        act.wait_ge(s.mm, NCH * (u - 1))
    src = m.pr[:, par, :].rearrange("p (k n) -> p k n", k=KD)[:, :, :width]
    dst = m.ph[:, par, 0, :].rearrange("p (k n) -> p k n", k=KD)[:, :, :width]
    nc.scalar.activation(dst, src, ACT.Copy).then_inc(s.hi, 1)


def proj_act(nc, act, m, s, s_io, o):
    def unit(name, j, par, u):
        width = dict((g[0], g[2]) for g in GROUPS)[name]
        if not (isinstance(u, int) and u == N_UNITS - 1):
            proj_act_split(nc, act, m, s, u + 1, 1 - par)
        out = {"ki": lambda c: m.kiw[:width, cols(c)],
               "qi": lambda c: m.qiT[:, j, cols(c)]}.get(name, lambda c: m.tmp[:, par, cols(c)])
        if name == "q":
            act.wait_ge(s.score, IDX_HEADS * (NB - 2))
        for c in range(NCH):
            act.wait_ge(s.mm, NCH * u + c + 1)
            src = m.ps[:width, 3 * par + c, :CH]
            if name in ("q", "k"):
                to = m.qT if name == "q" else m.kT
                nc.scalar.activation(to[:, bass.ds(j, 1), cols(c)].rearrange("p a t -> p (a t)"), src, ACT.Copy)
            f = ACT.Sigmoid if name[0] == "g" else ACT.Copy
            nc.scalar.activation(out(c), src, f).then_inc(s.ev, 1)
        if name in TOKEN_MAJOR:
            turn_out(name, j, par, u)
        if name[0] == "g":
            act.wait_ge(s.ev, NCH * (u + 1))
            g = j if name == "g" else j + 2 * KD - 2
            act.dma_start(o.gates[bass.ds(g * P, P), :], m.tmp[:, par, :]).then_inc(s.gate_out, 16)
            act.wait_ge(s.gate_out, 16 * (g + 1))

    def turn_out(name, j, par, u):
        width = IDX if name == "ki" else P
        n = u - FIRST[name] + TMAJ_BEFORE[name]
        if name != "ki":
            act.wait_ge(s.dram, 32 * n)
        for half in range(2):
            act.wait_ge(s.tr, 3 * n + half + 1)
            if name == "u":
                dst = m.stage[:].rearrange("p b n -> p (b n)").rearrange("p (g r c) -> p g r c", g=8, r=8)
                dst = dst[:, :, 4 * half:4 * half + 4, :]
                src = m.ps[:, 6 + half, :].rearrange("p (r g c) -> p g r c", r=4, g=8)
            else:
                dst = m.stage[:, 4 * half:4 * half + 4, :width]
                src = m.ps[:, 6 + half, :].rearrange("p (b n) -> p b n", b=4)[:, :, :width]
            nc.scalar.activation(dst, src, ACT.Copy).then_inc(s.tev, 1)
        act.wait_ge(s.tr, 3 * n + 3)
        nc.scalar.activation(m.stage_s[:, :width], m.ps[:TS, 3 * par, :width], ACT.Copy).then_inc(s.tev, 1)
        act.wait_ge(s.tev, 3 * n + 3)
        tok, smp = o.token_major[name]
        c0 = bass.ds(j * P, width) if name != "ki" else slice(0, IDX)
        if name == "u":
            act.dma_start(tok[:, bass.ds(j * NB * P, NB * P)],
                          m.stage[:].rearrange("p b n -> p (b n)")).then_inc(s.dram, 16)
        else:
            act.dma_start(tok[:, :, c0], m.stage[:, :, :width]).then_inc(s.dram, 16)
        act.dma_start(smp[:, c0], m.stage_s[:, :width]).then_inc(s.dram, 16)

    def after(name):
        if name == "ki":
            act.wait_ge(s.ev, NCH)
            act.dma_start(m.ki2[IDX:2 * IDX, :], m.kiw[0:IDX, :]).then_inc(s.ki_copied, 16)
            act.wait_ge(s.wi_T, 1)
            nc.scalar.activation(m.wi[:].rearrange("p b h -> p (b h)"), m.ps[:, 6, :NB * IDX_HEADS],
                                 ACT.Copy, scale=(IDX_HEADS * IDX) ** -0.5).then_inc(s.wi, 1)
            nc.scalar.activation(m.smp_i[:, 2 * P:], m.ps[:TS, 6, 2 * P:2 * P + IDX_HEADS],
                                 ACT.Copy, scale=(IDX_HEADS * IDX) ** -0.5).then_inc(s.wi, 1)
        if name == "k":
            act.wait_ge(s.smp_out, 32)
            act.wait_ge(s_io.x_away, 16)
            for dst, src in ((m.wib, o.wi_s), (m.qib, o.qi_s)):
                act.dma_start(dst, src.rearrange("(a b) c -> a (b c)", a=1)
                              .to_broadcast([P, dst.shape[1]])).then_inc(s.bcast, 16)
        if name == "qi":
            act.wait_ge(s.smp_T, 1)
            nc.scalar.activation(m.smp_i[:, :2 * P], m.ps[:TS, 7, :2 * P], ACT.Copy).then_inc(s.wi, 1)
            act.wait_ge(s.wi, 3)
            act.dma_start(o.qi_s, m.smp_i[:, :2 * P]).then_inc(s.smp_out, 16)
            act.dma_start(o.wi_s, m.smp_i[:, 2 * P:]).then_inc(s.smp_out, 16)
            for n, (b, h) in enumerate((b, h) for b in range(2, NB) for h in range(IDX_HEADS)):
                w = (b + 1) * P
                act.wait_ge(s.dots, n + 1)
                if n >= 2:
                    act.wait_ge(s.score, n - 1)
                nc.scalar.activation(m.tmp[:, n % 2, :w],
                                     m.ps[:, 4 + 2 * (n % 2):6 + 2 * (n % 2), :]
                                     .rearrange("p a n -> p (a n)")[:, :w], ACT.Relu).then_inc(s.relu, 1)

    run_units(act, unit, after)
    act.wait_ge(s.dram, 32 * N_TMAJ)
    act.wait_ge(s.smp_out, 32)
    act.wait_ge(s.gate_out, 16 * 2 * KD)


def proj_pool_split(nc, pool, m, s, name, par, u):
    width = dict((g[0], g[2]) for g in GROUPS)[name]
    pool.wait_ge(s.hi, u + 1)
    v = [x.rearrange("p (k n) -> p k n", k=KD)[:, :, :width]
         for x in (m.ph[:, par, 1, :], m.pr[:, par, :], m.ph[:, par, 0, :])]
    nc.gpsimd.tensor_tensor(v[0], v[1], v[2].bitcast(F32), ALU.subtract).then_inc(s.lo, 1)


def proj_pool(nc, pool, m, s):
    def unit(name, j, par, u):
        if name != "ki":
            proj_pool_split(nc, pool, m, s, name, par, u)
    run_units(pool, unit)


def proj_pe(nc, pe, m, s, s_norm):
    def unit(name, j, par, u):
        width = dict((g[0], g[2]) for g in GROUPS)[name]
        static = isinstance(u, int)
        pe.wait_ge(s.lo, u + 1)
        if not (static and u < 2):
            pe.wait_ge(s.ev, NCH * (u - 1))
        if name == "q":
            pe.wait_ge(s.relu, IDX_HEADS * (NB - 2))
        for c in range(NCH):
            if name == "ki":
                pe.wait_ge(s_norm.lo, s_norm.was.lo + KD * (c + 1))
            for k in range(KD):
                for n, (a, b) in enumerate(PASSES):
                    mm = nc.tensor.matmul(m.ps[:width, 3 * par + c, :CH],
                                          m.ph[:, par, a, k * P:k * P + width], m.xn[:, k, b, cols(c)],
                                          start=(k == 0 and n == 0), stop=(k == KD - 1 and n == 2))
            mm.then_inc(s.mm, 1)
        if name in TOKEN_MAJOR:
            turn(name, j, par, u)

    def turn(name, j, par, u):
        width = IDX if name == "ki" else P
        n = u - FIRST[name] + TMAJ_BEFORE[name]
        src = m.kiw[:, :] if name == "ki" else m.tmp[:, par, :]
        turn_blocks(src, name, width, par, u, n)

    def turn_blocks(src, name, width, par, u, n):
        pe.wait_ge(s.ev, NCH * (u + 1))
        if name != "ki":
            pe.wait_ge(s.tev, 3 * n)
        for b in range(NB):
            blk = src[:width, NB - 1 - b:TP:NB] if name == "u" else src[:width, b * P:(b + 1) * P]
            mm = nc.tensor.transpose(m.ps[:, 6 + b // 4, (b % 4) * P:(b % 4) * P + width], blk,
                                     m.ident[:width, :width])
            if b % 4 == 3:
                mm.then_inc(s.tr, 1)
        nc.tensor.transpose(m.ps[:TS, 3 * par, :width], src[:width, TP:T],
                            m.ident[:width, :width]).then_inc(s.tr, 1)
        if name == "ki":
            pe.wait_ge(s.tev, 3)
            for b in range(NB):
                mm = nc.tensor.transpose(m.ps[:, 6, b * IDX_HEADS:(b + 1) * IDX_HEADS],
                                         m.kiw[IDX:IDX + IDX_HEADS, b * P:(b + 1) * P],
                                         m.ident[IDX:IDX + IDX_HEADS, IDX:IDX + IDX_HEADS])
            nc.tensor.transpose(m.ps[:TS, 6, 2 * P:2 * P + IDX_HEADS], m.kiw[IDX:IDX + IDX_HEADS, TP:T],
                                m.ident[IDX:IDX + IDX_HEADS, IDX:IDX + IDX_HEADS]).then_inc(s.wi_T, 1)

    def after(name):
        if name != "qi":
            return
        pe.wait_ge(s.ki_copied, 16)
        pe.wait_ge(s.ev, NCH * 3)
        for j in range(2):
            mm = nc.tensor.transpose(m.ps[:TS, 7, j * P:(j + 1) * P], m.qiT[:, j, TP:T], m.ident[:])
        mm.then_inc(s.smp_T, 1)
        pe.wait_ge(s.wi, 3)
        for n, (b, h) in enumerate((b, h) for b in range(2, NB) for h in range(IDX_HEADS)):
            lo = (h % 2) * IDX
            keys = (m.kiw, m.ki2)[h % 2]
            if n >= 2:
                pe.wait_ge(s.relu, n - 1)
            for k0 in range(0, (b + 1) * P, 512):
                k1 = min(k0 + 512, (b + 1) * P)
                mm = nc.tensor.matmul(m.ps[:, 4 + 2 * (n % 2) + k0 // 512, :k1 - k0],
                                      m.qiT[lo:lo + IDX, h // 2, b * P:(b + 1) * P],
                                      keys[lo:lo + IDX, k0:k1], start=True, stop=True)
            mm.then_inc(s.dots, 1)

    run_units(pe, unit, after)
    smp_pe_rows(nc, pe, m, s)


def select_dve(nc, dve, m, s, s_io):
    dve.wait_ge(s.wi, 1)
    for n, (b, h) in enumerate((b, h) for b in range(2, NB) for h in range(IDX_HEADS)):
        w = (b + 1) * P
        sc = m.score[:, SCORE_AT[b]:SCORE_AT[b] + w]
        dve.wait_ge(s.relu, n + 1)
        if h == 0:
            nc.vector.tensor_scalar(sc, m.tmp[:, n % 2, :w], m.wi[:, b, 0:1], None,
                                    ALU.mult).then_inc(s.score, 1)
        else:
            dve.wait_ge(s.score, n)
            nc.vector.scalar_tensor_tensor(out=sc, in0=m.tmp[:, n % 2, :w], scalar=m.wi[:, b, h:h + 1],
                                           in1=sc, op0=ALU.mult, op1=ALU.add).then_inc(s.score, 1)
    dve.wait_ge(s.score, IDX_HEADS * (NB - 2))
    for b in range(2, NB):
        diag = m.score[:, SCORE_AT[b] + b * P:SCORE_AT[b] + (b + 1) * P]
        nc.vector.tensor_tensor(diag, diag, m.bias01[:, P:], ALU.add).then_inc(s.chain, 1)
    dve.wait_ge(s.chain, NB - 2)
    dve.wait_ge(s_io.x_away, 16)
    tile = lambda b: m.score[:, SCORE_AT[b]:SCORE_AT[b] + (b + 1) * P]
    best_keys(nc, dve, Steps(dve, s.steps), m, ([tile(b) for b in (7, 4, 3)], [tile(b) for b in (6, 5, 2)]), TOPK,
              m.work)
    smp_dve_scores(nc, dve, m, s, s_io)

class Steps:

    def __init__(self, engine, sem):
        self.engine, self.sem, self.n = engine, sem, 0

    def issued(self, instruction):
        instruction.then_inc(self.sem, 1)
        self.n += 1
        return self.n

    def done(self, *instructions):
        for x in instructions:
            self.issued(x)
        self.engine.wait_ge(self.sem, self.n)


def sel_memory(sb, m):
    m.sel_i = sb("selection_bits", [P, 6, NB - 2], I32)
    m.sel_n = sb("selection_counts", [P, 3, NB - 2])


def best_keys(nc, dve, steps, m, groups, k, work):
    V = nc.vector
    tiles = groups[0] + groups[1]
    n = [len(g) for g in groups]
    first = [0, n[0]]
    part = lambda x, g: x[:, first[g]:first[g] + n[g]]
    found, cand, flip, bit, top, reach = (m.sel_i[:, q, :] for q in range(6))
    count, more, need = (m.sel_n[:, q, :] for q in range(3))
    limit = flip.bitcast(F32)
    last = {}
    at = [0]

    def need_step(x):
        dve.wait_ge(steps.sem, at[0] + x)

    def short_steps(g, update):
        f, c, fl, b, t, r, cn = (part(x, g) for x in (found, cand, flip, bit, top, reach, count))
        ops = []
        if update:
            ops += [lambda: V.tensor_scalar(r, cn, float(k), -1.0, ALU.is_ge, ALU.mult),
                    lambda: V.tensor_tensor(c, r, b, ALU.bitwise_and),
                    lambda: V.tensor_tensor(f, f, c, ALU.bitwise_or),
                    lambda: V.tensor_scalar(b, b, 1, None, ALU.logical_shift_right)]
        ops += [lambda: V.tensor_tensor(c, f, b, ALU.bitwise_or),
                lambda: V.tensor_scalar(fl, c, 31, -1, ALU.arith_shift_right, ALU.bitwise_xor),
                lambda: V.tensor_tensor(fl, fl, t, ALU.bitwise_or),
                lambda: V.tensor_tensor(fl, fl, c, ALU.bitwise_xor)]

        def run(q, op):
            need_step(last[g])
            last[g] = steps.issued(op())
        return [lambda q=q, op=op: run(q, op) for q, op in enumerate(ops)]

    def counts(g, out, op, need_first):
        def run(q):
            need_step(need_first[0] if q < 2 else last["counts"][q - 2])
            t = first[g] + q
            w = tiles[t].shape[-1]
            last["counts"].append(steps.issued(V.tensor_scalar(
                work[:, q % 2, :w], tiles[t], limit[:, t:t + 1], 0.0, op, ALU.add, accum_out=out[:, t:t + 1])))
        last["counts"] = []
        return [lambda q=q: run(q) for q in range(n[g])]

    def side_by_side(long, short):
        per = -(-len(short) // len(long))
        for q, x in enumerate(long):
            x()
            for y in short[q * per:(q + 1) * per]:
                y()

    steps.done(V.memset(found, 0), V.memset(bit, 1))
    steps.done(V.tensor_scalar(bit, bit, 31, None, ALU.logical_shift_left))
    steps.done(V.tensor_copy(top, bit))
    for g in range(2):
        last[g] = steps.n
        for x in short_steps(g, False):
            x()
    need_step(steps.n)
    for x in counts(1, count, ALU.is_ge, [steps.n]):
        x()
    per_turn = len(tiles) + 2 * 8
    start = steps.n
    with dve.Fori(0, 32) as r:
        at[0] = per_turn * r
        last[1] = start
        side_by_side(counts(0, count, ALU.is_ge, [start]), short_steps(1, True))
        last[0] = last["counts"][-1]
        side_by_side(counts(1, count, ALU.is_ge, [last[1]]), short_steps(0, True))
    assert steps.n - start == per_turn
    steps.n += 31 * per_turn
    at[0] = 0
    need_step(steps.n)
    for g in range(2):
        for x in counts(g, more, ALU.is_gt, [steps.n]):
            x()
        need_step(steps.n)
    steps.done(V.tensor_scalar(need, more, -1.0, float(k), ALU.mult, ALU.add))
    for q, t in enumerate(tiles):
        w = t.shape[-1]
        equal, place = work[:, 0, :w], work[:, 1, :w]
        lim = limit[:, q:q + 1]
        steps.done(V.tensor_scalar(equal, t, lim, None, ALU.is_equal))
        steps.done(V.tensor_tensor_scan(out=place, data0=equal, data1=equal, initial=0.0, op0=ALU.add,
                                        op1=ALU.bypass))
        steps.done(V.scalar_tensor_tensor(out=equal, in0=place, scalar=need[:, q:q + 1], in1=equal,
                                          op0=ALU.is_le, op1=ALU.mult))
        steps.done(V.scalar_tensor_tensor(out=t, in0=t, scalar=lim, in1=equal, op0=ALU.is_gt, op1=ALU.add))
        steps.done(V.tensor_scalar(t, t, -1.0, -NEG, ALU.add, ALU.mult))

STEPS = [(b, h) for b in reversed(range(NB)) for h in range(N_HEADS)]
ATT_SEMS = ("v_in", "qk", "biased", "neg", "exp", "inv", "scaled", "turned", "pt", "pv", "ohi", "olo")


def att_memory(sb, m):
    m.v = sb("values", [P, NB, D_ATTN])
    m.prob = sb("probs", [P, 2, TP])
    m.pT = sb("probs_T", [P, 2, TP])
    m.st = sb("softmax_stats", [P, 2, 4])


def att_pe(nc, pe, m, s, samples):
    def qk(n):
        b, h = STEPS[n]
        lo = (h % 2) * HD
        if n >= 2:
            pe.wait_ge(s.biased, n - 1)
        for k0 in range(0, (b + 1) * P, 512):
            k1 = min(k0 + 512, (b + 1) * P)
            mm = nc.tensor.matmul(m.ps[:, 2 * (n % 2) + k0 // 512, :k1 - k0],
                                  m.qT[lo:lo + HD, h // 2, b * P:(b + 1) * P],
                                  m.kT[lo:lo + HD, h // 2, k0:k1], start=True, stop=True)
        mm.then_inc(s.qk, 1)

    def turn(n):
        b, h = STEPS[n]
        pe.wait_ge(s.scaled, n + 1)
        if n >= 1:
            pe.wait_ge(s.pt, n)
        for k in range(b + 1):
            mm = nc.tensor.transpose(m.ps[:, 4 + k // 4, (k % 4) * P:(k % 4 + 1) * P],
                                     m.prob[:, n % 2, k * P:(k + 1) * P], m.ident[:])
        mm.then_inc(s.turned, 1)

    def pv(n):
        b, h = STEPS[n]
        lo = (h % 2) * HD
        pe.wait_ge(s.pt, n + 1)
        if n >= 2:
            pe.wait_ge(s.olo, n - 1)
        for k in range(b + 1):
            mm = nc.tensor.matmul(m.ps[lo:lo + HD, 6, :P], m.v[:, k, h * HD:(h + 1) * HD],
                                  m.pT[:, n % 2, k * P:(k + 1) * P], start=(k == 0), stop=(k == b))
        mm.then_inc(s.pv, 1)

    n_last = len(STEPS)
    pe.wait_ge(s.v_in, 16)
    for n in range(n_last + 2):
        samples(n)
        if n < n_last:
            qk(n)
        if n >= 2:
            pv(n - 2)
        if 1 <= n <= n_last:
            turn(n - 1)


def att_dve(nc, dve, m, s, samples):
    def bias(n):
        b, h = STEPS[n]
        w = (b + 1) * P
        by = m.bias01[:, (1 - b) * P:2 * P] if b < 2 else m.score[:, SCORE_AT[b]:SCORE_AT[b] + w]
        dve.wait_ge(s.qk, n + 1)
        if n >= 2:
            dve.wait_ge(s.turned, n - 1)
        nc.vector.tensor_tensor_reduce(m.prob[:, n % 2, :w],
                                       m.ps[:, 2 * (n % 2):2 * (n % 2) + 2, :].rearrange("p a n -> p (a n)")[:, :w],
                                       by, HD ** -0.5, TAKEN, ALU.add, ALU.max,
                                       m.st[:, n % 2, 0:1]).then_inc(s.biased, 1)
        dve.wait_ge(s.biased, n + 1)
        nc.vector.tensor_scalar(m.st[:, n % 2, 1:2], m.st[:, n % 2, 0:1], -1.0, None,
                                ALU.mult).then_inc(s.neg, 1)

    def invert(n):
        dve.wait_ge(s.exp, n + 1)
        nc.vector.reciprocal(m.st[:, n % 2, 3:4], m.st[:, n % 2, 2:3]).then_inc(s.inv, 1)

    def low(n):
        b, h = STEPS[n]
        lo = (h % 2) * HD
        dve.wait_ge(s.ohi, n + 1)
        q = slice(b * P, (b + 1) * P)
        nc.vector.tensor_tensor(m.xn[lo:lo + HD, h // 2, 1, q], m.ps[lo:lo + HD, 6, :P],
                                m.xn[lo:lo + HD, h // 2, 0, q].bitcast(F32), ALU.subtract).then_inc(s.olo, 1)

    n_last = len(STEPS)
    for n in range(n_last + 2):
        samples(n)
        if 1 <= n <= n_last:
            invert(n - 1)
        if n < n_last:
            bias(n)
        if n >= 2:
            low(n - 2)


def att_act(nc, act, m, s, samples):
    def exp(n):
        b, h = STEPS[n]
        w = (b + 1) * P
        act.wait_ge(s.neg, n + 1)
        nc.scalar.activation(m.prob[:, n % 2, :w], m.prob[:, n % 2, :w], ACT.Exp, bias=m.st[:, n % 2, 1:2],
                             accum_out=m.st[:, n % 2, 2:3]).then_inc(s.exp, 1)

    def normalise(n):
        b, h = STEPS[n]
        w = (b + 1) * P
        act.wait_ge(s.inv, n + 1)
        nc.scalar.activation(m.prob[:, n % 2, :w], m.prob[:, n % 2, :w], ACT.Identity,
                             scale=m.st[:, n % 2, 3:4]).then_inc(s.scaled, 1)

    def keep_turned(n):
        b, h = STEPS[n]
        w = (b + 1) * P
        act.wait_ge(s.turned, n + 1)
        if n >= 2:
            act.wait_ge(s.pv, n - 1)
        nc.scalar.activation(m.pT[:, n % 2, :w],
                             m.ps[:, 4:6, :].rearrange("p a n -> p (a n)")[:, :w], ACT.Copy).then_inc(s.pt, 1)

    def high(n):
        b, h = STEPS[n]
        lo = (h % 2) * HD
        act.wait_ge(s.pv, n + 1)
        nc.scalar.activation(m.xn[lo:lo + HD, h // 2, 0, b * P:(b + 1) * P], m.ps[lo:lo + HD, 6, :P],
                             ACT.Copy).then_inc(s.ohi, 1)

    n_last = len(STEPS)
    for n in range(n_last + 2):
        samples(n)
        if 1 <= n <= n_last:
            normalise(n - 1)
        if n < n_last:
            exp(n)
        if n >= 2:
            high(n - 2)
        if 1 <= n <= n_last:
            keep_turned(n - 1)


PAGE = 128
PAST = TP
N_PAGES = PAST // PAGE
PER_ROW = PAST // P
NK = PAST + 1
SMP_SEMS = ("small", "small_out", "qb_in", "ddots", "c", "pc", "tree",
            "rows", "top", "mask_T", "k0", "k1", "v0", "v1", "kdone", "ln_out", "ln_in",
            "peak", "exp", "total", "ready", "olo", "vmm", "diag", "columns")
AT_NEW = 2
AT_TOP = AT_NEW + 1
ROUNDS = 2
AT_MASK = AT_TOP + TOPK // 8 // ROUNDS
AT_KEYS = {5: 1, 10: 3, 15: 5, 20: 7}
AT_SOFT = AT_MASK + 3
AT_PV = AT_SOFT + 3
PV_EVERY = 2
AT_OUT = AT_PV + PV_EVERY * TS


def smp_memory(sb, m):
    m.kidx = sb("past_k_index", [P, TS, PER_ROW, IDX])
    m.newi = sb("new_index_rows", [TS, IDX_HEADS + 1, IDX])
    m.sm8 = sb("new_small", [TS, 32 + IDX_HEADS * IDX])


def smp_views(m):
    x = m.x[:].rearrange("p k t -> p (k t)")
    m.page = x[:, :2 * PER_ROW * D_ATTN].rearrange("p (b j c) -> p b j c", b=2, j=PER_ROW)
    h = m.spare
    ends = np.cumsum([2 * TP, TS * IDX_HEADS * IDX, PER_ROW * IDX_HEADS * IDX, TS * PER_ROW * IDX_HEADS,
                      TS * PER_ROW, TS * IDX_HEADS]).tolist()
    work, m.qib, m.iprod, dot, sk, m.wib = (x[:, a:b] for a, b in zip([0] + ends, ends))
    m.work = work.rearrange("p (n w) -> p n w", n=2)
    m.dot = dot.rearrange("p (b j h) -> p b j h", b=TS, j=PER_ROW)
    m.sk = sk.rearrange("p (b j) -> p b j", b=TS)
    at = [0]

    def take(n, rows=P):
        at[0] += n
        return h[:rows, at[0] - n:at[0]]

    m.qb = take(TS * D_ATTN).rearrange("p (b c) -> p b c", b=TS)
    m.kb = take(PER_ROW * TS).rearrange("p (j b) -> p j b", j=PER_ROW)
    m.lg = take(TS * PER_ROW * N_HEADS).rearrange("p (b j h) -> p b j h", b=TS, j=PER_ROW)
    m.s64 = take(8 * TS * N_HEADS).rearrange("p (n c) -> p n c", n=8)
    m.of = take(4 * TS).rearrange("p (j b) -> p j b", j=4)
    m.pn = take(TS * N_HEADS, TS).rearrange("p (b h) -> p b h", b=TS)
    m.vnew = take(D_ATTN, TS)
    assert at[0] <= KD * T
    m.own = m.qb[:N_HEADS]
    m.kprod = m.kidx[:].rearrange("p b j d -> p (b j d)")
    m.qkn = m.kiw[:TS, :2 * D_ATTN].rearrange("p (n c) -> p n c", n=2)
    m.row = m.ki2[:TS, :NK]


def smp_load(pool, m, b, dst, cache, land):
    rows = cache.rearrange("n (r q) c -> (n r) (q c)", q=PER_ROW)
    pool.indirect_dma_start(dst.rearrange("p q c -> p (q c)"), None, rows,
                            bass.IndirectOffsetOnAxis(ap=m.pages[:, b:b + 1].bitcast(U32), axis=0)).then_inc(land, 16)


def smp_sp(nc, sp, m, s, i, o):
    sp.dma_start(m.qb.rearrange("p b c -> p (b c)"), o.q_s.rearrange("(a b) c -> a (b c)", a=1)
                 .to_broadcast([P, TS * D_ATTN])).then_inc(s.qb_in, 16)
    sp.dma_start(m.qkn[:, 0, :], o.q_s).then_inc(s.small_out, 16)
    sp.dma_start(m.qkn[:, 1, :], o.k_s).then_inc(s.small_out, 16)
    sp.dma_start(m.vnew, o.v_s).then_inc(s.small_out, 16)
    sp.dma_start(m.newi[:, IDX_HEADS, :], o.ki_s).then_inc(s.small_out, 16)
    sp.dma_start(m.newi[:, :IDX_HEADS, :].rearrange("p h d -> p (h d)"), o.qi_s).then_inc(s.small_out, 16)
    sp.dma_start(m.sm8[:, 0:IDX_HEADS], o.wi_s).then_inc(s.small_out, 16)
    sp.wait_ge(s.ln_out, 1)
    sp.dma_start(o.ln_s, m.sm8[:, 16:24]).then_inc(s.small, 16)
    sp.wait_ge(s.small, 16)
    sp.dma_start(m.s64[:, 4, :], o.ln_s.rearrange("(a b) c -> a (b c)", a=1)
                 .to_broadcast([P, TS * N_HEADS])).then_inc(s.ln_in, 16)


def smp_pool(nc, pool, m, s, i):
    G = nc.gpsimd
    steps = Steps(pool, s.tree)
    page = lambda b: m.page[:, b % 2]
    for b in range(2):
        smp_load(pool, m, b, page(b), i.cache_k, (s.k0, s.k1)[b])
    pool.wait_ge(s.qb_in, 16)
    for b in range(0, TS, 2):
        pool.wait_ge(s.k0, 16 * (b // 2 + 1))
        steps.done(G.tensor_tensor(page(b), page(b), m.qb[:, b:b + 1, :].to_broadcast([P, PER_ROW, D_ATTN]), ALU.mult))
        by_head = page(b).rearrange("p q (h d) -> p q h d", h=N_HEADS)
        n = HD // 2
        while n > 1:
            steps.done(G.tensor_tensor(by_head[:, :, :, :n], by_head[:, :, :, :n], by_head[:, :, :, n:2 * n], ALU.add))
            n //= 2
        steps.done(G.tensor_tensor(m.lg[:, b, :, :, None], by_head[:, :, :, :1], by_head[:, :, :, 1:2], ALU.add))
        for n in (b, b + 1):
            if n > b:
                pool.wait_ge(s.ddots, b // 2 + 1)
            nxt, cache, land = (n + 2, i.cache_k, (s.k0, s.k1)) if n + 2 < TS else (n + 2 - TS, i.cache_v, (s.v0, s.v1))
            smp_load(pool, m, nxt, page(n), cache, land[n % 2])
    pool.sem_inc(s.kdone, 1)
    pool.wait_ge(s.peak, 1)
    G.partition_all_reduce(m.s64[:, 1, :], m.s64[:, 0, :], P, bass.bass_isa.ReduceOp.max).then_inc(s.pc, 1)
    pool.wait_ge(s.total, 1)
    G.partition_all_reduce(m.s64[:, 3, :], m.s64[:, 2, :], P, bass.bass_isa.ReduceOp.add).then_inc(s.pc, 1)
    for b in range(2, TS):
        pool.wait_ge(s.vmm, b - 1)
        smp_load(pool, m, b, page(b), i.cache_v, (s.v0, s.v1)[b % 2])


def smp_dve_scores(nc, dve, m, s, s_io):
    V = nc.vector
    steps = Steps(dve, s.link)
    dve.wait_ge(s_io.ki_in, 16 * TS)
    dve.wait_ge(s.bcast, 32)
    sh = [P, PER_ROW, IDX_HEADS, IDX]
    prod = m.iprod.rearrange("p (q h d) -> p q h d", q=PER_ROW, h=IDX_HEADS)
    for b in range(TS):
        q = m.qib[:, b * IDX_HEADS * IDX:(b + 1) * IDX_HEADS * IDX].rearrange("p (a h d) -> p a h d", a=1, h=IDX_HEADS)
        steps.done(V.tensor_tensor(prod, m.kidx[:, b, :, None, :].to_broadcast(sh), q.to_broadcast(sh), ALU.mult))
        steps.done(V.tensor_reduce(m.dot[:, b], prod, AX.X, ALU.add))
    steps.done(V.tensor_scalar(m.dot, m.dot, 0.0, None, ALU.max))
    steps.done(V.tensor_tensor(m.dot, m.dot, m.wib.rearrange("p (b a h) -> p b a h", b=TS, a=1)
                               .to_broadcast([P, TS, PER_ROW, IDX_HEADS]), ALU.mult))
    V.tensor_reduce(m.sk, m.dot, AX.X, ALU.add).then_inc(s.rows, 1)
    for r in range(2):
        dve.wait_ge(s.turned, r + 1)
        V.tensor_copy(m.row[:, :NK - 1].rearrange("s (p q) -> s q p", q=PER_ROW)[:, 4 * r:4 * r + 4, :],
                      m.ps[:TS, 7, :].rearrange("s (q p) -> s q p", q=4)).then_inc(s.taken, 1)


def smp_pe_rows(nc, pe, m, s):
    pe.wait_ge(s.rows, 1)
    for r in range(2):
        if r:
            pe.wait_ge(s.taken, 1)
        for j in range(4 * r, 4 * r + 4):
            mm = nc.tensor.transpose(m.ps[:TS, 7, (j % 4) * P:(j % 4 + 1) * P], m.sk[:, :, j], m.ident[:])
        mm.then_inc(s.turned, 1)


def smp_dve(nc, dve, m, s):
    c = [0]

    def link(ins):
        c[0] += 1
        ins.then_inc(s.c, 1)
        dve.wait_ge(s.c, c[0])

    V = nc.vector
    S = lambda n: m.s64[:, n, :]
    S2 = lambda n: m.s64[:, n, :].rearrange("p (b h) -> p b h", b=TS)
    by_page = [P, TS, PER_ROW, N_HEADS]
    per_head = lambda n: m.s64[:, n, :].rearrange("p (b a h) -> p b a h", b=TS, a=1).to_broadcast(by_page)

    def new_keys():
        dve.wait_ge(s.small_out, 96)
        ip = m.sm8[:, 32:].rearrange("p (h d) -> p h d", h=IDX_HEADS)
        link(V.tensor_tensor(ip, m.newi[:, :IDX_HEADS, :],
                             m.newi[:, IDX_HEADS:, :].to_broadcast([TS, IDX_HEADS, IDX]), ALU.mult))
        link(V.tensor_reduce(m.sm8[:, 4:8], ip, AX.X, ALU.add))
        link(V.tensor_scalar(m.sm8[:, 4:8], m.sm8[:, 4:8], 0.0, None, ALU.max))
        link(V.tensor_tensor(m.sm8[:, 4:8], m.sm8[:, 4:8], m.sm8[:, 0:4], ALU.mult))
        link(V.tensor_reduce(m.row[:, NK - 1:NK], m.sm8[:, 4:8], AX.X, ALU.add))
        link(V.tensor_tensor(m.qkn[:, 0, :], m.qkn[:, 0, :], m.qkn[:, 1, :], ALU.mult))
        link(V.tensor_reduce(m.sm8[:, 8:16], m.qkn[:, 0, :].rearrange("p (h d) -> p h d", h=N_HEADS), AX.X, ALU.add))

    def key_dots(b):
        dve.wait_ge(s.k1, 16 * (b // 2 + 1))
        if b == 1:
            dve.wait_ge(s.qb_in, 16)
        page = m.page[:, 1]
        prod = m.kprod.rearrange("p (q c) -> p q c", q=PER_ROW)
        V.tensor_tensor(prod, page, m.qb[:, b:b + 1, :].to_broadcast([P, PER_ROW, D_ATTN]), ALU.mult).then_inc(s.ddots, 1)
        dve.wait_ge(s.ddots, b // 2 + 1)
        link(V.tensor_reduce(m.lg[:, b], prod.rearrange("p q (h d) -> p q h d", h=N_HEADS), AX.X, ALU.add))

    def select(n):
        for r in range((n - AT_TOP) * ROUNDS, (n - AT_TOP + 1) * ROUNDS):
            V.max(m.sm8[:, 24:32], m.row).then_inc(s.top, 1)
            dve.wait_ge(s.top, 2 * r + 1)
            V.match_replace(out=m.row, in_to_replace=m.sm8[:, 24:32], in_values=m.row,
                            imm_value=TAKEN).then_inc(s.top, 1)
            dve.wait_ge(s.top, 2 * r + 2)

    def mask():
        link(V.tensor_scalar(m.row, m.row, TAKEN / 2, NEG, ALU.is_gt, ALU.mult))
        dve.sem_inc(s.rows, 1)
        V.tensor_scalar(m.sm8[:, 16:24], m.sm8[:, 8:16], HD ** -0.5, m.row[:, NK - 1:NK], ALU.mult,
                        ALU.add).then_inc(s.ln_out, 1)

    def maxima():
        dve.wait_ge(s.mask_T, 1)
        link(V.tensor_copy(m.kb.rearrange("p j b -> p (j b)"), m.ps[:, 7, :PER_ROW * TS]))
        dve.wait_ge(s.kdone, 1)
        link(V.tensor_scalar(m.lg, m.lg, HD ** -0.5, None, ALU.mult))
        link(V.tensor_tensor(m.lg, m.lg, m.kb.rearrange("p j (b a) -> p b j a", a=1).to_broadcast(by_page), ALU.add))
        dve.wait_ge(s.ln_in, 16)
        link(V.tensor_reduce(S2(0), m.lg.rearrange("p b j h -> p b h j"), AX.X, ALU.max))
        V.tensor_tensor(S(0), S(0), S(4), ALU.max).then_inc(s.peak, 1)

    def subtract():
        dve.wait_ge(s.pc, 1)
        link(V.tensor_tensor(S(5), S(4), S(1), ALU.subtract))
        V.tensor_tensor(m.lg, m.lg, per_head(1), ALU.subtract).then_inc(s.ready, 1)

    def totals():
        dve.wait_ge(s.exp, 2)
        V.tensor_reduce(S2(2), m.lg.rearrange("p b j h -> p b h j"), AX.X, ALU.add).then_inc(s.total, 1)

    def probabilities():
        dve.wait_ge(s.pc, 2)
        link(V.tensor_tensor(S(6), S(3), S(5), ALU.add))
        link(V.reciprocal(S(7), S(6)))
        link(V.tensor_tensor(m.lg, m.lg, per_head(7), ALU.mult))
        link(V.tensor_tensor(S(5), S(5), S(7), ALU.mult))
        V.tensor_tensor(m.pn, m.s64[:TS, 5, :].rearrange("p (b h) -> p b h", b=TS),
                        m.ident[:TS, :TS, None].to_broadcast([TS, TS, N_HEADS]), ALU.mult).then_inc(s.ready, 1)

    def own_heads(b):
        dve.wait_ge(s.vmm, b + 1)
        V.tensor_tensor(m.own[:, b, :].rearrange("p (h d) -> p h d", h=N_HEADS),
                        m.ps[:N_HEADS, 7, :].rearrange("p (h d) -> p h d", h=N_HEADS),
                        m.ident[:N_HEADS, :N_HEADS, None].to_broadcast([N_HEADS, N_HEADS, HD]), ALU.mult).then_inc(s.diag, 1)

    def outputs():
        dve.wait_ge(s.columns, 1)
        link(V.tensor_copy(m.of, m.ps[:, 7, :4 * TS].rearrange("p (j b) -> p j b", j=4)))
        link(V.tensor_copy(m.xn[:, :4, 0, TP:T], m.of))
        V.tensor_tensor(m.xn[:, :4, 1, TP:T], m.of, m.xn[:, :4, 0, TP:T].bitcast(F32), ALU.subtract).then_inc(s.olo, 1)

    stages = {AT_NEW: new_keys, AT_MASK: mask, AT_SOFT: maxima,
              AT_SOFT + 1: subtract, AT_SOFT + 2: totals, AT_PV: probabilities, AT_OUT: outputs}

    def before(n):
        if AT_PV < n <= AT_OUT and (n - AT_PV) % PV_EVERY == 0:
            own_heads((n - AT_PV) // PV_EVERY - 1)
        if n in stages:
            stages[n]()
        elif AT_TOP <= n < AT_MASK:
            select(n)
        if n in AT_KEYS:
            key_dots(AT_KEYS[n])
    return before


def smp_pe(nc, pe, m, s):
    def biases():
        pe.wait_ge(s.rows, 1)
        for j in range(PER_ROW):
            mm = nc.tensor.transpose(m.ps[:, 7, j * TS:(j + 1) * TS], m.row[:, j:NK - 1:PER_ROW],
                                     m.ident[:TS, :TS])
        mm.then_inc(s.mask_T, 1)

    def values(b):
        if b == 0:
            pe.wait_ge(s.ready, 2)
        pe.wait_ge((s.v0, s.v1)[b % 2], 16 * (b // 2 + 1))
        if b:
            pe.wait_ge(s.diag, b)
        for q in range(PER_ROW):
            nc.tensor.matmul(m.ps[:N_HEADS, 7, :], m.lg[:, b, q, :], m.page[:, b % 2, q, :], start=(q == 0), stop=False)
        nc.tensor.matmul(m.ps[:N_HEADS, 7, :], m.pn[:, b, :], m.vnew, start=False, stop=True).then_inc(s.vmm, 1)

    def columns():
        pe.wait_ge(s.diag, TS)
        for j in range(4):
            for b in range(TS):
                mm = nc.tensor.matmul(m.ps[:, 7, j * TS + b:j * TS + b + 1], m.own[:, b, j * P:(j + 1) * P],
                                      m.ones[:N_HEADS, :1], start=True, stop=True)
        mm.then_inc(s.columns, 1)

    def before(n):
        if n == AT_MASK:
            biases()
        elif AT_PV <= n < AT_OUT and (n - AT_PV) % PV_EVERY == 0:
            values((n - AT_PV) // PV_EVERY)
        elif n == AT_OUT:
            columns()
    return before


def smp_act(nc, act, m, s):
    def before(n):
        if n == AT_SOFT + 1:
            act.wait_ge(s.ready, 1)
            lg = m.lg.rearrange("p b j h -> p (b j h)")
            nc.scalar.activation(lg, lg, ACT.Exp).then_inc(s.exp, 1)
            nc.scalar.activation(m.s64[:, 5, :], m.s64[:, 5, :], ACT.Exp).then_inc(s.exp, 1)
    return before
NG, GC, NS = 32, 16, 64
L = 8
NCK = TP // L
NI = NG // 2
HI = NI // 2
TWO_PI = (6.28125, 0.0019350051879882812, 3.0199159819567529e-07)
MAGIC = 12582912.0
SSM_SEMS = ("load", "c", "a", "dve", "pe", "evac", "kz_out", "m_in", "zero", "u_load", "u_T", "out", "late", "wg", "glu",
            "sig", "gate", "hi", "ut_in", "ub", "uc", "e8", "table", "q_built", "te")
NAMES = ("ar", "ai", "dt", "dtr", "dti", "n", "r", "mag", "sin", "sh", "er", "ei", "abr", "abi", "r8",
         "den", "nr", "fr", "fi", "t1", "t2", "e8r", "e8i", "u1", "u2")
SLOT = {n: k for k, n in enumerate(NAMES)}


def ssm_memory_keep(sb, m):
    m.Z = sb("chunk_states", [P, 2, NI, NCK + 1])
    m.y = sb("y_by_chunk", [P, L, SSM_W])
    m.ys = sb("y_samples", [TS, SSM_W])
    m.x0 = sb("sample_states", [P, 2, NI, TS])
    m.xs = sb("sample_new_states", [P, 2, NI, TS])
    z = m.Z[:].rearrange("p n i k -> p (n i k)")
    y = m.y[:].rearrange("p t c -> p (t c)")
    m.Qt = z[:, :2 * NI * L * GC].rearrange("p (n i r c) -> p n i r c", n=2, i=NI, r=L)
    m.xi = y[NS:NS + TS, :2 * NI * P].rearrange("p (n s) -> p n s", n=2)
    m.Kz = y[:GC].rearrange("p (g t) -> p g t", g=NG)
    x = m.x[:].rearrange("p k t -> p (k t)")
    m.ut = x[:, :L * SSM_W]
    m.Sm = x[:, :2 * HI * NCK].rearrange("p (n i k) -> p n i k", n=2, i=HI)
    m.tz = x[:, 2 * HI * NCK:2 * HI * NCK + HI * (NCK + 1)]
    ends = np.cumsum([L * SSM_W, NI * NCK // 2, SSM_W, NG * TS]).tolist()
    m.te, us, uT = (x[:, a:b] for a, b in zip(ends, ends[1:]))
    m.us = us[:TS]
    m.uT = uT[:GC].rearrange("p (g t) -> p g t", g=NG)
    n = 2 * NI * (NCK + 1)
    m.E = m.spare[:, :n].rearrange("p (n i k) -> p n i k", n=2, i=NI)
    m.U = m.spare[:, n:n + NG * NCK].rearrange("p (g k) -> p g k", g=NG)


def ssm_memory_base(sb, m):
    m.W = sb("state_to_output", [P, 2, NI, L + 1, GC])
    m.QL = sb("input_to_state_T", [P, NI, 2, P])
    m.M = sb("input_to_output", [P, NG, P])
    m.sc = sb("per_state", [P, len(NAMES), NI])
    m.pw = sb("powers", [P, 2, NI, L + 1])


def ssm_memory_build(sb, m):
    m.tb = sb("build_products", [P, NI * (L + 1) * GC])
    m.rows = sb("parameter_rows", [NI, 3, P])
    m.ldt = sb("log_dt_rows", [NI, 2])
    m.bin = sb("b_in", [P, 2, NI, GC])
    m.bb = sb("b_bar", [P, 2, NI, GC])
    m.cin = sb("c_in", [P, 2, 4, 2, NS])
    m.cs = sb("c_by_state", [P, 2, NI, GC])


def ssm_memory_run(sb, m):
    m.u2 = m.U.rearrange("p g k -> p (g k)").rearrange("p (g r c) -> p g r c", g=NG, r=L)
    m.db = sb("d_skip_on_all", [P, SSM_W])


def ssm_memory_glu(sb, m):
    m.yT = sb("y_T", [P, 4, T])
    m.wgl = sb("w_glu", [P, 4, SSM_W])
    m.bgr = sb("b_glu_rows", [4, P])
    m.bg = sb("b_glu_column", [P, 4])
    m.gl = sb("glu", [P, 2, CH])
    m.so = sb("state_out", [NI, 2, P])
    m.sos = sb("state_out_samples", [TS, 2, NI * P])


def ssm_sp(nc, sp, m, s, i, o):
    sp.dma_start(m.ut, o.u_p).then_inc(s.ut_in, 16)
    sp.dma_start(m.us, o.u_s).then_inc(s.u_load, 16)
    for n, x in enumerate((i.state_re, i.state_im)):
        sp.dma_start(m.xi[:, n, :], x).then_inc(s.u_load, 16)
    sp.dma_start(m.rows[:, 0, :], i.a_re.rearrange("(i e) s -> i (e s)", e=2)).then_inc(s.load, 16)
    sp.dma_start(m.rows[:, 1, :], i.a_im.rearrange("(i e) s -> i (e s)", e=2)).then_inc(s.load, 16)
    sp.dma_start(m.ldt[:], i.log_dt.rearrange("(i e) -> i e", e=2)).then_inc(s.load, 16)
    for n, b in enumerate((i.b_re, i.b_im)):
        sp.dma_start(m.bin[:, n], b.rearrange("(i e) s c -> (e s) i c", e=2)).then_inc(s.load, 16)
    for n, c in enumerate((i.c_re, i.c_im)):
        for d in range(2):
            sp.dma_start(m.cin[:, n, :, d, :], c.rearrange("(q g) c s -> (g c) q s", q=4)).then_inc(s.load, 16)
    sp.wait_ge(s.zero, 1)
    sp.wait_ge(s.evac, 16)
    for r in range(L):
        t0 = L - 1 - r
        sp.dma_start(m.M[GC * r:GC * (r + 1), :, GC * t0:], m.Kz[:, :, :P - GC * t0]).then_inc(s.m_in, 16)
    sp.wait_ge(s.a, 16)
    sp.dma_start(m.U.rearrange("p g k -> p (g k)"), o.u_p).then_inc(s.wg, 16)
    sp.dma_start(m.us, o.u_s).then_inc(s.wg, 16)
    sp.dma_start(m.db[:], i.d_skip.rearrange("(a n) -> a n", a=1).to_broadcast([P, SSM_W])).then_inc(s.wg, 16)
    sp.wait_ge(s.late, 1)
    sp.dma_start(m.wgl[:], i.w_glu.rearrange("(k p) n -> p k n", p=P)).then_inc(s.wg, 16)
    sp.dma_start(m.bgr[:], i.b_glu.rearrange("(k p) -> k p", p=P)).then_inc(s.wg, 16)
    sp.wait_ge(s.out, 2)
    for n in range(2):
        sp.dma_start((o.ssm_re_p, o.ssm_im_p)[n], m.so[:, n, :]).then_inc(s.kz_out, 16)
        sp.dma_start((o.ssm_re_s, o.ssm_im_s)[n], m.sos[:, n, :]).then_inc(s.kz_out, 16)
    sp.wait_ge(s.kz_out, 64)


def complex_product(tt, done, o, a, b, t1, conj_b=False):
    sr, si = (ALU.add, ALU.subtract) if conj_b else (ALU.subtract, ALU.add)
    done(tt(o[0], a[0], b[0], ALU.mult), tt(t1, a[1], b[1], ALU.mult))
    done(tt(o[0], o[0], t1, sr))
    done(tt(o[1], a[1], b[0], ALU.mult), tt(t1, a[0], b[1], ALU.mult))
    done(tt(o[1], o[1], t1, si))


def ssm_pool(nc, pool, m, s):
    G = nc.gpsimd
    G.memset(m.M[:], 0.0).then_inc(s.zero, 1)
    done = Steps(pool, s.te).done
    k = lambda n: m.sc[:, SLOT[n], :]
    E = lambda a, b: [m.E[:, q, :, a:b] for q in range(2)]
    pool.wait_ge(s.e8, 1)
    done(G.memset(m.E[:, 0, :, 0], 1.0), G.memset(m.E[:, 1, :, 0], 0.0),
         G.tensor_copy(m.E[:, 0, :, 1], k("e8r")), G.tensor_copy(m.E[:, 1, :, 1], k("e8i")))
    n = 1
    while n < NCK:
        top = [x.to_broadcast([P, NI, n]) for x in E(n, n + 1)]
        t = m.te[:, :NI * n].rearrange("p (i n) -> p i n", n=n)
        complex_product(G.tensor_tensor, done, E(n + 1, 2 * n + 1), E(1, n + 1), top, t)
        n *= 2
    pool.sem_inc(s.table, 1)


def ssm_act(nc, act, m, s):
    A = nc.scalar.activation
    k = lambda n: m.sc[:, SLOT[n], :]
    act.wait_ge(s.dve, 1)
    A(k("dt"), k("dt"), ACT.Exp).then_inc(s.a, 1)
    act.wait_ge(s.dve, 2)
    A(k("mag"), k("dtr"), ACT.Exp).then_inc(s.a, 1)
    A(k("r8"), k("dtr"), ACT.Exp, scale=float(L)).then_inc(s.a, 1)
    A(k("sin"), k("r"), ACT.Sin).then_inc(s.a, 1)
    A(k("sh"), k("r"), ACT.Sin, scale=0.5).then_inc(s.a, 1)
    for bank in range(8):
        act.wait_ge(s.ub, bank + 1)
        A(m.U[:, 4 * bank:4 * bank + 4, :].rearrange("p g t -> p (g t)"), m.ps[:, 4 + bank % 4, :],
          ACT.Copy).then_inc(s.uc, 1)
    act.wait_ge(s.u_T, 1)
    A(m.uT.rearrange("p g t -> p (g t)"), m.ps[:GC, 4, :NG * TS], ACT.Copy).then_inc(s.a, 1)
    A(m.x0[:].rearrange("p n g t -> p (n g t)"), m.ps[:, 5, :2 * NI * TS], ACT.Copy).then_inc(s.a, 1)
    n = [0]

    def evac(out, src):
        n[0] += 1
        act.wait_ge(s.pe, 1 + n[0])
        A(out, src, ACT.Copy).then_inc(s.evac, 1)

    for bank in range(8):
        evac(m.QL[:, 2 * bank:2 * bank + 2].rearrange("p i n s -> p (i n s)"), m.ps[:, bank, :])
    for bank in range(8):
        evac(m.Kz[:].rearrange("p (q i e) t -> p q e i t", q=4, e=2)[:, bank % 4, bank // 4],
             m.ps[:GC, bank, :].rearrange("p (i t) -> p i t", i=4))
    for bank in range(8):
        act.wait_ge(s.u_T, 2 + bank)
        A(m.y[:].rearrange("p t (q i e c) -> p q e i t c", q=4, i=4, e=2)[:, bank % 4, bank // 4],
          m.ps[:, bank, :].rearrange("p (g t c) -> p g t c", g=4, t=L), ACT.Copy).then_inc(s.a, 1)
    act.wait_ge(s.u_T, 10)
    A(m.ys[:].rearrange("p (i e c) -> p e i c", e=2, c=GC),
      m.ps[:TS, 0:2, :NI * GC].rearrange("p e (i c) -> p e i c", c=GC), ACT.Copy).then_inc(s.a, 1)
    act.wait_ge(s.dve, 8)
    A(m.y[:].rearrange("p t c -> p (t c)"), m.y[:].rearrange("p t c -> p (t c)"),
      ACT.Gelu_apprx_tanh).then_inc(s.a, 1)
    A(m.ys[:], m.ys[:], ACT.Gelu_apprx_tanh).then_inc(s.late, 1)
    act.wait_ge(s.late, 1)
    for h in range(8):
        j, half = h // 2, h % 2
        act.wait_ge(s.u_T, 11 + h)
        A(m.yT[:, j, :TP].rearrange("p (k t) -> p t k", t=L)[:, 4 * half:4 * half + 4, :],
          m.ps[:, h, :].rearrange("p (t k) -> p t k", t=4), ACT.Copy).then_inc(s.a, 1)
    act.wait_ge(s.u_T, 19)
    A(m.yT[:, :, TP:T], m.ps[:, 0, :4 * TS].rearrange("p (j t) -> p j t", j=4), ACT.Copy).then_inc(s.a, 1)
    A(m.bg[:], m.ps[:, 1, :4], ACT.Copy).then_inc(s.a, 1)
    A(m.so[:].rearrange("p n s -> p (n s)"), m.ps[:NI, 2, :2 * P], ACT.Copy).then_inc(s.out, 1)
    for n in range(8):
        act.wait_ge(s.u_T, 20 + n)
        A(m.sos[:, n // 4, (n % 4) * 512:(n % 4 + 1) * 512], m.ps[:TS, 3 + n % 4, :], ACT.Copy).then_inc(s.a, 1)
    act.wait_ge(s.a, 35)
    act.sem_inc(s.out, 1)
    for n in range(4 * NCH):
        j, c = divmod(n, NCH)
        act.wait_ge(s.glu, n + 1)
        if n >= 2:
            act.wait_ge(s.gate, n - 1)
        A(m.gl[:, n % 2, :], m.ps[:, n % 4, :CH], ACT.Sigmoid, bias=m.bg[:, j:j + 1]).then_inc(s.sig, 1)
        act.wait_ge(s.gate, n + 1)
        A(m.xn[:, 4 + j, 0, cols(c)], m.gl[:, n % 2, :], ACT.Copy).then_inc(s.hi, 1)


def ssm_pe(nc, pe, m, s):
    tr = nc.tensor.transpose
    mm = nc.tensor.matmul
    pe.wait_ge(s.load, 16 * 9)
    pe.wait_ge(s.c, 1)
    for n in range(3):
        tr(m.ps[:, 0, n * NI:(n + 1) * NI], m.rows[:, n, :], m.ident[:NI, :NI])
    for n in range(2):
        for q in range(4):
            x = tr(m.ps[:, 1 + n, q * P:(q + 1) * P], m.cin[:, n, q].rearrange("p d s -> p (d s)"), m.ident[:])
    x.then_inc(s.pe, 1)
    pe.wait_ge(s.ut_in, 16)
    for g in range(NG):
        bank = g // 4
        if g % 4 == 0 and bank >= 4:
            pe.wait_ge(s.uc, bank - 3)
        x = tr(m.ps[:, 4 + bank % 4, (g % 4) * P:(g % 4 + 1) * P], m.ut[:, P * g:P * (g + 1)], m.ident[:])
        if g % 4 == 3:
            x.then_inc(s.ub, 1)
    pe.wait_ge(s.u_load, 48)
    pe.wait_ge(s.uc, 6)
    for g in range(NG):
        tr(m.ps[:GC, 4, g * TS:(g + 1) * TS], m.us[:, GC * g:GC * (g + 1)], m.ident[:TS, :TS])
    for n in range(2):
        for i in range(NI):
            x = tr(m.ps[:, 5, (n * NI + i) * TS:(n * NI + i + 1) * TS], m.xi[:, n, i * P:(i + 1) * P],
                   m.ident[NS:NS + TS, NS:NS + TS])
    x.then_inc(s.u_T, 1)
    pe.wait_ge(s.a, 7)
    pe.wait_ge(s.q_built, 1)
    for i in range(NI):
        for n in range(2):
            x = tr(m.ps[:, i // 2, ((i % 2) * 2 + n) * P:((i % 2) * 2 + n + 1) * P],
                   m.Qt[:, n, i].rearrange("p r c -> p (r c)"), m.ident[:])
        if i % 2:
            x.then_inc(s.pe, 1)
    pe.wait_ge(s.dve, 3)
    for n_g in range(NG):
        bank = n_g // 4
        i, e = 4 * (bank % 4) + n_g % 4, bank // 4
        if n_g % 4 == 0:
            pe.wait_ge(s.evac, bank + 1)
        for n in range(2):
            x = mm(m.ps[:GC, bank, (n_g % 4) * P:(n_g % 4 + 1) * P], m.bb[NS * e:NS * (e + 1), n, i, :],
                   m.W[NS * e:NS * (e + 1), n, i, :L, :].rearrange("p t c -> p (t c)"), start=(n == 0), stop=(n == 1))
        if n_g % 4 == 3:
            x.then_inc(s.pe, 1)
    pe.wait_ge(s.evac, 16)
    for h in range(2):
        for n in range(2):
            for il in range(HI):
                i = h * HI + il
                for e in range(2):
                    x = mm(m.ps[NS * e:NS * (e + 1), 4 * h + 2 * n + il // 4, (il % 4) * P:(il % 4 + 1) * P],
                           m.QL[:, i, n, NS * e:NS * (e + 1)], m.U[:, 2 * i + e, :], start=True, stop=True)
        x.then_inc(s.pe, 1)
    pe.wait_ge(s.dve, 5)
    for n in range(2):
        for i in range(NI):
            for e in range(2):
                x = mm(m.ps[NS * e:NS * (e + 1), 0, (n * NI + i) * TS:(n * NI + i + 1) * TS],
                       m.QL[:GC, i, n, NS * e:NS * (e + 1)], m.uT[:, 2 * i + e, :], start=True, stop=True)
    x.then_inc(s.pe, 1)
    pe.wait_ge(s.dve, 7)
    pe.wait_ge(s.m_in, 16 * L)
    for n_g in range(NG):
        bank = n_g // 4
        i, e = 4 * (bank % 4) + n_g % 4, bank // 4
        g = 2 * i + e
        out = m.ps[:, bank, (n_g % 4) * P:(n_g % 4 + 1) * P]
        mm(out, m.U[:, g, :], m.M[:, g, :], start=True, stop=False)
        for n in range(2):
            x = mm(out, m.Z[NS * e:NS * (e + 1), n, i, :NCK],
                   m.W[NS * e:NS * (e + 1), n, i, 1:, :].rearrange("p t c -> p (t c)"), start=False, stop=(n == 1))
        if n_g % 4 == 3:
            x.then_inc(s.u_T, 1)
    pe.wait_ge(s.a, 9)
    for g in range(NG):
        i, e = divmod(g, 2)
        for n in range(2):
            x = mm(m.ps[:TS, e, i * GC:(i + 1) * GC], m.xs[NS * e:NS * (e + 1), n, i, :],
                   m.W[NS * e:NS * (e + 1), n, i, 0, :], start=(n == 0), stop=(n == 1))
    x.then_inc(s.u_T, 1)
    pe.wait_ge(s.late, 1)
    for h in range(8):
        j, half = h // 2, h % 2
        for t in range(4):
            x = tr(m.ps[:, h, t * P:(t + 1) * P], m.y[:, 4 * half + t, j * P:(j + 1) * P], m.ident[:])
        x.then_inc(s.u_T, 1)
    pe.wait_ge(s.a, 22)
    pe.wait_ge(s.wg, 16 * 5)
    for j in range(4):
        tr(m.ps[:, 0, j * TS:(j + 1) * TS], m.ys[:, j * P:(j + 1) * P], m.ident[:TS, :TS])
    tr(m.ps[:, 1, :4], m.bgr[:], m.ident[:4, :4])
    for n in range(2):
        x = tr(m.ps[:NI, 2, n * P:(n + 1) * P], m.Z[:, n, :, NCK], m.ident[:])
    x.then_inc(s.u_T, 1)
    for n in range(8):
        if n < 4:
            pe.wait_ge(s.a, 22 + n)
        else:
            pe.wait_ge(s.a, 28 + n - 4)
        for q in range(4):
            i = (n % 4) * 4 + q
            x = tr(m.ps[:TS, 3 + n % 4, q * P:(q + 1) * P], m.xs[:, n // 4, i, :], m.ident[:])
        x.then_inc(s.u_T, 1)
    pe.wait_ge(s.a, 33)
    for n in range(4 * NCH):
        j, c = divmod(n, NCH)
        if n >= 4:
            pe.wait_ge(s.sig, n - 3)
        for k in range(4):
            x = mm(m.ps[:, n % 4, :CH], m.wgl[:, k, j * P:(j + 1) * P], m.yT[:, k, cols(c)],
                   start=(k == 0), stop=(k == 3))
        x.then_inc(s.glu, 1)


def ssm_dve(nc, dve, m, s):
    V = nc.vector
    cnt = [0]

    def done(*ins):
        for x in ins:
            x.then_inc(s.c, 1)
        cnt[0] += len(ins)
        dve.wait_ge(s.c, cnt[0])

    def tt(o, a, b, op):
        return V.tensor_tensor(o, a, b, op)

    def cmul(o, a, b, t1, t2=None, conj_b=False, negate_im=False):
        sr, si = (ALU.add, ALU.subtract) if conj_b else (ALU.subtract, ALU.add)
        if t2 is None:
            done(tt(o[0], a[0], b[0], ALU.mult), tt(t1, a[1], b[1], ALU.mult))
            done(tt(o[0], o[0], t1, sr))
            done(tt(o[1], a[1], b[0], ALU.mult), tt(t1, a[0], b[1], ALU.mult))
            done(tt(o[1], o[1], t1, si))
        else:
            done(tt(o[0], a[0], b[0], ALU.mult), tt(t1, a[1], b[1], ALU.mult),
                 tt(o[1], a[1], b[0], ALU.mult), tt(t2, a[0], b[1], ALU.mult))
            done(tt(o[0], o[0], t1, sr), tt(o[1], o[1], t2, si))

    k = lambda n: m.sc[:, SLOT[n], :]
    dve.wait_ge(s.load, 16 * 9)
    done(V.tensor_copy(m.rows[:, 2, :].rearrange("p (e s) -> p e s", e=2),
                       m.ldt[:, :, None].to_broadcast([NI, 2, NS])))
    dve.wait_ge(s.pe, 1)
    pr = lambda n: m.ps[:, 0, n * NI:(n + 1) * NI]
    done(V.tensor_copy(k("ar"), pr(0)), V.tensor_copy(k("ai"), pr(1)))
    V.tensor_copy(k("dt"), pr(2)).then_inc(s.dve, 1)
    for n in range(2):
        for e in range(2):
            r = slice(NS * e, NS * (e + 1))
            done(V.tensor_copy(m.cs[r, n].rearrange("p (q g) c -> p q g c", q=4),
                               m.ps[r, 1 + n, :].rearrange("p (q g e c) -> p q g e c", q=4, g=4, e=2)[:, :, :, e, :]))
    dve.wait_ge(s.a, 1)
    done(tt(k("dtr"), k("dt"), k("ar"), ALU.mult), tt(k("dti"), k("dt"), k("ai"), ALU.mult))
    done(V.tensor_scalar(k("n"), k("dti"), float(1 / (2 * np.pi)), MAGIC, ALU.mult, ALU.add))
    done(V.tensor_scalar(k("n"), k("n"), -MAGIC, None, ALU.add))
    src = k("dti")
    for part in TWO_PI:
        done(V.scalar_tensor_tensor(out=k("r"), in0=k("n"), scalar=-part, in1=src, op0=ALU.mult, op1=ALU.add))
        src = k("r")
    V.tensor_scalar(k("r"), k("r"), 3.1415925, -3.1415925, ALU.min, ALU.max).then_inc(s.dve, 1)
    dve.wait_ge(s.a, 5)
    done(tt(k("t1"), k("sh"), k("sh"), ALU.mult))
    done(V.tensor_scalar(k("er"), k("t1"), -2.0, 1.0, ALU.mult, ALU.add), V.tensor_copy(k("ei"), k("sin")))
    done(tt(k("abr"), k("mag"), k("er"), ALU.mult), tt(k("abi"), k("mag"), k("ei"), ALU.mult))
    cmul((k("u1"), k("u2")), (k("er"), k("ei")), (k("er"), k("ei")), k("t1"), k("t2"))
    cmul((k("e8r"), k("e8i")), (k("u1"), k("u2")), (k("u1"), k("u2")), k("t1"), k("t2"))
    cmul((k("u1"), k("u2")), (k("e8r"), k("e8i")), (k("e8r"), k("e8i")), k("t1"), k("t2"))
    done(V.tensor_copy(k("e8r"), k("u1")), V.tensor_copy(k("e8i"), k("u2")))
    dve.sem_inc(s.e8, 1)
    done(V.memset(m.pw[:, 0, :, 0], 1.0), V.memset(m.pw[:, 1, :, 0], 0.0),
         V.tensor_copy(m.pw[:, 0, :, 1], k("abr")), V.tensor_copy(m.pw[:, 1, :, 1], k("abi")))
    n = 1
    while n < L:
        pw = lambda a, b: [m.pw[:, q, :, a:b] for q in range(2)]
        top = [x.to_broadcast([P, NI, n]) for x in pw(n, n + 1)]
        t = [m.tb[:, q * NI * n:(q + 1) * NI * n].rearrange("p (i n) -> p i n", n=n) for q in range(2)]
        cmul(pw(n + 1, 2 * n + 1), pw(1, n + 1), top, *t)
        n *= 2
    done(tt(k("t1"), k("ar"), k("ar"), ALU.mult), tt(k("t2"), k("ai"), k("ai"), ALU.mult),
         V.tensor_scalar(k("nr"), k("abr"), -1.0, None, ALU.add))
    done(tt(k("den"), k("t1"), k("t2"), ALU.add))
    cmul((k("fr"), k("fi")), (k("nr"), k("abi")), (k("ar"), k("ai")), k("t1"), k("t2"), conj_b=True)
    done(V.reciprocal(k("u1"), k("den")))
    done(tt(k("fr"), k("fr"), k("u1"), ALU.mult), tt(k("fi"), k("fi"), k("u1"), ALU.mult))
    f = [k(q)[:, :, None].to_broadcast([P, NI, GC]) for q in ("fr", "fi")]
    t = m.tb[:, :NI * GC].rearrange("p (i c) -> p i c", i=NI)
    cmul((m.bb[:, 0], m.bb[:, 1]), (m.bin[:, 0], m.bin[:, 1]), f, t)
    sh = [P, NI, L, GC]
    t = m.tb[:, :NI * L * GC].rearrange("p (i r c) -> p i r c", i=NI, r=L)
    bbx = [m.bb[:, q, :, None, :].to_broadcast(sh) for q in range(2)]
    pwx = [m.pw[:, q, :, :L, None].to_broadcast(sh) for q in range(2)]
    cmul((m.Qt[:, 0], m.Qt[:, 1]), bbx, pwx, t)
    dve.sem_inc(s.q_built, 1)
    sh = [P, NI, L + 1, GC]
    t = m.tb[:].rearrange("p (i r c) -> p i r c", i=NI, r=L + 1)
    cx = [m.cs[:, q, :, None, :].to_broadcast(sh) for q in range(2)]
    pwx = [m.pw[:, q, :, :, None].to_broadcast(sh) for q in range(2)]
    cmul((m.W[:, 0], m.W[:, 1]), cx, pwx, t)
    V.tensor_scalar(m.W[:, 1].rearrange("p i t c -> p (i t c)"), m.W[:, 1].rearrange("p i t c -> p (i t c)"),
                    -1.0, None, ALU.mult).then_inc(s.dve, 1)
    dve.wait_ge(s.pe, 17)
    dve.wait_ge(s.u_T, 1)
    V.memset(m.Z[:, :, :, 0], 0.0).then_inc(s.dve, 1)
    dve.wait_ge(s.dve, 4)
    for h in range(2):
        il = slice(h * HI, (h + 1) * HI)
        E = lambda a, b: [m.E[:, q, il, a:b] for q in range(2)]
        if h == 0:
            dve.wait_ge(s.table, 1)
        dve.wait_ge(s.pe, 18 + h)
        S = [m.ps[:, 4 * h + 2 * q:4 * h + 2 * q + 2, :].rearrange("p a (i n) -> p (a i) n", n=NCK) for q in range(2)]
        t = m.tz[:, :HI * NCK].rearrange("p (i n) -> p i n", n=NCK)
        cmul([m.Sm[:, q] for q in range(2)], S, E(1, NCK + 1), t, conj_b=True)
        done(*[V.tensor_tensor_scan(out=m.Z[:, q, h * HI + j, 1:], data0=k("r8")[:, h * HI + j:h * HI + j + 1]
                                    .to_broadcast([P, NCK]), data1=m.Sm[:, q, j, :], initial=0.0,
                                    op0=ALU.mult, op1=ALU.add) for j in range(HI) for q in range(2)])
        Zh = [m.Z[:, q, il, :] for q in range(2)]
        Ef = E(0, NCK + 1)
        t = m.tz[:].rearrange("p (i n) -> p i n", n=NCK + 1)
        t2 = m.Sm[:].rearrange("p q i n -> p (q i n)")[:, :HI * (NCK + 1)].rearrange("p (i n) -> p i n", n=NCK + 1)
        done(tt(t, Zh[1], Ef[1], ALU.mult), tt(t2, Zh[0], Ef[1], ALU.mult))
        done(tt(Zh[0], Zh[0], Ef[0], ALU.mult), tt(Zh[1], Zh[1], Ef[0], ALU.mult))
        done(tt(Zh[0], Zh[0], t, ALU.subtract), tt(Zh[1], Zh[1], t2, ALU.add))
        dve.sem_inc(s.dve, 1)
    dve.wait_ge(s.pe, 20)
    a = [k(q)[:, :, None].to_broadcast([P, NI, TS]) for q in ("abr", "abi")]
    t = m.tz[:, :NI * TS].rearrange("p (i n) -> p i n", n=TS)
    cmul([m.xs[:, q] for q in range(2)], [m.x0[:, q] for q in range(2)], a, t)
    bx = m.ps[:, 0, :2 * NI * TS].rearrange("p (q i n) -> p q i n", q=2, n=TS)
    done(tt(m.xs[:], m.xs[:], bx, ALU.add))
    dve.sem_inc(s.dve, 1)
    dve.wait_ge(s.wg, 48)
    byg = lambda x: x.rearrange("p (g c) -> p g c", g=NG)
    done(tt(m.u2, m.u2, byg(m.db[:])[:, :, None, :].to_broadcast([P, NG, L, GC]), ALU.mult),
         tt(m.us, m.us, m.db[:TS, :], ALU.mult))
    dve.wait_ge(s.a, 16)
    done(*[tt(byg(m.y[:, t, :]), byg(m.y[:, t, :]), m.u2[:, :, L - 1 - t, :], ALU.add) for t in range(L)],
         tt(m.ys[:], m.ys[:], m.us, ALU.add))
    dve.sem_inc(s.dve, 1)
    for n in range(4 * NCH):
        j, c = divmod(n, NCH)
        dve.wait_ge(s.sig, n + 1)
        tt(m.gl[:, n % 2, :], m.gl[:, n % 2, :], m.yT[:, j, cols(c)], ALU.mult).then_inc(s.gate, 1)
        dve.wait_ge(s.hi, n + 1)
        done(tt(m.xn[:, 4 + j, 1, cols(c)], m.gl[:, n % 2, :], m.xn[:, 4 + j, 0, cols(c)].bitcast(F32), ALU.subtract))
OUT_SEMS = ("raw0", "raw1", "gates0", "gates1", "hi", "lo", "a", "b", "prod", "sum", "mhi", "mlo",
            "draw0", "draw1", "dhi", "dlo", "down", "acc")
ORDER = (0, 1, 2, 3, "d0", 4, 5, "d1", 6, 7, "d2", "d3")


def out_memory(sb, m):
    m.wh = sb("branch_weights_split", [P, 2, 2, KD * P], F32R)
    m.wr = sb("branch_weights_raw", [P, 2, KD * P])
    m.hh = sb("merged_split", [P, 4, 2, T], F32R)
    m.dh = sb("out_weights_split", [P, 2, 2, D], F32R)
    m.dr = sb("out_weights_raw", [P, 2, D])
    m.gt = sb("gates", [P, 2, 2, CH * NCH])
    m.mg = sb("merged", [P, 2, 2, CH])


def out_sp(nc, sp, m, s, i, o, x_back):
    for t in ORDER:
        if t == 2:
            x_back()
        if isinstance(t, int):
            e = t % 2
            if t >= 2:
                sp.wait_ge(s.lo, t - 1)
            for n, w in enumerate((i.w_pa, i.w_pb)):
                sp.dma_start(m.wr[:, e, n * 4 * P:(n + 1) * 4 * P].rearrange("p (k n) -> p k n", k=4),
                             w.rearrange("(k p) n -> p k n", p=P)[:, :, t * P:(t + 1) * P]).then_inc((s.raw0, s.raw1)[e], 16)
            if t >= 2:
                sp.wait_ge(s.sum, NCH * (t - 1))
            for n in range(2):
                sp.dma_start(m.gt[:, e, n, :], o.gates[(n * KD + t) * P:(n * KD + t + 1) * P, :]).then_inc((s.gates0, s.gates1)[e], 16)
        else:
            p = int(t[1])
            for e in range(2):
                if p:
                    sp.wait_ge(s.dlo, 2 * p + e - 1)
                sp.dma_start(m.dr[:, e, :], i.w_out[(2 * p + e) * P:(2 * p + e + 1) * P, :]).then_inc((s.draw0, s.draw1)[e], 16)


def out_act(nc, act, m, s):
    def split(t):
        e = t % 2
        act.wait_ge((s.raw0, s.raw1)[e], 32 * (t // 2 + 1))
        if t >= 2:
            act.wait_ge(s.b, NCH * (t - 1))
        nc.scalar.activation(m.wh[:, e, 0, :], m.wr[:, e, :], ACT.Copy).then_inc(s.hi, 1)

    split(0)
    for t in ORDER:
        if isinstance(t, int):
            if t + 1 < KD:
                split(t + 1)
            for c in range(NCH):
                n = NCH * t + c
                act.wait_ge(s.sum, n + 1)
                nc.scalar.activation(m.hh[:, t % 4, 0, cols(c)], m.mg[:, n % 2, 0, :], ACT.Copy).then_inc(s.mhi, 1)
        else:
            p = int(t[1])
            for e in range(2):
                act.wait_ge((s.draw0, s.draw1)[e], 16 * (p + 1))
                if p:
                    act.wait_ge(s.down, NCH * KD * p)
                nc.scalar.activation(m.dh[:, e, 0, :], m.dr[:, e, :], ACT.Copy).then_inc(s.dhi, 1)


def out_pool(nc, pool, m, s):
    def split(t):
        pool.wait_ge(s.hi, t + 1)
        nc.gpsimd.tensor_tensor(m.wh[:, t % 2, 1, :], m.wr[:, t % 2, :], m.wh[:, t % 2, 0, :].bitcast(F32),
                                ALU.subtract).then_inc(s.lo, 1)

    split(0)
    for t in ORDER:
        if isinstance(t, int):
            if t + 1 < KD:
                split(t + 1)
            for c in range(NCH):
                n = NCH * t + c
                pool.wait_ge(s.mhi, n + 1)
                nc.gpsimd.tensor_tensor(m.hh[:, t % 4, 1, cols(c)], m.mg[:, n % 2, 0, :],
                                        m.hh[:, t % 4, 0, cols(c)].bitcast(F32), ALU.subtract).then_inc(s.mlo, 1)
        else:
            p = int(t[1])
            for e in range(2):
                pool.wait_ge(s.dhi, 2 * p + e + 1)
                nc.gpsimd.tensor_tensor(m.dh[:, e, 1, :], m.dr[:, e, :], m.dh[:, e, 0, :].bitcast(F32),
                                        ALU.subtract).then_inc(s.dlo, 1)


def out_pe(nc, pe, m, s):
    for t in ORDER:
        if isinstance(t, int):
            pe.wait_ge(s.lo, t + 1)
            for c in range(NCH):
                if t:
                    pe.wait_ge(s.prod, NCH * (t - 1) + c + 1)
                for half, done in ((0, s.a), (1, s.b)):
                    for k in range(4 * half, 4 * half + 4):
                        for n, (a, b) in enumerate(PASSES):
                            mm = nc.tensor.matmul(m.ps[:, NCH * half + c, :CH], m.wh[:, t % 2, a, k * P:(k + 1) * P],
                                                  m.xn[:, k, b, cols(c)], start=(k % 4 == 0 and n == 0),
                                                  stop=(k % 4 == 3 and n == 2))
                    mm.then_inc(done, 1)
        else:
            p = int(t[1])
            pe.wait_ge(s.mlo, NCH * (2 * p + 2))
            pe.wait_ge(s.dlo, 2 * p + 2)
            for n in range(NCH * KD):
                o, c = divmod(n, NCH)
                if p or n >= 2:
                    pe.wait_ge(s.acc, NCH * KD * p + n - 1)
                for e in range(2):
                    for q, (a, b) in enumerate(PASSES):
                        mm = nc.tensor.matmul(m.ps[:, 6 + n % 2, :CH], m.dh[:, e, a, o * P:(o + 1) * P],
                                              m.hh[:, (2 * p + e) % 4, b, cols(c)], start=(e == 0 and q == 0),
                                              stop=(e == 1 and q == 2))
                mm.then_inc(s.down, 1)


def out_dve(nc, dve, m, s, s_io):
    for t in ORDER:
        if isinstance(t, int):
            dve.wait_ge((s.gates0, s.gates1)[t % 2], 32 * (t // 2 + 1))
            for c in range(NCH):
                n = NCH * t + c
                dve.wait_ge(s.b, n + 1)
                if n >= 2:
                    dve.wait_ge(s.mlo, n - 1)
                mg = [m.mg[:, n % 2, h, :] for h in range(2)]
                nc.vector.tensor_tensor(mg[0], m.gt[:, t % 2, 0, cols(c)], m.ps[:, c, :CH], ALU.mult)
                nc.vector.tensor_tensor(mg[1], m.gt[:, t % 2, 1, cols(c)], m.ps[:, NCH + c, :CH],
                                        ALU.mult).then_inc(s.prod, 1)
                dve.wait_ge(s.prod, n + 1)
                nc.vector.tensor_tensor(mg[0], mg[0], mg[1], ALU.add).then_inc(s.sum, 1)
        else:
            p = int(t[1])
            dve.wait_ge(s_io.x_back, 16)
            for n in range(NCH * KD):
                o, c = divmod(n, NCH)
                dve.wait_ge(s.down, NCH * KD * p + n + 1)
                xs = m.x[:, o, cols(c)]
                nc.vector.tensor_tensor(xs, xs, m.ps[:, 6 + n % 2, :CH], ALU.add).then_inc(s.acc, 1)


IO_SEMS = ("x_in0", "x_in1", "turned", "kept", "gain_in", "gain_T", "gains", "const", "sq", "sum", "var", "std",
           "rs", "y", "back", "staged", "y_out0", "y_out1", "phase", "leave", "x_away", "x_back",
           "ki_in", "table", "iota", "steps")


def in_sp(nc, sp, m, s, i):
    for n, g in enumerate(i.gains):
        sp.dma_start(m.grow[KD * n:KD * (n + 1), :], g.rearrange("(k p) -> k p", p=P)).then_inc(s.gain_in, 16)
    for b in range(NB + 1):
        rows = P if b < NB else TS
        if b >= 2:
            sp.wait_ge(s.turned, 2 * (b - 1))
        src = i.x_prompt[b * P:(b + 1) * P, :] if b < NB else i.x_sample
        sp.dma_start(m.xin[:rows, b % 2, :], src).then_inc((s.x_in0, s.x_in1)[b % 2], 16)


def in_pe(nc, pe, m, s):
    pe.wait_ge(s.const, 5)
    pe.wait_ge(s.gain_in, 16 * 4)
    nc.tensor.transpose(m.ps[:, 7, :4 * KD], m.grow[:], m.ident[:4 * KD, :4 * KD]).then_inc(s.gain_T, 1)
    for b in range(NB + 1):
        rows = P if b < NB else TS
        pe.wait_ge((s.x_in0, s.x_in1)[b % 2], 16 * (b // 2 + 1))
        for h in range(2):
            n = 2 * b + h
            if n >= 4:
                pe.wait_ge(s.kept, n - 3)
            for q in range(4):
                k = 4 * h + q
                mm = nc.tensor.transpose(m.ps[:, n % 4, q * P:q * P + rows], m.xin[:rows, b % 2, k * P:(k + 1) * P],
                                         m.ident[:rows, :rows])
            mm.then_inc(s.turned, 1)


def in_act(nc, act, m, s):
    act.wait_ge(s.gain_T, 1)
    nc.scalar.activation(m.gains[:], m.ps[:, 7, :4 * KD], ACT.Copy).then_inc(s.gains, 1)
    for b in range(NB + 1):
        rows = P if b < NB else TS
        for h in range(2):
            n = 2 * b + h
            act.wait_ge(s.turned, n + 1)
            nc.scalar.activation(m.x[:, 4 * h:4 * h + 4, b * P:b * P + rows],
                                 m.ps[:, n % 4, :].rearrange("p (q t) -> p q t", q=4)[:, :, :rows],
                                 ACT.Copy).then_inc(s.kept, 1)
    act.wait_ge(s.kept, 2 * NB + 2)


def fin_memory(sb, m):
    m.sg = sb("final_squares", [P, NCH, CH])
    m.rstd = sb("final_rstd", [P, 3, CH])
    m.yn = sb("final_normed", [P, KD, T])
    m.yo = sb("final_rows", [P, 2, D])


def fin_act(nc, act, m, s, o):
    def squares(c):
        for k in range(KD):
            n = c * KD + k
            if n >= 3:
                act.wait_ge(s.sum, n - 2)
            nc.scalar.activation(m.sg[:, n % 3, :], m.x[:, k, cols(c)], ACT.Square).then_inc(s.sq, 1)

    squares(0)
    for c in range(NCH):
        if c + 1 < NCH:
            squares(c + 1)
        act.wait_ge(s.var, c + 1)
        nc.scalar.activation(m.rstd[:, 1, :], m.rstd[:, 0, :], ACT.Sqrt).then_inc(s.std, 1)
    for b in range(NB + 1):
        rows = P if b < NB else TS
        if b >= 2:
            act.wait_ge((s.y_out0, s.y_out1)[b % 2], 16 * (b // 2))
        for h in range(2):
            act.wait_ge(s.back, 2 * b + h + 1)
            nc.scalar.activation(m.yo[:rows, b % 2, h * 512:(h + 1) * 512], m.ps[:rows, (2 * b + h) % 4, :],
                                 ACT.Copy).then_inc(s.staged, 1)


def fin_pe(nc, pe, m, s):
    for n in range(NCH * KD):
        c, k = divmod(n, KD)
        if c == 2 and k == 0:
            pe.wait_ge(s.var, 1)
        pe.wait_ge(s.sq, n + 1)
        nc.tensor.matmul(m.ps[:, 4 + c % 2, :CH], m.ones[:], m.sg[:, n % 3, :],
                         start=(k == 0), stop=(k == KD - 1)).then_inc(s.sum, 1)
    for b in range(NB + 1):
        rows = P if b < NB else TS
        pe.wait_ge(s.y, KD * ((b * P + rows - 1) // CH + 1))
        for h in range(2):
            n = 2 * b + h
            if n >= 4:
                pe.wait_ge(s.staged, n - 3)
            for q in range(4):
                mm = nc.tensor.transpose(m.ps[:rows, n % 4, q * P:(q + 1) * P],
                                         m.yn[:, 4 * h + q, b * P:b * P + rows], m.ident[:])
            mm.then_inc(s.back, 1)


def fin_dve(nc, dve, m, s):
    for c in range(NCH):
        dve.wait_ge(s.sum, KD * (c + 1))
        nc.vector.tensor_scalar(m.rstd[:, 0, :], m.ps[:, 4 + c % 2, :CH], 1.0 / D, EPS, ALU.mult, ALU.add).then_inc(s.var, 1)
        dve.wait_ge(s.std, c + 1)
        nc.vector.reciprocal(m.rstd[:, 2, :], m.rstd[:, 1, :]).then_inc(s.rs, 1)
        dve.wait_ge(s.rs, c + 1)
        for k in range(KD):
            nc.vector.scalar_tensor_tensor(out=m.yn[:, k, cols(c)], in0=m.x[:, k, cols(c)],
                                           scalar=m.gains[:, 3 * KD + k:3 * KD + k + 1], in1=m.rstd[:, 2, :],
                                           op0=ALU.mult, op1=ALU.mult).then_inc(s.y, 1)


def fin_sp(nc, sp, m, s, i, o):
    for b in range(NB + 1):
        rows = P if b < NB else TS
        sp.wait_ge(s.staged, 2 * b + 2)
        dst = o.y_prompt[b * P:(b + 1) * P, :] if b < NB else o.y_sample
        sp.dma_start(dst, m.yo[:rows, b % 2, :]).then_inc((s.y_out0, s.y_out1)[b % 2], 16)
    sp.wait_ge(s.y_out0, 16 * 5)
    sp.wait_ge(s.y_out1, 16 * 4)


OUTS = (("y_prompt", (1, TP, D)), ("y_sample", (TS, 1, D)),
        ("k_prompt", (1, 1, TP, N_HEADS, HD)), ("v_prompt", (1, 1, TP, N_HEADS, HD)), ("kidx_prompt", (1, 1, TP, IDX)),
        ("ssm_re_prompt", (1, 1, NG, NS)), ("ssm_im_prompt", (1, 1, NG, NS)),
        ("k_sample", (1, TS, 1, N_HEADS, HD)), ("v_sample", (1, TS, 1, N_HEADS, HD)), ("kidx_sample", (1, TS, 1, IDX)),
        ("ssm_re_sample", (1, TS, NG, NS)), ("ssm_im_sample", (1, TS, NG, NS)))
INS = ("x_prompt", "x_sample", "cache_k", "cache_v", "cache_kidx", "state_ssm_re", "state_ssm_im", "page_table",
       "g_ffn1", "w1_gate", "w1_up", "w1_down", "g_mix", "w_in", "a_re", "a_im", "log_dt", "b_re", "b_im",
       "c_re", "c_im", "d_skip", "w_glu", "b_glu", "w_pa", "w_pb", "w_out", "g_ffn2", "w2_gate", "w2_up",
       "w2_down", "g_final")


def build_layer(nc, i, o):
    with ExitStack() as stack:
        def sem(name):
            return stack.enter_context(nc.semaphore(name))

        def sems(prefix, names):
            return record("Sems", {n: sem(f"{prefix}_{n}") for n in names})

        def scope(*makers):
            inner = ExitStack()
            for make in makers:
                make(lambda name, shape, dt=F32: inner.enter_context(nc.sbuf_tensor(name, shape, dt)))
            return inner

        def space():
            m = Space()
            m.x, m.xn, m.spare, m.ident, m.ones, m.gains, m.pages, m.ps = (
                base.x, base.xn, base.spare, base.ident, base.ones, base.gains, base.pages, base.ps)
            return m

        base = Space()

        def spare_memory(sb):
            sb("first_half", [P, KD * T])
            base.spare = sb("samples_attention", [P, KD * T])

        def persistent(sb):
            base.x = sb("x_T", [P, KD, T])
            scope(spare_memory).close()
            base.xn = sb("normed_split", [P, KD, 2, T], F32R)
            base.ident = sb("identity", [P, P])
            base.ones = sb("ones", [P, P])
            base.gains = sb("gains", [P, 4 * KD])
            base.pages = sb("page_rows", [P, TS], I32)
            base.row_in_page = sb("row_in_page", [P, 1], I32)

        base.ps = stack.enter_context(nc.psum_tensor("ps", [P, 8, 512], F32))
        stack.enter_context(scope(persistent))

        m_in = space()

        def in_memory(sb):
            m_in.xin = sb("x_rows", [P, 2, D])
            m_in.grow = sb("gain_rows", [4 * KD, P])
        scope(in_memory).close()
        m_f1, m_f2, m_mix, m_out, m_fin = (space() for _ in range(5))
        scope(lambda sb: ffn_memory(sb, m_f1, "f1")).close()

        with scope(lambda sb: mix_memory(sb, m_mix), lambda sb: sel_memory(sb, m_mix),
                   lambda sb: smp_memory(sb, m_mix)):
            m_mix.sg, m_mix.hf, m_mix.rstd = (
                m_mix.score[:, n * NCH * CH:(n + 1) * NCH * CH].rearrange("p (n t) -> p n t", n=NCH) for n in range(3))
            scope(lambda sb: proj_memory(sb, m_mix)).close()
            scope(lambda sb: att_memory(sb, m_mix)).close()
        smp_views(m_mix)
        m_ssm = space()
        with scope(lambda sb: ssm_memory_keep(sb, m_ssm)):
            with scope(lambda sb: ssm_memory_base(sb, m_ssm)):
                scope(lambda sb: ssm_memory_build(sb, m_ssm)).close()
                scope(lambda sb: ssm_memory_run(sb, m_ssm)).close()
            scope(lambda sb: ssm_memory_glu(sb, m_ssm)).close()
        scope(lambda sb: out_memory(sb, m_out)).close()
        scope(lambda sb: ffn_memory(sb, m_f2, "f2")).close()
        scope(lambda sb: fin_memory(sb, m_fin)).close()

        s_io = sems("io", IO_SEMS)
        s_ffn = ffn_sems(sem, "ffn")
        s_mix = sems("mix", MIX_SEMS)
        s_att = sems("att", ATT_SEMS)
        s_smp = sems("smp", SMP_SEMS)
        s_ssm = sems("ssm", SSM_SEMS)
        s_out = sems("out", OUT_SEMS)
        s_f1, s_nm, s_f2 = after_uses(s_ffn, 0, 0), after_uses(s_ffn, 1, 1), after_uses(s_ffn, 2, 1)

        def barrier(engine, n):
            engine.drain().then_inc(s_io.phase, 1)
            engine.wait_ge(s_io.phase, 5 * n)

        gain = lambda n: base.gains[:, n * KD:(n + 1) * KD]
        block = stack.enter_context(nc.Block())

        @block.sync
        def _(sp):
            in_sp(nc, sp, m_in, s_io, i)
            rows = PAGE // PER_ROW
            for j in range(N_PAGES):
                sp.dma_start(base.pages[rows * j:rows * (j + 1), :],
                             i.page_table[:, j:j + 1].rearrange("b a -> a b").to_broadcast([rows, TS]),
                             allow_slow_non_contiguous=True).then_inc(s_io.table, 16)
            barrier(sp, 1)
            ffn_sp(nc, sp, m_f1, s_f1, i.w1_gate, i.w1_up, i.w1_down)
            barrier(sp, 2)
            barrier(sp, 3)
            proj_sp(nc, sp, m_mix, s_mix, i.w_in, o, lambda: sp.dma_start(
                o.x_away, base.x[:].rearrange("p k t -> p (k t)")).then_inc(s_io.x_away, 16))
            barrier(sp, 4)
            sp.dma_start(m_mix.v[:], o.token_major["v"][0]).then_inc(s_att.v_in, 16)
            smp_sp(nc, sp, m_mix, s_smp, i, o)
            barrier(sp, 5)
            ssm_sp(nc, sp, m_ssm, s_ssm, i, o)
            barrier(sp, 6)
            out_sp(nc, sp, m_out, s_out, i, o, lambda: sp.dma_start(
                base.x[:].rearrange("p k t -> p (k t)"), o.x_away).then_inc(s_io.x_back, 16))
            barrier(sp, 7)
            ffn_sp(nc, sp, m_f2, s_f2, i.w2_gate, i.w2_up, i.w2_down)
            barrier(sp, 8)
            fin_sp(nc, sp, m_fin, s_io, i, o)

        @block.scalar
        def _(act):
            in_act(nc, act, m_in, s_io)
            barrier(act, 1)
            norm_act(nc, act, m_f1, s_f1, lambda: [
                ffn_act_split(nc, act, m_f1, s_f1, 0, 0, half, False) for half in range(2)])
            ffn_act(nc, act, m_f1, s_f1)
            barrier(act, 2)
            barrier(act, 3)
            norm_act(nc, act, m_mix, s_nm, lambda: proj_act_split(nc, act, m_mix, s_mix, 0, 0, IDX + IDX_HEADS))
            proj_act(nc, act, m_mix, s_mix, s_io, o)
            barrier(act, 4)
            att_act(nc, act, m_mix, s_att, smp_act(nc, act, m_mix, s_smp))
            barrier(act, 5)
            ssm_act(nc, act, m_ssm, s_ssm)
            barrier(act, 6)
            out_act(nc, act, m_out, s_out)
            barrier(act, 7)
            norm_act(nc, act, m_f2, s_f2, lambda: [
                ffn_act_split(nc, act, m_f2, s_f2, 0, 0, half, False) for half in range(2)])
            ffn_act(nc, act, m_f2, s_f2)
            barrier(act, 8)
            fin_act(nc, act, m_fin, s_io, o)

        @block.vector
        def _(dve):
            nc.vector.memset(base.ones[:], 1.0).then_inc(s_io.const, 1)
            rows = PAGE // PER_ROW
            dve.wait_ge(s_io.table, 16 * N_PAGES)
            dve.wait_ge(s_io.iota, 1)
            steps = Steps(dve, s_io.steps)
            steps.done(nc.vector.tensor_scalar(base.row_in_page[:], base.row_in_page[:], rows - 1, None, ALU.bitwise_and),
                       nc.vector.tensor_scalar(base.pages[:], base.pages[:], rows.bit_length() - 1, None,
                                               ALU.logical_shift_left))
            steps.done(nc.vector.tensor_tensor(base.pages[:], base.pages[:], base.row_in_page[:].to_broadcast([P, TS]),
                                               ALU.bitwise_or))
            barrier(dve, 1)
            norm_dve(nc, dve, m_f1, s_f1, gain(0))
            ffn_dve(nc, dve, m_f1, s_f1)
            barrier(dve, 2)
            barrier(dve, 3)
            norm_dve(nc, dve, m_mix, s_nm, gain(1))
            select_dve(nc, dve, m_mix, s_mix, s_io)
            barrier(dve, 4)
            att_dve(nc, dve, m_mix, s_att, smp_dve(nc, dve, m_mix, s_smp))
            barrier(dve, 5)
            ssm_dve(nc, dve, m_ssm, s_ssm)
            barrier(dve, 6)
            out_dve(nc, dve, m_out, s_out, s_io)
            barrier(dve, 7)
            norm_dve(nc, dve, m_f2, s_f2, gain(2))
            ffn_dve(nc, dve, m_f2, s_f2)
            barrier(dve, 8)
            fin_dve(nc, dve, m_fin, s_io)

        @block.gpsimd
        def _(pool):
            nc.gpsimd.memset(base.ident[:], 0.0).then_inc(s_io.const, 1)
            pool.wait_ge(s_io.const, 2)
            nc.gpsimd.affine_select(out=base.ident[:], in_=base.ident[:], compare_op=ALU.not_equal, fill=1.0,
                                    base=0, pattern=[[-1, P]], channel_multiplier=1).then_inc(s_io.const, 3)
            nc.gpsimd.iota(base.row_in_page[:], [[0, 1]], base=0, channel_multiplier=1).then_inc(s_io.iota, 1)
            barrier(pool, 1)
            norm_pool(nc, pool, m_f1, s_f1, lambda: [
                ffn_pool_split(nc, pool, m_f1, s_f1, 0, 0, half) for half in range(2)])
            ffn_pool(nc, pool, m_f1, s_f1)
            barrier(pool, 2)
            nc.gpsimd.memset(m_mix.bias01[:], 0.0).then_inc(s_io.leave, 1)
            pool.wait_ge(s_io.leave, 1)
            nc.gpsimd.affine_select(out=m_mix.bias01[:, P:], in_=m_mix.bias01[:, P:], compare_op=ALU.is_ge, fill=NEG,
                                    base=0, pattern=[[-1, P]], channel_multiplier=1)
            barrier(pool, 3)
            for b in range(TS):
                smp_load(pool, m_mix, b, m_mix.kidx[:, b], i.cache_kidx, s_io.ki_in)
            norm_pool(nc, pool, m_mix, s_nm, lambda: proj_pool_split(nc, pool, m_mix, s_mix, "ki", 0, 0))
            proj_pool(nc, pool, m_mix, s_mix)
            pool.wait_ge(s_io.ki_in, 16 * TS)
            barrier(pool, 4)
            smp_pool(nc, pool, m_mix, s_smp, i)
            barrier(pool, 5)
            ssm_pool(nc, pool, m_ssm, s_ssm)
            barrier(pool, 6)
            out_pool(nc, pool, m_out, s_out)
            barrier(pool, 7)
            norm_pool(nc, pool, m_f2, s_f2, lambda: [
                ffn_pool_split(nc, pool, m_f2, s_f2, 0, 0, half) for half in range(2)])
            ffn_pool(nc, pool, m_f2, s_f2)
            barrier(pool, 8)

        @block.tensor
        def _(pe):
            in_pe(nc, pe, m_in, s_io)
            barrier(pe, 1)
            norm_pe(nc, pe, m_f1, s_f1)
            ffn_pe(nc, pe, m_f1, s_f1)
            barrier(pe, 2)
            barrier(pe, 3)
            norm_pe(nc, pe, m_mix, s_nm)
            proj_pe(nc, pe, m_mix, s_mix, s_nm)
            barrier(pe, 4)
            att_pe(nc, pe, m_mix, s_att, smp_pe(nc, pe, m_mix, s_smp))
            barrier(pe, 5)
            ssm_pe(nc, pe, m_ssm, s_ssm)
            barrier(pe, 6)
            out_pe(nc, pe, m_out, s_out)
            barrier(pe, 7)
            norm_pe(nc, pe, m_f2, s_f2)
            ffn_pe(nc, pe, m_f2, s_f2)
            barrier(pe, 8)
            fin_pe(nc, pe, m_fin, s_io)


def views(nc, ins, outs):
    i = {}
    i["x_prompt"] = ins["x_prompt"].rearrange("b t d -> (b t) d")
    i["x_sample"] = ins["x_sample"].rearrange("b t d -> (b t) d")
    i["cache_k"] = ins["cache_k"].rearrange("l n p h d -> (l n) p (h d)")
    i["cache_v"] = ins["cache_v"].rearrange("l n p h d -> (l n) p (h d)")
    i["cache_kidx"] = ins["cache_kidx"].rearrange("l n p d -> (l n) p d")
    i["state_re"] = ins["state_ssm_re"].rearrange("l b g s -> (l b) (g s)")
    i["state_im"] = ins["state_ssm_im"].rearrange("l b g s -> (l b) (g s)")
    i["page_table"] = ins["page_table"]
    for name in ("w1_gate", "w1_up", "w1_down", "w_in", "w_glu", "w_pa", "w_pb", "w_out", "w2_gate", "w2_up",
                 "w2_down", "a_re", "a_im"):
        i[name] = ins[name].rearrange("l a b -> (l a) b")
    for name in ("b_re", "b_im", "c_re", "c_im"):
        i[name] = ins[name].rearrange("l a b c -> (l a) b c")
    for name in ("log_dt", "d_skip", "b_glu"):
        i[name] = ins[name].rearrange("l a -> (l a)")
    i["gains"] = [ins[n].rearrange("l a -> (l a)") for n in ("g_ffn1", "g_mix", "g_ffn2")] + [ins["g_final"]]

    def scratch(name, shape):
        return nc.dram_tensor(name, shape, F32).ap()

    o = {}
    o["y_prompt"] = outs["y_prompt"].rearrange("b t d -> (b t) d")
    o["y_sample"] = outs["y_sample"].rearrange("b t d -> (b t) d")
    k_p, v_p = (outs[n].rearrange("l b (n p) h d -> p (l b n) (h d)", p=P) for n in ("k_prompt", "v_prompt"))
    ki_p = outs["kidx_prompt"].rearrange("l b (n p) d -> p (l b n) d", p=P)
    o["k_s"], o["v_s"] = (outs[n].rearrange("l b t h d -> (l b t) (h d)") for n in ("k_sample", "v_sample"))
    o["ki_s"] = outs["kidx_sample"].rearrange("l b t d -> (l b t) d")
    o["ssm_re_p"], o["ssm_im_p"] = (outs[n].rearrange("l b (i e) s -> (l b i) (e s)", e=2)
                              for n in ("ssm_re_prompt", "ssm_im_prompt"))
    o["ssm_re_s"], o["ssm_im_s"] = (outs[n].rearrange("l b g s -> (l b) (g s)")
                              for n in ("ssm_re_sample", "ssm_im_sample"))
    o["x_away"] = scratch("x_meanwhile", (P, KD * T))
    o["q_s"] = scratch("q_sample_rows", (TS, D_ATTN))
    o["q_p"] = scratch("q_rows", (P, NB, D_ATTN))
    o["qi_s"] = scratch("q_index_sample_rows", (TS, IDX_HEADS * IDX))
    o["wi_s"] = scratch("index_weight_sample_rows", (TS, IDX_HEADS))
    o["ln_s"] = scratch("new_key_logits", (TS, N_HEADS))
    o["u_p"] = scratch("u_by_chunk_rows", (P, L * SSM_W))
    o["u_s"] = scratch("u_sample_rows", (TS, SSM_W))
    o["gates"] = scratch("gates_T", (2 * D, T))
    o["token_major"] = {"k": (k_p, o["k_s"]), "v": (v_p, o["v_s"]), "ki": (ki_p, o["ki_s"]), "q": (o["q_p"], o["q_s"]),
                     "u": (o["u_p"], o["u_s"])}
    return record("Ins", i), record("Outs", o)


def kernel(**inputs):
    import concourse.bacc as bacc
    from concourse.bass_utils import run_bass_kernel_spmd as run

    nc = bacc.Bacc("TRN2", target_bir_lowering=False, num_devices=1, dynamic_dma_scratch_size=1024)
    arrays, ins, outs = {}, {}, {}
    for name in INS:
        a = np.ascontiguousarray(inputs[name])
        arrays[f"in_{name}"] = a
        ins[name] = nc.dram_tensor(f"in_{name}", a.shape, mybir.dt.from_np(a.dtype), kind="ExternalInput").ap()
    for name, shape in OUTS:
        outs[name] = nc.dram_tensor(f"out_{name}", shape, F32, kind="ExternalOutput").ap()
    build_layer(nc, *views(nc, ins, outs))
    r = run(nc, [arrays], core_ids=[0])
    return tuple(r.results[0][f"out_{name}"] for name, _ in OUTS)
```
